# Optimizing a Trainium2 kernel written in Bass

```python
import jax, jax.numpy as jnp
from jax import lax
import numpy as np

D_MODEL = 1024
BATCH = 1
SEQ = 256
DEPTH = 2

GRID_W = 64
CTX_LEN = 256
EPS = 1e-6
HEAD_DIM = 64
ATT_HEADS = D_MODEL // 128
ATT_KV_HEADS = ATT_HEADS // 4
ATT_GROUP = ATT_HEADS // ATT_KV_HEADS
WINDOW = 128
BLOCK = 128
ROPE_THETA = 10000.0
ATT_W = ATT_HEADS * HEAD_DIM
KV_W = ATT_KV_HEADS * HEAD_DIM
GLA_HEADS = D_MODEL // 256
GLA_DK = 64
GLA_DV = 64
GLA_LOWRANK = 16
GLA_TAU = 16.0
GLA_CHUNK = 64
GLA_KW = GLA_HEADS * GLA_DK
GLA_VW = GLA_HEADS * GLA_DV
CONV_CH = D_MODEL // 4
CONV_K = 3
MIX_W = ATT_W + GLA_VW + CONV_CH
IN_SIZES = (ATT_W, KV_W, KV_W, GLA_KW, GLA_KW, GLA_VW, GLA_VW, GLA_VW, GLA_LOWRANK, GLA_LOWRANK, CONV_CH, CONV_CH, CONV_CH)
IN_W = ATT_W + 2 * KV_W + 2 * GLA_KW + 3 * GLA_VW + 2 * GLA_LOWRANK + 3 * CONV_CH
D_FF = ((8 * D_MODEL // 3 + 127) // 128) * 128
N_EXPERTS = 8
TOP_K = 2
D_FF_EXPERT = D_FF // 2
N_DENSE = (DEPTH + 1) // 2
N_MOE = DEPTH // 2

kernel_name = 'hybrid_parallel_heads_dit_block'

F32 = jnp.float32

def rmsnorm(t, g):
    t32 = t.astype(F32)
    return (t32 * lax.rsqrt(jnp.mean(t32 * t32, axis=-1, keepdims=True) + EPS) * g.astype(F32)).astype(t.dtype)

def axial_rope(rows, cols):
    nf = HEAD_DIM // 4
    inv = ROPE_THETA ** (-jnp.arange(nf, dtype=F32) / nf)
    ang = jnp.concatenate([rows.astype(F32)[:, None] * inv, cols.astype(F32)[:, None] * inv], axis=-1)
    return jnp.cos(ang), jnp.sin(ang)

def apply_rope(t, cos, sin):
    half = HEAD_DIM // 2
    t1, t2 = t[..., :half], t[..., half:]
    c, s = cos[None, :, None, :], sin[None, :, None, :]
    return jnp.concatenate([t1 * c - t2 * s, t2 * c + t1 * s], axis=-1).astype(t.dtype)

def softmax_with_sink(scores, sink):
    sk = jnp.broadcast_to(sink.astype(F32)[:, :, None, None], scores.shape[:-1] + (1,))
    p = jax.nn.softmax(jnp.concatenate([sk, scores], axis=-1), axis=-1)
    return p[..., 1:]

def window_attention(q, k, v, k_ctx, v_ctx, sink):
    B, S = q.shape[:2]
    L = k_ctx.shape[1]
    nb = S // BLOCK
    qb = q.reshape(B, nb, BLOCK, ATT_KV_HEADS, ATT_GROUP, HEAD_DIM) * HEAD_DIM ** -0.5
    pad = ((0, 0), (BLOCK, BLOCK), (0, 0), (0, 0))
    kp = jnp.pad(k, pad).reshape(B, nb + 2, BLOCK, ATT_KV_HEADS, HEAD_DIM)
    vp = jnp.pad(v, pad).reshape(B, nb + 2, BLOCK, ATT_KV_HEADS, HEAD_DIM)
    kw = jnp.concatenate([kp[:, :-2], kp[:, 1:-1], kp[:, 2:]], axis=2)
    vw = jnp.concatenate([vp[:, :-2], vp[:, 1:-1], vp[:, 2:]], axis=2)
    qpos = jnp.arange(S).reshape(nb, BLOCK)
    kpos = (jnp.arange(nb)[:, None] - 1) * BLOCK + jnp.arange(3 * BLOCK)[None, :]
    valid = ((kpos[:, None, :] >= 0) & (kpos[:, None, :] < S)
             & (jnp.abs(qpos[:, :, None] - kpos[:, None, :]) <= WINDOW))
    s_loc = jnp.einsum('bnqhgd,bnkhd->bnhgqk', qb, kw).astype(F32)
    s_loc = jnp.where(valid[None, :, None, None], s_loc, -jnp.inf)
    s_ctx = jnp.einsum('bnqhgd,bkhd->bnhgqk', qb, k_ctx).astype(F32)
    p = softmax_with_sink(jnp.concatenate([s_ctx, s_loc], axis=-1),
                          sink.reshape(ATT_KV_HEADS, ATT_GROUP)).astype(v.dtype)
    o = (jnp.einsum('bnhgqk,bkhd->bnqhgd', p[..., :L], v_ctx)
         + jnp.einsum('bnhgqk,bnkhd->bnqhgd', p[..., L:], vw))
    return o.reshape(B, S, ATT_W)

def context_attention(q, k, v, sink):
    B, L = q.shape[:2]
    qg = q.reshape(B, L, ATT_KV_HEADS, ATT_GROUP, HEAD_DIM) * HEAD_DIM ** -0.5
    s = jnp.einsum('bqhgd,bkhd->bhgqk', qg, k).astype(F32)
    p = softmax_with_sink(s, sink.reshape(ATT_KV_HEADS, ATT_GROUP)).astype(v.dtype)
    return jnp.einsum('bhgqk,bkhd->bqhgd', p, v).reshape(B, L, ATT_W)

def gla_chunked(q, k, v, log_a, s0):
    B, T, H, DK = q.shape
    DV = v.shape[-1]
    C = GLA_CHUNK
    n = T // C
    q32 = q.astype(F32).reshape(B, n, C, H, DK)
    k32 = k.astype(F32).reshape(B, n, C, H, DK)
    v32 = v.astype(F32).reshape(B, n, C, H, DV)
    b = jnp.cumsum(log_a.astype(F32).reshape(B, n, C, H, DK), axis=2)
    b_ref = b[:, :, C // 2:C // 2 + 1]
    b_last = b[:, :, -1]
    lower = jnp.tril(jnp.ones((C, C), bool))
    a = jnp.einsum('bnthd,bnshd->bnhts', q32 * jnp.exp(b - b_ref), k32 * jnp.exp(b_ref - b))
    a = jnp.where(lower, a, 0.0)
    o = jnp.einsum('bnhts,bnshe->bnthe', a, v32)
    u = jnp.einsum('bnshd,bnshe->bnhde', k32 * jnp.exp(b_last[:, :, None] - b), v32)

    def step(s, xs):
        d, ui = xs
        return d[..., None] * s + ui, s

    s_fin, s_in = lax.scan(step, s0.astype(F32), (jnp.moveaxis(jnp.exp(b_last), 1, 0), jnp.moveaxis(u, 1, 0)))
    s_in = jnp.moveaxis(s_in, 0, 1)
    o = o + jnp.einsum('bnthd,bnhde->bnthe', q32 * jnp.exp(b), s_in)
    return o.reshape(B, T, H, DV).astype(v.dtype), s_fin

def gla_final_state(k, v, log_a):
    b = jnp.cumsum(log_a.astype(F32), axis=1)
    w = jnp.exp(b[:, -1:] - b)
    return jnp.einsum('bthd,bthe->bhde', k.astype(F32) * w, v.astype(F32))

def head_rmsnorm(o, g):
    o32 = o.astype(F32)
    return (o32 * lax.rsqrt(jnp.mean(o32 * o32, axis=-1, keepdims=True) + EPS) * g.astype(F32)).astype(o.dtype)

def gla_merge(o_f, o_b, g_f, g_b, norm_g):
    B, T = g_f.shape[:2]
    gf = jax.nn.silu(g_f).reshape(B, T, GLA_HEADS, GLA_DV)
    gb = jax.nn.silu(g_b).reshape(B, T, GLA_HEADS, GLA_DV)
    y = head_rmsnorm(o_f, norm_g) * gf + head_rmsnorm(o_b, norm_g) * gb
    return y.reshape(B, T, GLA_VW)

def short_conv(u, w):
    return lax.conv_general_dilated(u, w[:, None, :].astype(u.dtype), window_strides=(1,),
                                    padding=((CONV_K // 2, CONV_K // 2),),
                                    dimension_numbers=('NWC', 'WIO', 'NWC'),
                                    feature_group_count=u.shape[-1])

def token_mixers(hc, hl, w_in, w_out, sink, w2_f, b_f, w2_b, b_b, gla_g, conv_w, cos, sin, ctx_out):
    B, L, _ = hc.shape
    T = L + hl.shape[1]
    offs = np.cumsum(np.array(IN_SIZES))[:-1].tolist()
    proj = jnp.concatenate([hc, hl], axis=1) @ w_in
    (a_q, a_k, a_v, l_q, l_k, l_v, l_gf, l_gb, l_af, l_ab, s_b, s_c, s_x) = jnp.split(proj, offs, axis=-1)
    flip = lambda t: jnp.flip(t, axis=1)

    q = a_q.reshape(B, T, ATT_HEADS, HEAD_DIM)
    k = a_k.reshape(B, T, ATT_KV_HEADS, HEAD_DIM)
    v = a_v.reshape(B, T, ATT_KV_HEADS, HEAD_DIM)
    att_lat = window_attention(apply_rope(q[:, L:], cos, sin), apply_rope(k[:, L:], cos, sin), v[:, L:],
                               k[:, :L], v[:, :L], sink)

    gq = l_q.reshape(B, T, GLA_HEADS, GLA_DK) * GLA_DK ** -0.5
    gk = l_k.reshape(B, T, GLA_HEADS, GLA_DK)
    gv = l_v.reshape(B, T, GLA_HEADS, GLA_DV)
    la_f = (jax.nn.log_sigmoid((l_af @ w2_f + b_f).astype(F32)) / GLA_TAU).reshape(B, T, GLA_HEADS, GLA_DK)
    la_b = (jax.nn.log_sigmoid((l_ab @ w2_b + b_b).astype(F32)) / GLA_TAU).reshape(B, T, GLA_HEADS, GLA_DK)
    zero = jnp.zeros((B, GLA_HEADS, GLA_DK, GLA_DV), F32)
    if ctx_out:
        oc_f, st_f = gla_chunked(gq[:, :L], gk[:, :L], gv[:, :L], la_f[:, :L], zero)
        oc_b, st_b = gla_chunked(flip(gq[:, :L]), flip(gk[:, :L]), flip(gv[:, :L]), flip(la_b[:, :L]), zero)
        oc_b = flip(oc_b)
    else:
        st_f = gla_final_state(gk[:, :L], gv[:, :L], la_f[:, :L])
        st_b = gla_final_state(flip(gk[:, :L]), flip(gv[:, :L]), flip(la_b[:, :L]))
    ol_f, _ = gla_chunked(gq[:, L:], gk[:, L:], gv[:, L:], la_f[:, L:], st_f)
    ol_b, _ = gla_chunked(flip(gq[:, L:]), flip(gk[:, L:]), flip(gv[:, L:]), flip(la_b[:, L:]), st_b)
    gla_lat = gla_merge(ol_f, flip(ol_b), l_gf[:, L:], l_gb[:, L:], gla_g)

    conv_lat = s_b[:, L:] * short_conv(s_c[:, L:] * s_x[:, L:], conv_w)

    lat = jnp.concatenate([att_lat, gla_lat, conv_lat], axis=-1)
    if not ctx_out:
        return lat @ w_out, None
    att_ctx = context_attention(q[:, :L], k[:, :L], v[:, :L], sink)
    gla_ctx = gla_merge(oc_f, oc_b, l_gf[:, :L], l_gb[:, :L], gla_g)
    conv_ctx = s_b[:, :L] * short_conv(s_c[:, :L] * s_x[:, :L], conv_w)
    cmix = jnp.concatenate([att_ctx, gla_ctx, conv_ctx], axis=-1)
    y = jnp.concatenate([cmix, lat], axis=1) @ w_out
    return y[:, L:], y[:, :L]

def swiglu(t, w_gu, w_down):
    g, u = jnp.split(t @ w_gu, 2, axis=-1)
    return (jax.nn.silu(g) * u) @ w_down

def moe_swiglu(h, router, w_gu, w_down):
    shp = h.shape
    t = h.reshape(-1, shp[-1])
    logits = (t @ router).astype(F32)
    top_v, top_i = lax.top_k(logits, TOP_K)
    gates = jax.nn.softmax(top_v, axis=-1)
    combine = jnp.sum(jax.nn.one_hot(top_i, N_EXPERTS, dtype=F32) * gates[..., None], axis=1).astype(t.dtype)
    y = jnp.zeros_like(t)
    for e in range(N_EXPERTS):
        y = y + combine[:, e:e + 1] * swiglu(t, w_gu[e], w_down[e])
    return y.reshape(shp)

def setup_inputs(seed: int = 0) -> dict:
    key = jax.random.key(seed)
    ks = jax.random.split(key, 24)
    D = D_MODEL
    nrm = lambda k, shape, s: jax.random.normal(k, shape, F32) * s
    return {
        'x': nrm(ks[0], (BATCH, SEQ, D), 1.0),
        'c': nrm(ks[1], (BATCH, D), 1.0),
        'ctx': nrm(ks[2], (BATCH, CTX_LEN, D), 1.0),
        'c_ctx': nrm(ks[3], (D,), 1.0),
        'w_mod': nrm(ks[4], (DEPTH, D, 6 * D), 0.5 * D ** -0.5),
        'b_mod': nrm(ks[5], (DEPTH, 6 * D), 0.02),
        'norm1_g': 1.0 + nrm(ks[6], (DEPTH, D), 0.05),
        'norm2_g': 1.0 + nrm(ks[7], (DEPTH, D), 0.05),
        'w_in': nrm(ks[8], (DEPTH, D, IN_W), D ** -0.5),
        'w_out': nrm(ks[9], (DEPTH, MIX_W, D), MIX_W ** -0.5),
        'attn_sink': nrm(ks[10], (DEPTH, ATT_HEADS), 0.5),
        'gla_w2_f': nrm(ks[11], (DEPTH, GLA_LOWRANK, GLA_KW), GLA_LOWRANK ** -0.5),
        'gla_b_f': nrm(ks[12], (DEPTH, GLA_KW), 0.5),
        'gla_w2_b': nrm(ks[13], (DEPTH, GLA_LOWRANK, GLA_KW), GLA_LOWRANK ** -0.5),
        'gla_b_b': nrm(ks[14], (DEPTH, GLA_KW), 0.5),
        'gla_norm_g': 1.0 + nrm(ks[15], (DEPTH, GLA_DV), 0.05),
        'conv_w': nrm(ks[16], (DEPTH, CONV_K, CONV_CH), CONV_K ** -0.5),
        'ffn_w_gu': nrm(ks[17], (N_DENSE, D, 2 * D_FF), D ** -0.5),
        'ffn_w_down': nrm(ks[18], (N_DENSE, D_FF, D), D_FF ** -0.5),
        'router_w': nrm(ks[19], (N_MOE, D, N_EXPERTS), D ** -0.5),
        'expert_w_gu': nrm(ks[20], (N_MOE, N_EXPERTS, D, 2 * D_FF_EXPERT), D ** -0.5),
        'expert_w_down': nrm(ks[21], (N_MOE, N_EXPERTS, D_FF_EXPERT, D), D_FF_EXPERT ** -0.5),
        'final_norm_g': 1.0 + nrm(ks[22], (D,), 0.05),
    }

def reference(x, c, ctx, c_ctx, w_mod, b_mod, norm1_g, norm2_g, w_in, w_out, attn_sink,
              gla_w2_f, gla_b_f, gla_w2_b, gla_b_b, gla_norm_g, conv_w,
              ffn_w_gu, ffn_w_down, router_w, expert_w_gu, expert_w_down, final_norm_g):
    S = x.shape[1]
    L = ctx.shape[1]
    ROWS = S // GRID_W
    rows = jnp.repeat(jnp.arange(ROWS, dtype=jnp.int32), GRID_W)
    cols = jnp.tile(jnp.arange(GRID_W, dtype=jnp.int32), ROWS)
    cos, sin = axial_rope(rows, cols)
    silu_c = jax.nn.silu(c)
    silu_cc = jax.nn.silu(c_ctx)
    xl, xc = x, ctx
    for l in range(DEPTH):
        last = l == DEPTH - 1
        mod_l = (silu_c @ w_mod[l] + b_mod[l])[:, None, :]
        mod_c = silu_cc @ w_mod[l] + b_mod[l]
        sh1, sc1, g1, sh2, sc2, g2 = jnp.split(mod_l, 6, axis=-1)
        ch1, cs1, cg1, ch2, cs2, cg2 = jnp.split(mod_c, 6, axis=-1)
        hl = rmsnorm(xl, norm1_g[l]) * (1 + sc1) + sh1
        hc = rmsnorm(xc, norm1_g[l]) * (1 + cs1) + ch1
        yl, yc = token_mixers(hc, hl, w_in[l], w_out[l], attn_sink[l], gla_w2_f[l], gla_b_f[l],
                              gla_w2_b[l], gla_b_b[l], gla_norm_g[l], conv_w[l], cos, sin, not last)
        xl = xl + g1 * yl
        if not last:
            xc = xc + cg1 * yc
        hl = rmsnorm(xl, norm2_g[l]) * (1 + sc2) + sh2
        if last:
            h2 = hl
        else:
            hc = rmsnorm(xc, norm2_g[l]) * (1 + cs2) + ch2
            h2 = jnp.concatenate([hc, hl], axis=1)
        if l % 2 == 0:
            f = swiglu(h2, ffn_w_gu[l // 2], ffn_w_down[l // 2])
        else:
            f = moe_swiglu(h2, router_w[l // 2], expert_w_gu[l // 2], expert_w_down[l // 2])
        xl = xl + g2 * f[:, h2.shape[1] - S:]
        if not last:
            xc = xc + cg2 * f[:, :L]
    return rmsnorm(xl, final_norm_g)


_drawn_inputs = setup_inputs


def setup_inputs(seed=0):
    import zlib

    import numpy as np

    out = dict(_drawn_inputs(seed))
    spreads = {}
    factors = {'attn_sink': 27.296, 'gla_norm_g': 3.801}
    for name, (base, spread) in spreads.items():
        noise = np.random.default_rng([zlib.crc32(name.encode()), seed]).standard_normal(out[name].shape)
        drawn = base * np.exp(spread * noise) if base else spread * noise
        out[name] = __import__('jax').numpy.asarray(drawn.astype(out[name].dtype))
    for name, factor in factors.items():
        out[name] = (out[name] * factor).astype(out[name].dtype)
    return out
```

```python
from contextlib import ExitStack

import numpy as np

import concourse.bass as bass
from concourse import mybir

F32 = mybir.dt.float32
F32R = mybir.dt.float32r
I32 = mybir.dt.int32
U32 = mybir.dt.uint32
ALU = mybir.AluOpType
ACT = mybir.ActivationFunctionType
AX = mybir.AxisListType

P = 128
D = 1024
KT = D // P
CTX, LAT = 256, 256
T = CTX + LAT
NTT = T // P
EPS = 1e-6
LAYERS = 2
HEADS, HD = 8, 64
AT = HEADS * HD // P
CH = 64
NCH = T // CH
GT = 2
TAU = 16.0
FM = 16
FJ = 11
NE = 8
MODT = 6 * D // P
UNIT = KT * P
DUNIT = FJ * P
R = 5
H = 3
PROJ, OUT, BLOCK = FM + 8, KT, 2 * FJ + KT
M0 = 16

LA, LK, LQ, AK, AQ, SB, SC, SX = 0, 1, 3, 5, 6, 10, 12, 14


def build(nc, d, out):
    ctx = ExitStack()
    with ctx:
        def sb(name, shape, dt=F32, stack=ctx):
            return stack.enter_context(nc.sbuf_tensor(name, shape, dt))

        raw = sb("raw", [P, R, DUNIT])
        whi = sb("whi", [P, H, DUNIT], F32R)
        wlo = sb("wlo", [P, H, DUNIT], F32R)
        xT = sb("xT", [P, KT, T])
        ident = sb("ident", [P, P])
        rot = sb("rot", [P, P])
        ones = sb("ones", [P, P])
        cos = sb("cos", [P, LAT])
        sin = sb("sin", [P, LAT])
        amask = sb("amask", [P, 2, P])
        gmask = sb("gmask", [P, 2, 4 * P], I32)
        reset = sb("reset", [P, T])
        iota = sb("iota", [P, NE])
        c_raw = sb("c_raw", [P, 2 * KT])
        c_act = sb("c_act", [P, 2 * KT])
        b_mod = sb("b_mod", [P, LAYERS, 2 * MODT])
        norm_g = sb("norm_g", [P, LAYERS, 2, 2 * KT])
        final_g = sb("final_g", [P, KT])
        sink = sb("sink", [P, LAYERS, HEADS])
        w2 = sb("w2", [CH, LAYERS, GT * P])
        gla_b = sb("gla_b", [P, LAYERS, 2, GT])
        gla_g = sb("gla_g", [P, LAYERS])
        conv_w = sb("conv_w", [P, LAYERS, 3, 2])
        router = sb("router", [P, KT, NE])
        mod = sb("mod", [P, LAYERS, 2 * MODT])
        gain = sb("gain", [P, LAYERS, 2, 2 * KT])
        epsc = sb("epsc", [P, 1])
        rs = sb("rs", [P, T])
        sq = sb("sq", [P, 2, T])
        xn = sb("xn", [P, 2, T])
        hf = sb("hf", [P, 2, T])
        negsink = sb("negsink", [P, LAYERS, HEADS])
        mx = sb("mx", [P, NTT * HEADS])
        negm = sb("negm", [P, NTT * HEADS])
        psumrow = sb("psumrow", [P, NTT * HEADS])
        esink = sb("esink", [P, HEADS])
        rden = sb("rden", [P, HEADS])
        decay = sb("decay", [P, 2, GT * NCH])
        gss = sb("gss", [P, NTT * 8])
        logits = sb("logits", [P, 2, NE])
        top = sb("top", [P, 2, 8])
        topi = sb("topi", [P, 2, 8], U32)
        topf = sb("topf", [P, 2, 8])
        gate2 = sb("gate2", [P, 2, 4])
        pick = sb("pick", [P, 2, 2, NE])

        region = ExitStack()
        hhi = sb("hhi", [P, KT, T], F32R, region)
        hlo = sb("hlo", [P, KT, T], F32R, region)
        region.close()
        gtt = sb("gtt", [P, 2, GT, T])
        gt1, gt2 = gtt[:, 0, :, :], gtt[:, 1, :, :]
        gk = sb("gk", [P, GT, T])
        gb = sb("gb", [P, GT, T])
        gqp = sb("gqp", [P, GT, T])
        gkp = sb("gkp", [P, GT, T])
        gqb = sb("gqb", [P, GT, T])
        gkt = sb("gkt", [P, NTT, GT * P])

        region = ExitStack()
        fhi = sb("fhi", [P, FJ, T], F32R, region)
        flo = sb("flo", [P, FJ, T], F32R, region)
        sg = sb("sg", [P, 2, T], F32, region)
        yacc = sb("yacc", [P, KT, LAT], F32, region)
        cb = sb("cb", [P, NE, LAT], F32, region)
        diag = sb("diag", [P, 2, 2, P], F32, region)
        region.close()
        region = ExitStack()
        la = sb("la", [CH, T], F32, region)
        lk = sb("lk", [P, GT, T], F32, region)
        lq = sb("lq", [P, GT, T], F32, region)
        ak = sb("ak", [P, T], F32, region)
        aq = sb("aq", [P, AT, T], F32, region)
        s_b = sb("s_b", [P, 2, T], F32, region)
        s_c = sb("s_c", [P, 2, T], F32, region)
        cx = sb("cx", [P, 2, 2, LAT + 2], F32, region)
        vt = sb("vt", [P, NTT, 384], F32, region)
        gate = sb("gate", [P, NTT, 512], F32, region)
        part = ExitStack()
        state = sb("state", [P, 2, NCH + 1, GT * CH], F32, part)
        am = sb("am", [P, 2, 4 * P], F32, part)
        go = sb("go", [P, NTT, 512], F32, part)
        part.close()
        asc = sb("asc", [P, 3072], F32, region)
        region.close()
        region = ExitStack()
        outT = sb("outT", [P, KT, LAT], F32, region)
        region.close()

        prob = asc[:, 0:1536].rearrange("p (s n) -> p s n", s=3)
        probT = asc[:, 1536:2560].rearrange("p (s n) -> p s n", s=2)
        osb = asc[:, 2560:3072]
        rt1 = asc[:, 0:1024]
        rt2 = asc[:, 1024:2048]

        ps = ctx.enter_context(nc.psum_tensor("ps", [P, 8, 512], F32))

        def sem(name):
            return ctx.enter_context(nc.semaphore(name))

        def sems(name, n):
            return [sem(f"{name}{i}") for i in range(n)]

        landed = sems("landed", R)
        hi_ready = sem("hi_ready")
        lo_ready = sem("lo_ready")
        split_used = sem("split_used")
        mod_used = sem("mod_used")
        mod_out = sem("mod_out")
        const_in = sem("const_in")
        x_in = sem("x_in")
        c_in = sem("c_in")
        c_ready = sem("c_ready")
        init_done = sem("init_done")
        gain_ready = sem("gain_ready")
        sq_ready = sem("sq_ready")
        sumsq_done = sem("sumsq_done")
        rs_ready = sem("rs_ready")
        hf_ready = sem("hf_ready")
        hhi_done = sem("hhi_done")
        hlo_done = sem("hlo_done")
        fm_done = sems("fm_done", LAYERS)
        fm_out = sems("fm_out", LAYERS)
        cx_out = sems("cx_out", LAYERS)
        v_done = sems("v_done", LAYERS)
        v_out = sems("v_out", LAYERS)
        g_done = sems("g_done", LAYERS)
        g_out = sems("g_out", LAYERS)
        conv_out = sems("conv_out", LAYERS)
        z_done = sems("z_done", LAYERS)
        abs_done = sems("abs_done", LAYERS)
        sp_ready = sems("sp_ready", LAYERS)
        d_ready = sems("d_ready", LAYERS)
        e_ready = sems("e_ready", LAYERS)
        e_used = sems("e_used", LAYERS)
        kt_done = sems("kt_done", LAYERS)
        kt_out = sems("kt_out", LAYERS)
        dec_ready = sems("dec_ready", LAYERS)
        u_done = sems("u_done", LAYERS)
        st_ready = sems("st_ready", LAYERS)
        at_done = sems("at_done", LAYERS)
        am_ready = sems("am_ready", LAYERS)
        o_done = sems("o_done", LAYERS)
        o_out = sems("o_out", LAYERS)
        ss_ready = sems("ss_ready", LAYERS)
        grs_ready = sems("grs_ready", LAYERS)
        y_ready = sems("y_ready", LAYERS)
        yT_done = sems("yT_done", LAYERS)
        mixhi = sems("mixhi", LAYERS)
        mixlo = sems("mixlo", LAYERS)
        rot_done = sems("rot_done", LAYERS)
        rope_out = sems("rope_out", LAYERS)
        s_done = sems("s_done", LAYERS)
        negm_ready = sems("negm_ready", LAYERS)
        p_ready = sems("p_ready", LAYERS)
        pT_done = sems("pT_done", LAYERS)
        pT_out = sems("pT_out", LAYERS)
        pv_done = sems("pv_done", LAYERS)
        sk_ready = sems("sk_ready", LAYERS)
        esk_ready = sems("esk_ready", LAYERS)
        osb_ready = sems("osb_ready", LAYERS)
        oT_done = sems("oT_done", LAYERS)
        ahi_ready = sems("ahi_ready", LAYERS)
        alo_ready = sems("alo_ready", LAYERS)
        proj_done = sems("proj_done", LAYERS)
        x_mixed = sems("x_mixed", LAYERS)
        gate_done = sems("gate_done", LAYERS)
        up_done = sems("up_done", LAYERS)
        sg_ready = sems("sg_ready", LAYERS)
        fh_ready = sems("fh_ready", LAYERS)
        fhi_ready = sems("fhi_ready", LAYERS)
        flo_ready = sems("flo_ready", LAYERS)
        down_done = sems("down_done", LAYERS)
        down_out = sems("down_out", LAYERS)
        swiglu_ready = sem("swiglu_ready")
        lg_done = sem("lg_done")
        topd_ready = sem("topd_ready")
        tope_ready = sem("tope_ready")
        diag_ready = sem("diag_ready")
        cb_done = sem("cb_done")
        cb_out = sem("cb_out")
        x_last = sem("x_last")
        out_ready = sem("out_ready")
        stored = sem("stored")
        act_order = sem("act_order")
        dve_order = sem("dve_order")

        stream = []

        def mod_units(l, m0, m1):
            return [(d["w_mod"][l, m], UNIT, False) for m in range(m0, m1)]

        def proj_units(l):
            fm = [(d["w_fm"][l, m], UNIT, True) for m in range(FM)]
            tv = [(d["w_tv"][l, i], 768, True) for i in range(4)]
            tg = [(d["w_tg"][l, i], UNIT, True) for i in range(4)]
            return fm[:5] + tv + fm[5:10] + tg + fm[10:]

        MODS_AFTER = [1] * 16 + [2] * 8
        m = M0
        stream += mod_units(0, 0, M0)
        for n, unit in enumerate(proj_units(0)):
            stream.append(unit)
            stream += mod_units(0, m, m + MODS_AFTER[n])
            m += MODS_AFTER[n]
        assert m == MODT
        stream += mod_units(1, 0, MODT)
        stream += [(d["w_out"][0, m], UNIT, True) for m in range(OUT)]
        n_before_ffn0 = len(stream)
        after = proj_units(1) + [(d["w_out"][1, m], UNIT, True) for m in range(OUT)]

        split_u = [u for u, s in enumerate(stream) if s[2]]
        mod_u = [u for u, s in enumerate(stream) if not s[2]]
        V_OUT0 = PROJ
        V_FFN0 = PROJ + OUT
        V_PROJ1 = V_FFN0 + 2 * BLOCK
        V_OUT1 = V_PROJ1 + PROJ
        V_MOE = V_OUT1 + OUT
        GAP = n_before_ffn0 - V_FFN0

        def u_of(v):
            return split_u[v] if isinstance(v, int) and v < V_FFN0 else v + GAP

        def cols_of(v):
            if isinstance(v, int):
                if v < V_FFN0:
                    return stream[split_u[v]][1]
                if V_PROJ1 <= v < V_MOE:
                    return after[v - V_PROJ1][1]
            raise AssertionError(v)

        def block_unit(l, i, r):
            if r < 2 * FJ:
                src = d["w_gu"][l][bass.ds(i * 2 * FJ + r, 1)]
                n = UNIT
            else:
                src = d["w_dn"][l][bass.ds(i * KT + r - 2 * FJ, 1)]
                n = DUNIT
            return src.rearrange("a p n -> (a p) n"), n

        block = ctx.enter_context(nc.Block())

        @block.sync
        def _(sp):
            def slot_free(u):
                prev = u - R
                if stream[prev][2]:
                    sp.wait_ge(lo_ready, split_u.index(prev) + 1)
                else:
                    sp.wait_ge(mod_used, mod_u.index(prev) + 1)

            for u, (src, n, _s) in enumerate(stream):
                if u >= R:
                    slot_free(u)
                sp.dma_start(raw[:, u % R, 0:n], src).then_inc(landed[u % R], 16)

            def ffn(l, v0, blocks):
                with sp.Fori(0, blocks) as i:
                    for r in range(BLOCK):
                        src, n = block_unit(l, i, r)
                        sp.wait_ge(lo_ready, i * BLOCK + (v0 + r - R + 1))
                        slot = (v0 + GAP + r) % R
                        sp.dma_start(raw[:, slot, 0:n], src).then_inc(landed[slot], 16)

            ffn(0, V_FFN0, 2)
            for n, (src, cols, _s) in enumerate(after):
                v = V_PROJ1 + n
                sp.wait_ge(lo_ready, v - R + 1)
                slot = (v + GAP) % R
                sp.dma_start(raw[:, slot, 0:cols], src).then_inc(landed[slot], 16)
            ffn(1, V_MOE, NE)
            for n in range(H):
                v = V_MOE + NE * BLOCK + n
                sp.wait_ge(lo_ready, v - R + 1)
                slot = (v + GAP) % R
                sp.dma_start(raw[:, slot, 0:UNIT], d["w_gu"][1][NE * 2 * FJ + n]).then_inc(landed[slot], 16)

            for k in range(KT):
                sp.wait_ge(out_ready, k + 1)
                sp.dma_start(out[:, k, :], outT[:, k, :]).then_inc(stored, 16)
            sp.wait_ge(stored, 16 * KT)

        def split_hi(act, v, base, per_iter, i, cols):
            vi = base if i is None else i * per_iter + base
            u = u_of(base)
            slot = u % R
            if i is None:
                act.wait_ge(landed[slot], 16 * (u // R + 1))
            else:
                act.wait_ge(landed[slot], i * (16 * per_iter // R) + 16 * (u // R + 1))
            if base >= H:
                act.wait_ge(split_used, vi - H + 1)
            nc.scalar.activation(whi[:, base % H, 0:cols], raw[:, slot, 0:cols], ACT.Copy).then_inc(hi_ready, 1)

        def split_lo(dve, base, per_iter, i, cols):
            vi = base if i is None else i * per_iter + base
            slot = u_of(base) % R
            dve.wait_ge(hi_ready, vi + 1)
            nc.vector.tensor_tensor(wlo[:, base % H, 0:cols], raw[:, slot, 0:cols],
                                    whi[:, base % H, 0:cols].bitcast(F32), ALU.subtract).then_inc(lo_ready, 1)

        def x_ready(eng, n, k):
            if n == 0:
                if k == 0:
                    eng.wait_ge(x_in, 16)
            elif n in (1, 3):
                eng.wait_ge(x_mixed[n // 2], k + 1)
            elif n == 2:
                eng.wait_ge(down_out[0], 1 + KT + k + 1)
            else:
                eng.wait_ge(x_last, k + 1)

        def first_col(n):
            return CTX if n >= 3 else 0

        def q_col(l):
            return CTX if l else 0

        def att_tiles(l):
            return [2, 3] if l else [2, 3, 0, 1]

        def gla_tiles(dr):
            return [0, 1, 2, 3] if dr == 0 else [1, 0, 3, 2]

        def gla_chunks(dr):
            return [0, 1] if dr == 0 else [1, 0]

        def gla_reads(l):
            return range(2 if l else 0, NTT)

        @block.tensor
        def _(pe):
            mods = [0]

            def mod_unit():
                n = mods[0]
                mods[0] += 1
                u = mod_u[n]
                m = n % MODT
                if n == 0:
                    pe.wait_ge(c_ready, 1)
                if n == M0 or n == MODT:
                    pe.wait_ge(mod_out, 1 if n == M0 else 2)
                pe.wait_ge(landed[u % R], 16 * (u // R + 1))
                for k in range(KT):
                    mm = nc.tensor.matmul(ps[:, 7, 2 * m:2 * m + 2], raw[:, u % R, k * P:(k + 1) * P],
                                          c_act[:, 2 * k:2 * k + 2], start=(k == 0), stop=(k == KT - 1))
                mm.then_inc(mod_used, 1)

            def three(outp, whs, wls, xh, xl, first, last):
                nc.tensor.matmul(outp, whs, xh, start=first, stop=False)
                nc.tensor.matmul(outp, whs, xl, start=False, stop=False)
                return nc.tensor.matmul(outp, wls, xh, start=False, stop=last)

            def fm_tile(v, outp, xh, xl, nk, wait=True):
                s = v % H
                for k in range(nk):
                    mm = three(outp, whi[:, s, k * P:(k + 1) * P], wlo[:, s, k * P:(k + 1) * P],
                               xh(k), xl(k), k == 0, k == nk - 1)
                return mm

            def norm_sum(n, k):
                pe.wait_ge(sq_ready, KT * n + k + 1)
                nc.tensor.matmul(ps[:, 6, first_col(n):T], ones[:, :], sq[:, k % 2, first_col(n):T],
                                 start=(k == 0), stop=(k == KT - 1)).then_inc(sumsq_done, 1)

            def projection(l):
                v = V_PROJ1 if l else 0
                f = 0

                def fm(v, f):
                    c0 = q_col(l) if f not in (LA, LK, LK + 1, AK) else 0
                    pe.wait_ge(lo_ready, v + 1)
                    if f >= 2:
                        pe.wait_ge(fm_out[l], f - 1)
                    fm_tile(v, ps[:, f % 2, c0:T], lambda k: hhi[:, k, c0:T], lambda k: hlo[:, k, c0:T],
                            KT).then_inc(split_used, 1)

                def tm(v, i, n, t0):
                    pe.wait_ge(lo_ready, v + 1)
                    s = v % H
                    for kk in range(2):
                        k = 2 * i + kk
                        for t in range(t0, NTT):
                            o = ps[:, 2 + t, 0:n]
                            wh, wl = whi[:, s, kk * n:(kk + 1) * n], wlo[:, s, kk * n:(kk + 1) * n]
                            hh, hl = hhi[:, k, t * P:(t + 1) * P], hlo[:, k, t * P:(t + 1) * P]
                            nc.tensor.matmul(o, hh, wh, start=(k == 0), stop=False)
                            nc.tensor.matmul(o, hh, wl, start=False, stop=False)
                            mm = nc.tensor.matmul(o, hl, wh, start=False, stop=(k == KT - 1))
                    mm.then_inc(split_used, 1)

                kinds = ["f"] * 5 + ["v"] * 4 + ["f"] * 5 + ["g"] * 4 + ["f"] * 6
                pe.wait_ge(hlo_done, KT * (2 * l) + KT)
                for n, kind in enumerate(kinds):
                    if kind == "f":
                        fm(v + n, f)
                        f += 1
                    elif kind == "v":
                        tm(v + n, n - 5, 384, 0)
                    else:
                        if n == 14:
                            pe.wait_ge(v_out[l], NTT)
                        tm(v + n, n - 14, 512, 2 if l else 0)
                    if l == 0:
                        for _ in range(MODS_AFTER[n]):
                            mod_unit()

            def gla(l):
                reads = list(gla_reads(l))
                n_u = n_at = n_o = 0
                for dr in range(2):
                    if dr == 0:
                        pe.wait_ge(fm_out[l], 14)
                        pe.wait_ge(cx_out[l], 2)
                        pe.wait_ge(v_out[l], NTT)
                        pe.wait_ge(g_out[l], len(reads))
                    else:
                        pe.wait_ge(o_out[l], len(reads))
                    for p in range(GT):
                        nc.tensor.matmul(ps[:, 2 * dr + p, :], w2[32 * dr:32 * dr + 32, l, p * P:(p + 1) * P],
                                         la[32 * dr:32 * dr + 32, :], start=True, stop=True
                                         ).then_inc(z_done[l], 1)
                    pe.wait_ge(e_used[l], 4 * dr + 4)
                    if dr:
                        pe.wait_ge(st_ready[l], 2 * NTT)
                    for p in range(GT):
                        for t in range(NTT):
                            mm = nc.tensor.transpose(ps[:, 4 + p, t * P:(t + 1) * P], gk[:, p, t * P:(t + 1) * P],
                                                     ident[:, :])
                        mm.then_inc(kt_done[l], 1)
                    pe.wait_ge(kt_out[l], GT * (dr + 1))
                    if dr == 0 and l == 0:
                        pe.wait_ge(mod_out, 2)
                    for step, t in enumerate(gla_tiles(dr)):
                        if n_u >= 2:
                            pe.wait_ge(st_ready[l], 2 * (n_u - 1))
                        for c in range(2):
                            for p in range(GT):
                                for hh in range(2):
                                    rows = slice(CH * c, CH * c + CH)
                                    mm = nc.tensor.matmul(
                                        ps[CH * hh:CH * hh + CH, (6, 4)[n_u % 2] + c, p * CH:(p + 1) * CH],
                                        gkt[rows, t, p * P + CH * hh:p * P + CH * hh + CH],
                                        vt[rows, t, P + (2 * p + hh) * CH:P + (2 * p + hh + 1) * CH],
                                        start=True, stop=True)
                        mm.then_inc(u_done[l], 1)
                        n_u += 1
                        if t not in reads:
                            continue
                        if n_at:
                            pe.wait_ge(am_ready[l], n_at)
                        for h in range(4):
                            p, b = h // 2, CH * (h % 2)
                            mm = nc.tensor.matmul(ps[:, h % 2, p * P:(p + 1) * P],
                                                  gkp[b:b + CH, p, t * P:(t + 1) * P],
                                                  gqp[b:b + CH, p, t * P:(t + 1) * P], start=True, stop=True)
                        mm.then_inc(at_done[l], 1)
                        n_at += 1
                        pe.wait_ge(am_ready[l], n_at)
                        pe.wait_ge(st_ready[l], 8 * dr + 2 * step + 1)
                        if n_o:
                            pe.wait_ge(o_out[l], n_o)
                        for h in range(4):
                            a = 2 * (h % 2) + h // 2
                            nc.tensor.matmul(ps[:, 2 + h % 2, h // 2 * CH:(h // 2 + 1) * CH],
                                             am[:, dr, a * P:(a + 1) * P],
                                             vt[:, t, P + h * CH:P + (h + 1) * CH], start=(h < 2), stop=False,
                                             skip_group_check=True)
                        for ci, c in enumerate(gla_chunks(dr)):
                            for h in range(4):
                                p, b = h // 2, CH * (h % 2)
                                mm = nc.tensor.matmul(
                                    ps[CH * c:CH * c + CH, 2 + h % 2, p * CH:(p + 1) * CH],
                                    gqb[b:b + CH, p, t * P + CH * c:t * P + CH * c + CH],
                                    state[b:b + CH, dr, 2 * step + ci, p * CH:(p + 1) * CH],
                                    start=False, stop=(ci == 1), skip_group_check=True)
                        mm.then_inc(o_done[l], 1)
                        n_o += 1
                pe.wait_ge(y_ready[l], 1)
                pe.wait_ge(st_ready[l], 4 * NTT)
                for f in range(GT):
                    for n, t in enumerate(reads):
                        mm = nc.tensor.transpose(ps[:, 4 + f, t * P:(t + 1) * P],
                                                 gb[:, n // 2, (n % 2) * 256 + f * P:(n % 2) * 256 + (f + 1) * P],
                                                 ident[:, :])
                    mm.then_inc(yT_done[l], 1)

            def attention(l):
                tiles = att_tiles(l)
                for j in range(AT + 1):
                    src = aq[:, j, CTX:T] if j < AT else ak[:, CTX:T]
                    mm = nc.tensor.matmul(ps[:, j // 2, (j % 2) * LAT:(j % 2) * LAT + LAT], rot[:, :], src,
                                          start=True, stop=True)
                mm.then_inc(rot_done[l], 1)
                n_items = len(tiles) * HEADS
                pe.wait_ge(rope_out[l], 1)
                pe.wait_ge(mixlo[l], GT)

                def keys(i):
                    return 4 if tiles[i // HEADS] >= 2 else 2

                def scores(i):
                    t, h = tiles[i // HEADS], i % HEADS
                    b = CH * (h % 2)
                    if i >= 3:
                        pe.wait_ge(p_ready[l], i - 2)
                    nc.tensor.matmul(ps[:, i % 3, 0:keys(i) * P], aq[b:b + CH, h // 2, t * P:(t + 1) * P],
                                     ak[b:b + CH, 0:keys(i) * P], start=True, stop=True).then_inc(s_done[l], 1)

                def turn(i):
                    pe.wait_ge(p_ready[l], i + 1)
                    if i >= 2:
                        pe.wait_ge(pT_out[l], i - 1)
                    for k in range(keys(i)):
                        mm = nc.tensor.transpose(ps[:, 3 + i % 2, k * P:(k + 1) * P],
                                                 prob[:, i % 3, k * P:(k + 1) * P], ident[:, :])
                    mm.then_inc(pT_done[l], 1)

                def pv(i):
                    h = i % HEADS
                    pe.wait_ge(pT_out[l], i + 1)
                    if h == 0 and i:
                        pe.wait_ge(osb_ready[l], i // HEADS)
                    kv = CH * (h % 2)
                    for k in range(keys(i)):
                        mm = nc.tensor.matmul(ps[:, 5, h * HD:(h + 1) * HD], probT[:, i % 2, k * P:(k + 1) * P],
                                              vt[:, k, kv:kv + HD], start=(k == 0), stop=(k == keys(i) - 1))
                    mm.then_inc(pv_done[l], 1)

                def tail(n):
                    pe.wait_ge(osb_ready[l], n + 1)
                    if n:
                        pe.wait_ge(alo_ready[l], n)
                    for j in range(AT):
                        mm = nc.tensor.transpose(ps[:, 6, j * P:(j + 1) * P], osb[:, j * P:(j + 1) * P], ident[:, :])
                    mm.then_inc(oT_done[l], 1)

                for i in range(n_items + 3):
                    if i < n_items:
                        scores(i)
                    if 1 <= i <= n_items:
                        turn(i - 1)
                    if i >= 10 and i % 8 == 2:
                        if 2 <= i < n_items + 2:
                            pv(i - 2)
                        tail((i - 10) // 8)
                    elif 2 <= i < n_items + 2:
                        pv(i - 2)
                    if l == 0:
                        for _ in range(2 if i < 16 else 1):
                            if mods[0] < 2 * MODT:
                                mod_unit()
                assert l or mods[0] == 2 * MODT

            def out_projection(l):
                v0 = V_OUT1 if l else V_OUT0
                c0 = q_col(l)
                n_att = len(att_tiles(l))
                pe.wait_ge(mixlo[l], 4)
                pe.wait_ge(alo_ready[l], n_att)
                for m in range(KT):
                    v = v0 + m
                    pe.wait_ge(lo_ready, v + 1)
                    if m >= 2:
                        pe.wait_ge(x_mixed[l], m - 1)
                    fm_tile(v, ps[:, m % 2, c0:T], lambda k: hhi[:, k, c0:T], lambda k: hlo[:, k, c0:T],
                            KT).then_inc(split_used, 1)
                    if m:
                        norm_sum(2 * l + 1, m - 1)
                norm_sum(2 * l + 1, KT - 1)

            def ffn(l, v0, blocks):
                c0 = q_col(l)
                pe.wait_ge(hlo_done, KT * (2 * l + 1) + KT)
                with pe.Fori(0, blocks) as i:
                    for j in range(FJ):
                        for part in range(2):
                            r = 2 * j + part
                            v = v0 + r
                            pe.wait_ge(lo_ready, i * BLOCK + (v + 1))
                            if part == 0 and j >= 2:
                                pe.wait_ge(fh_ready[l], i * FJ + (j - 1))
                            fm_tile(v, ps[:, 2 * part + j % 2, c0:T], lambda k: hhi[:, k, c0:T],
                                    lambda k: hlo[:, k, c0:T], KT).then_inc(split_used, 1)
                    pe.wait_ge(flo_ready[l], i * FJ + FJ)
                    for m in range(KT):
                        v = v0 + 2 * FJ + m
                        pe.wait_ge(lo_ready, i * BLOCK + (v + 1))
                        if m == 0:
                            pe.wait_ge(down_out[l], i * KT + 1)
                        if m >= 2:
                            pe.wait_ge(down_out[l], i * KT + m)
                        fm_tile(v, ps[:, 4 + m % 2, c0:T], lambda k: fhi[:, k, c0:T], lambda k: flo[:, k, c0:T],
                                FJ).then_inc(split_used, 1)

            pe.wait_ge(init_done, 1)
            pe.wait_ge(const_in, 16 * N_CONST)
            for k in range(KT):
                norm_sum(0, k)
            for _ in range(M0):
                mod_unit()
            projection(0)
            gla(0)
            attention(0)
            out_projection(0)
            ffn(0, V_FFN0, 2)
            for k in range(KT):
                norm_sum(2, k)
            projection(1)
            gla(1)
            attention(1)
            out_projection(1)
            pe.wait_ge(hlo_done, KT * 3 + KT)
            for t in range(2):
                for k in range(KT):
                    for part in (hhi, hlo):
                        mm = nc.tensor.matmul(ps[:, 7, t * NE:(t + 1) * NE],
                                              part[:, k, CTX + t * P:CTX + (t + 1) * P].bitcast(F32),
                                              router[:, k, :], start=(k == 0 and part is hhi),
                                              stop=(k == KT - 1 and part is hlo))
            mm.then_inc(lg_done, 1)
            for e in range(NE):
                pe.wait_ge(diag_ready, 2 * e + 2)
                if e >= 2:
                    pe.wait_ge(cb_out, e - 1)
                nc.tensor.matmul(ps[:, 4 + e % 2, 0:LAT], ones[:, :], diag[:, e % 2, :, :], start=True,
                                 stop=True).then_inc(cb_done, 1)
            ffn(1, V_MOE, NE)
            for k in range(KT):
                norm_sum(4, k)

        @block.scalar
        def _(act):
            done = [0]

            def then(ins):
                done[0] += 1
                ins.then_inc(act_order, 1)
                act.wait_ge(act_order, done[0])

            for name, dst in CONSTS(locals_=dict(
                    ident=ident, rot=rot, cos=cos, sin=sin, amask=amask, gmask=gmask, reset=reset, iota=iota,
                    b_mod=b_mod, norm_g=norm_g, final_g=final_g, sink=sink, w2=w2, gla_b=gla_b, gla_g=gla_g,
                    conv_w=conv_w, router=router)):
                act.dma_start(dst[:], d[name]).then_inc(const_in, 16)

            def hi(v):
                split_hi(act, v, v, None, None, cols_of(v))

            def norm_squares(n, k):
                x_ready(act, n, k)
                if k >= 2:
                    act.wait_ge(sumsq_done, KT * n + k - 1)
                c0 = first_col(n)
                nc.scalar.activation(sq[:, k % 2, c0:T], xT[:, k, c0:T], ACT.Square).then_inc(sq_ready, 1)

            def norm_scale(n):
                act.wait_ge(sumsq_done, KT * n + KT)
                c0 = first_col(n)
                then(nc.scalar.activation(rs[:, c0:T], ps[:, 6, c0:T], ACT.Ln, bias=epsc[:, 0:1], scale=1.0 / D))
                nc.scalar.activation(rs[:, c0:T], rs[:, c0:T], ACT.Exp, scale=-0.5).then_inc(rs_ready, 1)

            def norm_hi(n):
                c0 = first_col(n)
                for k in range(KT):
                    act.wait_ge(hf_ready, KT * n + k + 1)
                    nc.scalar.activation(hhi[:, k, c0:T], hf[:, k % 2, c0:T], ACT.Copy).then_inc(hhi_done, 1)

            def projection(l):
                v0 = V_PROJ1 if l else 0
                c0 = q_col(l)
                kinds = ["f"] * 5 + ["v"] * 4 + ["f"] * 5 + ["g"] * 4 + ["f"] * 6
                f = 0
                for n, kind in enumerate(kinds):
                    if kind == "f":
                        if f < SX:
                            act.wait_ge(split_used, v0 + n + 1)
                            src = ps[:, f % 2, :]
                            if f == LA:
                                dst, src = la[:, :], src[0:CH, :]
                            elif f < LQ:
                                dst = lk[:, f - LK, :]
                            elif f < AK:
                                dst, src = lq[:, f - LQ, c0:T], src[:, c0:T]
                            elif f == AK:
                                dst = ak[:, :]
                            elif f < SB:
                                dst, src = aq[:, f - AQ, c0:T], src[:, c0:T]
                            elif f < SC:
                                dst, src = s_b[:, f - SB, c0:T], src[:, c0:T]
                            else:
                                dst, src = s_c[:, f - SC, c0:T], src[:, c0:T]
                            nc.scalar.activation(dst, src, ACT.Copy).then_inc(fm_out[l], 1)
                        f += 1
                    if n == 17:
                        act.wait_ge(split_used, v0 + n + 1)
                        for t in gla_reads(l):
                            nc.scalar.activation(gate[:, t, :], ps[:, 2 + t, :], ACT.Silu).then_inc(g_out[l], 1)
                    if n + H < PROJ or l:
                        hi(v0 + n + H)

            def gla(l):
                reads = list(gla_reads(l))
                n_o = 0
                for dr in range(2):
                    if dr:
                        act.wait_ge(e_used[l], 4)
                        act.wait_ge(kt_done[l], GT)
                    for p in range(GT):
                        act.wait_ge(z_done[l], 2 * dr + p + 1)
                        nc.scalar.activation(gt1[:, p, :], ps[:, 2 * dr + p, :], ACT.Abs,
                                             bias=gla_b[:, l, dr, p:p + 1]).then_inc(abs_done[l], 1)
                    act.wait_ge(abs_done[l], GT * (dr + 1))
                    then(nc.scalar.activation(gt1[:, :, :], gt1[:, :, :], ACT.Exp, scale=-1.0))
                    nc.scalar.activation(gt1[:, :, :], gt1[:, :, :], ACT.Ln, bias=1.0).then_inc(sp_ready[l], 1)
                    act.wait_ge(d_ready[l], 2 * dr + 1)
                    nc.scalar.activation(gt1[:, :, :], gt2[:, :, :], ACT.Exp, scale=1.0 / TAU
                                         ).then_inc(e_ready[l], 1)
                    nc.scalar.activation(gk[:, :, :], gt2[:, :, :], ACT.Exp, scale=-1.0 / TAU
                                         ).then_inc(e_ready[l], 1)
                    act.wait_ge(e_used[l], 4 * dr + 1)
                    nc.scalar.activation(gt1[:, :, :], gb[:, :, :], ACT.Exp, scale=1.0 / TAU
                                         ).then_inc(e_ready[l], 1)
                    last = 0 if dr else CH - 1
                    nc.scalar.activation(decay[:, dr, :],
                                         gb[:, :, :].rearrange("p g (c n) -> p (g c) n", n=CH)[:, :, last],
                                         ACT.Exp, scale=1.0 / TAU).then_inc(dec_ready[l], 1)
                    act.wait_ge(d_ready[l], 2 * dr + 2)
                    act.wait_ge(e_used[l], 4 * dr + 2)
                    nc.scalar.activation(gk[:, :, :], gt2[:, :, :], ACT.Exp, scale=1.0 / TAU
                                         ).then_inc(e_ready[l], 1)
                    for p in range(GT):
                        act.wait_ge(kt_done[l], 2 * dr + p + 1)
                        if dr and p == 0:
                            act.wait_ge(u_done[l], NTT)
                        nc.scalar.activation(gkt[:, :, p * P:(p + 1) * P],
                                             ps[:, 4 + p, :].rearrange("p (t n) -> p t n", t=NTT),
                                             ACT.Copy).then_inc(kt_out[l], 1)
                    for t in gla_tiles(dr):
                        if t in reads:
                            act.wait_ge(o_done[l], n_o + 1)
                            nc.scalar.activation(
                                go[:, t, 256 * dr:256 * dr + 256].rearrange("p (g b n) -> p b g n", b=2, n=CH),
                                ps[:, 2:4, 0:2 * CH].rearrange("p b (g n) -> p b g n", n=CH),
                                ACT.Copy).then_inc(o_out[l], 1)
                            n_o += 1
                act.wait_ge(ss_ready[l], 1)
                n8 = 8 * len(reads)
                then(nc.scalar.activation(gss[:, 0:n8], gss[:, 0:n8], ACT.Ln, bias=epsc[:, 0:1], scale=1.0 / CH))
                nc.scalar.activation(gss[:, 0:n8], gss[:, 0:n8], ACT.Exp, scale=-0.5).then_inc(grs_ready[l], 1)
                c0 = q_col(l)
                act.wait_ge(yT_done[l], GT)
                for f in range(GT):
                    nc.scalar.activation(hhi[:, AT + f, c0:T], ps[:, 4 + f, c0:T], ACT.Copy,
                                         scale=gla_g[:, l:l + 1]).then_inc(mixhi[l], 1)
                act.wait_ge(conv_out[l], 1)
                for f in range(2):
                    nc.scalar.activation(hhi[:, AT + GT + f, c0:T], s_b[:, f, c0:T], ACT.Copy
                                         ).then_inc(mixhi[l], 1)

            def attention(l):
                tiles = att_tiles(l)
                n_items = len(tiles) * HEADS

                def keys(i):
                    return 4 if tiles[i // HEADS] >= 2 else 2

                def tail(n):
                    act.wait_ge(sk_ready[l], n + 1)
                    nc.scalar.activation(esink[:, :], esink[:, :], ACT.Exp).then_inc(esk_ready[l], 1)
                    act.wait_ge(oT_done[l], n + 1)
                    t = tiles[n]
                    nc.scalar.activation(hhi[:, 0:AT, t * P:(t + 1) * P],
                                         ps[:, 6, :].rearrange("p (j n) -> p j n", j=AT), ACT.Copy
                                         ).then_inc(ahi_ready[l], 1)

                for i in range(n_items + 3):
                    if i >= 11 and i % 8 == 3:
                        tail((i - 11) // 8)
                    if i < n_items:
                        act.wait_ge(negm_ready[l], i + 1)
                        if i >= 3:
                            act.wait_ge(pT_done[l], i - 2)
                        nc.scalar.activation(prob[:, i % 3, 0:keys(i) * P], ps[:, i % 3, 0:keys(i) * P], ACT.Exp,
                                             bias=negm[:, i:i + 1], scale=HD ** -0.5,
                                             accum_out=psumrow[:, i:i + 1]).then_inc(p_ready[l], 1)
                    if 1 <= i <= n_items:
                        j = i - 1
                        act.wait_ge(pT_done[l], j + 1)
                        if j >= 2:
                            act.wait_ge(pv_done[l], j - 1)
                        nc.scalar.activation(probT[:, j % 2, 0:keys(j) * P], ps[:, 3 + j % 2, 0:keys(j) * P],
                                             ACT.Copy).then_inc(pT_out[l], 1)
                tail(len(tiles) - 1)

            def out_projection(l):
                v0 = V_OUT1 if l else V_OUT0
                if l == 0:
                    for n in range(H):
                        hi(v0 + n)
                for m in range(KT):
                    if m:
                        norm_squares(2 * l + 1, m - 1)
                    if m + H < KT:
                        hi(v0 + m + H)
                    else:
                        split_hi(act, None, v0 + m + H, None, None, UNIT)
                norm_squares(2 * l + 1, KT - 1)
                norm_scale(2 * l + 1)
                norm_hi(2 * l + 1)

            def ffn(l, v0, blocks):
                c0 = q_col(l)
                with act.Fori(0, blocks) as i:
                    for r in range(BLOCK):
                        j = r // 2
                        if r < 2 * FJ and r % 2 == 0:
                            act.wait_ge(split_used, i * BLOCK + (v0 + r + 1))
                            if j >= 2:
                                act.wait_ge(fh_ready[l], i * FJ + (j - 1))
                            nc.scalar.activation(sg[:, j % 2, c0:T], ps[:, j % 2, c0:T], ACT.Silu
                                                 ).then_inc(sg_ready[l], 1)
                        if r < 2 * FJ and r % 2 == 1:
                            act.wait_ge(fh_ready[l], i * FJ + (j + 1))
                            nc.scalar.activation(fhi[:, j, c0:T], hf[:, j % 2, c0:T], ACT.Copy
                                                 ).then_inc(fhi_ready[l], 1)
                        b = v0 + r + H
                        cols = DUNIT if 2 * FJ <= r + H < BLOCK else UNIT
                        split_hi(act, None, b, BLOCK, i, cols)

            act.dma_start(c_raw[:, :], d["c"]).then_inc(c_in, 16)
            act.dma_start(xT[:, :, :], d["x"]).then_inc(x_in, 16)
            act.wait_ge(c_in, 16)
            nc.scalar.activation(c_act[:, :], c_raw[:, :], ACT.Silu).then_inc(c_ready, 1)
            act.wait_ge(init_done, 1)
            for k in range(KT):
                norm_squares(0, k)
            norm_scale(0)
            for v in range(H):
                hi(v)
            norm_hi(0)
            projection(0)
            gla(0)
            attention(0)
            out_projection(0)
            ffn(0, V_FFN0, 2)
            for k in range(KT):
                norm_squares(2, k)
            norm_scale(2)
            norm_hi(2)
            projection(1)
            gla(1)
            attention(1)
            out_projection(1)
            act.wait_ge(topd_ready, 1)
            nc.scalar.activation(gate2[:, :, 1:2], gate2[:, :, 0:1], ACT.Exp).then_inc(tope_ready, 1)
            for e in range(NE):
                act.wait_ge(cb_done, e + 1)
                nc.scalar.activation(cb[:, e, :], ps[:, 4 + e % 2, 0:LAT], ACT.Copy).then_inc(cb_out, 1)
            ffn(1, V_MOE, NE)
            for k in range(KT):
                norm_squares(4, k)
            norm_scale(4)

        @block.gpsimd
        def _(pool):
            def norm_lo(n):
                c0 = first_col(n)
                for k in range(KT):
                    pool.wait_ge(hhi_done, KT * n + k + 1)
                    nc.gpsimd.tensor_tensor(hlo[:, k, c0:T], hf[:, k % 2, c0:T], hhi[:, k, c0:T].bitcast(F32),
                                            ALU.subtract).then_inc(hlo_done, 1)

            def ffn(l, blocks):
                c0 = q_col(l)
                with pool.Fori(0, blocks) as i:
                    for j in range(FJ):
                        pool.wait_ge(fhi_ready[l], i * FJ + (j + 1))
                        nc.gpsimd.tensor_tensor(flo[:, j, c0:T], hf[:, j % 2, c0:T], fhi[:, j, c0:T].bitcast(F32),
                                                ALU.subtract).then_inc(flo_ready[l], 1)

            norm_lo(0)
            norm_lo(1)
            ffn(0, 2)
            norm_lo(2)
            norm_lo(3)
            ffn(1, NE)

        @block.vector
        def _(dve):
            V = nc.vector
            done = [0]

            def then(ins):
                done[0] += 1
                ins.then_inc(dve_order, 1)
                dve.wait_ge(dve_order, done[0])

            def lo(v, cols=None):
                split_lo(dve, v, None, None, cols or cols_of(v))

            def take_mods(l, m0, m1, n):
                dve.wait_ge(mod_used, l * MODT + m1)
                V.tensor_tensor(mod[:, l, 2 * m0:2 * m1], ps[:, 7, 2 * m0:2 * m1], b_mod[:, l, 2 * m0:2 * m1],
                                ALU.add).then_inc(mod_out, 1)
                dve.wait_ge(mod_out, n)

            def make_gain(l, which):
                m0 = 2 * (KT + 3 * KT * which)
                then(V.scalar_tensor_tensor(gain[:, l, which, :], mod[:, l, m0:m0 + 2 * KT], 1.0,
                                            norm_g[:, l, which, :], ALU.add, ALU.mult))

            def kinds_of(c0):
                return [(0, 0, CTX), (1, CTX, T)] if c0 == 0 else [(1, CTX, T)]

            def norm_apply(n):
                c0 = first_col(n)
                l, which = n // 2, n % 2
                dve.wait_ge(rs_ready, n + 1)
                for k in range(KT):
                    then(V.tensor_tensor(xn[:, k % 2, c0:T], xT[:, k, c0:T], rs[:, c0:T], ALU.mult))
                    if k >= 2:
                        dve.wait_ge(hlo_done, KT * n + k - 1)
                    for kind, a, b in kinds_of(c0):
                        sh = 2 * (3 * KT * which + k) + kind
                        ins = V.tensor_scalar(hf[:, k % 2, a:b], xn[:, k % 2, a:b],
                                              gain[:, l, which, 2 * k + kind:2 * k + kind + 1],
                                              mod[:, l, sh:sh + 1], ALU.mult, ALU.add)
                        if kind == 1:
                            ins.then_inc(hf_ready, 1)

            def projection(l):
                v0 = V_PROJ1 if l else 0
                c0 = q_col(l)
                kinds = ["f"] * 5 + ["v"] * 4 + ["f"] * 5 + ["g"] * 4 + ["f"] * 6
                f = 0
                for n, kind in enumerate(kinds):
                    if n == 8:
                        dve.wait_ge(split_used, v0 + n + 1)
                        for t in range(NTT):
                            V.tensor_copy(vt[:, t, :], ps[:, 2 + t, 0:384]).then_inc(v_out[l], 1)
                    if kind == "f":
                        if f >= SX:
                            g = f - SX
                            dve.wait_ge(split_used, v0 + n + 1)
                            dve.wait_ge(fm_out[l], SC + g + 1)
                            if g == 0:
                                then(V.memset(cx[:, :, :, :], 0.0))
                            s0 = c0 // CTX
                            V.tensor_tensor(cx[:, g, s0:2, 1:LAT + 1],
                                            ps[:, f % 2, c0:T].rearrange("p (s n) -> p s n", n=LAT),
                                            s_c[:, g, c0:T].rearrange("p (s n) -> p s n", n=LAT),
                                            ALU.mult).then_inc(cx_out[l], 1)
                        f += 1
                    if n + H < PROJ or l:
                        lo(v0 + n + H)

            def conv(l):
                c0 = q_col(l)
                s0 = c0 // CTX
                dve.wait_ge(cx_out[l], 2)
                for g in range(2):
                    y = s_c[:, g, c0:T].rearrange("p (s n) -> p s n", n=LAT)
                    then(V.tensor_scalar(y, cx[:, g, s0:2, 1:LAT + 1], conv_w[:, l, 1, g:g + 1], None, ALU.mult))
                    then(V.scalar_tensor_tensor(y, cx[:, g, s0:2, 0:LAT], conv_w[:, l, 0, g:g + 1], y,
                                                ALU.mult, ALU.add))
                    then(V.scalar_tensor_tensor(y, cx[:, g, s0:2, 2:LAT + 2], conv_w[:, l, 2, g:g + 1], y,
                                                ALU.mult, ALU.add))
                    ins = V.tensor_tensor(s_b[:, g, c0:T], s_c[:, g, c0:T], s_b[:, g, c0:T], ALU.mult)
                    if g == 0:
                        then(ins)
                ins.then_inc(conv_out[l], 1)

            def gla(l):
                reads = list(gla_reads(l))
                c0 = q_col(l)
                n_at = 0

                def chunks(x):
                    return x[:, :, :].rearrange("p g (c n) -> p (g c) n", n=CH)

                then(V.memset(am[:, :, :], 0.0))
                then(V.memset(state[:, :, 0, :], 0.0))
                for dr in range(2):
                    for p in range(GT):
                        dve.wait_ge(abs_done[l], 2 * dr + p + 1)
                        if dr and p == 0:
                            dve.wait_ge(e_ready[l], 4)
                        then(V.tensor_scalar(gt2[:, p, :], ps[:, 2 * dr + p, :], gla_b[:, l, dr, p:p + 1], 0.0,
                                             ALU.add, ALU.min))
                    dve.wait_ge(sp_ready[l], dr + 1)
                    then(V.tensor_tensor(gt2[:, :, :], gt2[:, :, :], gt1[:, :, :], ALU.subtract))
                    if dr:
                        dve.wait_ge(dec_ready[l], 1)
                    for p in range(GT):
                        if dr == 0:
                            o, m, x = gb[:, p, :], reset[:, :], gt2[:, p, :]
                        else:
                            o, m, x = gb[:, p, ::-1], reset[:, :], gt2[:, p, ::-1]
                        then(V.tensor_tensor_scan(o, m, x, 0.0, ALU.mult, ALU.add))
                    ref = CH // 2 if dr == 0 else CH - 1 - CH // 2
                    last = 0 if dr else CH - 1
                    V.tensor_tensor(chunks(gt2), chunks(gb),
                                    chunks(gb)[:, :, ref:ref + 1].broadcast_to([P, GT * NCH, CH]), ALU.subtract
                                    ).then_inc(d_ready[l], 1)
                    dve.wait_ge(e_ready[l], 4 * dr + 1)
                    if dr:
                        dve.wait_ge(o_done[l], len(reads))
                    V.scalar_tensor_tensor(gqp[:, :, c0:T], gt1[:, :, c0:T], HD ** -0.5, lq[:, :, c0:T],
                                           ALU.mult, ALU.mult).then_inc(e_used[l], 1)
                    dve.wait_ge(e_ready[l], 4 * dr + 2)
                    V.tensor_tensor(gkp[:, :, :], gk[:, :, :], lk[:, :, :], ALU.mult).then_inc(e_used[l], 1)
                    V.tensor_tensor(chunks(gt2), chunks(gb)[:, :, last:last + 1].broadcast_to([P, GT * NCH, CH]),
                                    chunks(gb), ALU.subtract).then_inc(d_ready[l], 1)
                    dve.wait_ge(e_ready[l], 4 * dr + 3)
                    V.scalar_tensor_tensor(gqb[:, :, c0:T], gt1[:, :, c0:T], HD ** -0.5, lq[:, :, c0:T],
                                           ALU.mult, ALU.mult).then_inc(e_used[l], 1)
                    dve.wait_ge(e_ready[l], 4 * dr + 4)
                    V.tensor_tensor(gk[:, :, :], gk[:, :, :], lk[:, :, :], ALU.mult).then_inc(e_used[l], 1)
                    dve.wait_ge(dec_ready[l], dr + 1)
                    for step, t in enumerate(gla_tiles(dr)):
                        n_u = NTT * dr + step
                        if t in reads:
                            dve.wait_ge(at_done[l], n_at + 1)
                            if n_at:
                                dve.wait_ge(o_done[l], n_at)
                            V.copy_predicated(am[:, dr, :].rearrange("p (b n) -> p b n", b=2),
                                              gmask[:, dr, :].rearrange("p (b n) -> p b n", b=2),
                                              ps[:, 0:2, 0:2 * P]).then_inc(am_ready[l], 1)
                            n_at += 1
                        dve.wait_ge(u_done[l], n_u + 1)
                        for ci, c in enumerate(gla_chunks(dr)):
                            for p in range(GT):
                                col = p * NCH + 2 * t + c
                                ins = V.scalar_tensor_tensor(
                                    state[:, dr, 2 * step + ci + 1, p * CH:(p + 1) * CH],
                                    state[:, dr, 2 * step + ci, p * CH:(p + 1) * CH],
                                    decay[:, dr, col:col + 1],
                                    ps[:, (6, 4)[n_u % 2] + c, p * CH:(p + 1) * CH], ALU.mult, ALU.add)
                            ins.then_inc(st_ready[l], 1)
                            dve.wait_ge(st_ready[l], 2 * n_u + ci + 1)
                n = len(reads)
                t0 = reads[0]
                o4 = go[:, t0:NTT, :]
                sqv = gtt[:, :, :, :].rearrange("p a g t -> p (a g t)")[:, 0:512 * n]
                dve.wait_ge(o_out[l], 2 * n)
                then(V.tensor_tensor(sqv.rearrange("p (t n) -> p t n", t=n), o4, o4, ALU.mult))
                V.tensor_reduce(gss[:, 0:8 * n], sqv.rearrange("p (h n) -> p h n", n=CH), AX.X, ALU.add
                                ).then_inc(ss_ready[l], 1)
                then(V.tensor_tensor(o4, o4, gate[:, t0:NTT, :], ALU.mult))
                dve.wait_ge(grs_ready[l], 1)
                oh = o4.rearrange("p t (h n) -> p (t h) n", n=CH)
                then(V.tensor_tensor(oh, oh, gss[:, 0:8 * n].rearrange("p (h o) -> p h o", o=1
                                                                       ).broadcast_to([P, 8 * n, CH]), ALU.mult))
                yv = gb[:, 0:n // 2, :].rearrange("p g (t n) -> p (g t) n", n=256)
                V.tensor_tensor(yv, o4[:, :, 0:256], o4[:, :, 256:512], ALU.add).then_inc(y_ready[l], 1)
                for f in range(GT):
                    dve.wait_ge(mixhi[l], f + 1)
                    V.scalar_tensor_tensor(hlo[:, AT + f, c0:T], ps[:, 4 + f, c0:T], gla_g[:, l:l + 1],
                                           hhi[:, AT + f, c0:T].bitcast(F32), ALU.mult, ALU.subtract
                                           ).then_inc(mixlo[l], 1)
                for f in range(2):
                    dve.wait_ge(mixhi[l], GT + f + 1)
                    V.tensor_tensor(hlo[:, AT + GT + f, c0:T], s_b[:, f, c0:T],
                                    hhi[:, AT + GT + f, c0:T].bitcast(F32), ALU.subtract).then_inc(mixlo[l], 1)

            def attention(l):
                tiles = att_tiles(l)
                n_items = len(tiles) * HEADS
                dve.wait_ge(y_ready[l], 1)
                dve.wait_ge(yT_done[l], GT)
                dve.wait_ge(rot_done[l], 1)
                r1 = rt1.rearrange("p (j n) -> p j n", j=AT)
                r2 = rt2.rearrange("p (j n) -> p j n", j=AT)
                V.tensor_tensor(r1, aq[:, :, CTX:T], cos[:, :].rearrange("p (o n) -> p o n", o=1
                                                                        ).broadcast_to([P, AT, LAT]), ALU.mult)
                then(V.tensor_tensor(r2, ps[:, 0:2, :].rearrange("p b (j n) -> p (b j) n", j=2),
                                     sin[:, :].rearrange("p (o n) -> p o n", o=1).broadcast_to([P, AT, LAT]),
                                     ALU.mult))
                then(V.tensor_tensor(aq[:, :, CTX:T], r1, r2, ALU.add))
                then(V.tensor_tensor(rt1[:, 0:LAT], ak[:, CTX:T], cos[:, :], ALU.mult))
                then(V.tensor_tensor(rt2[:, 0:LAT], ps[:, 2, 0:LAT], sin[:, :], ALU.mult))
                V.tensor_tensor(ak[:, CTX:T], rt1[:, 0:LAT], rt2[:, 0:LAT], ALU.add).then_inc(rope_out[l], 1)

                def tail(n):
                    cols = slice(n * HEADS, (n + 1) * HEADS)
                    if n:
                        dve.wait_ge(esk_ready[l], n)
                    dve.wait_ge(negm_ready[l], (n + 1) * HEADS)
                    V.tensor_tensor(esink[:, :], sink[:, l, :], negm[:, cols], ALU.add).then_inc(sk_ready[l], 1)
                    dve.wait_ge(esk_ready[l], n + 1)
                    dve.wait_ge(p_ready[l], (n + 1) * HEADS)
                    then(V.tensor_tensor(rden[:, :], psumrow[:, cols], esink[:, :], ALU.add))
                    then(V.reciprocal(rden[:, :], rden[:, :]))
                    dve.wait_ge(pv_done[l], (n + 1) * HEADS)
                    if n:
                        dve.wait_ge(oT_done[l], n)
                    V.tensor_tensor(osb.rearrange("p (h n) -> p h n", n=HD),
                                    ps[:, 5, :].rearrange("p (h n) -> p h n", n=HD),
                                    rden[:, :].rearrange("p (h o) -> p h o", o=1).broadcast_to([P, HEADS, HD]),
                                    ALU.mult).then_inc(osb_ready[l], 1)
                    dve.wait_ge(ahi_ready[l], n + 1)
                    t = tiles[n]
                    V.tensor_tensor(hlo[:, 0:AT, t * P:(t + 1) * P],
                                    ps[:, 6, :].rearrange("p (j n) -> p j n", j=AT),
                                    hhi[:, 0:AT, t * P:(t + 1) * P].bitcast(F32), ALU.subtract
                                    ).then_inc(alo_ready[l], 1)

                for i in range(n_items):
                    if i >= 11 and i % 8 == 3:
                        tail((i - 11) // 8)
                    t, h = tiles[i // HEADS], i % HEADS
                    n_k = 4 if t >= 2 else 2
                    dve.wait_ge(s_done[l], i + 1)
                    if t >= 2:
                        blk = slice(3 * P, 4 * P) if t == 2 else slice(2 * P, 3 * P)
                        then(V.tensor_tensor(ps[:, i % 3, blk], ps[:, i % 3, blk], amask[:, t - 2, :], ALU.add))
                    then(V.tensor_reduce(mx[:, i:i + 1], ps[:, i % 3, 0:n_k * P], AX.X, ALU.max))
                    V.tensor_scalar(negm[:, i:i + 1], mx[:, i:i + 1], -(HD ** -0.5), negsink[:, l, h:h + 1],
                                    ALU.mult, ALU.min).then_inc(negm_ready[l], 1)
                tail(len(tiles) - 1)

            def out_projection(l):
                v0 = V_OUT1 if l else V_OUT0
                c0 = q_col(l)
                if l == 0:
                    take_mods(1, 0, MODT, 3)
                    make_gain(1, 0)
                    make_gain(1, 1)
                    for n in range(H):
                        lo(v0 + n)
                for m in range(KT):
                    dve.wait_ge(split_used, v0 + m + 1)
                    for kind, a, b in kinds_of(c0):
                        g = 2 * (2 * KT + m) + kind
                        ins = V.scalar_tensor_tensor(xT[:, m, a:b], ps[:, m % 2, a:b], mod[:, l, g:g + 1],
                                                     xT[:, m, a:b], ALU.mult, ALU.add)
                        if kind == 1:
                            ins.then_inc(x_mixed[l], 1)
                    lo(v0 + m + H, UNIT)
                norm_apply(2 * l + 1)

            def ffn(l, v0, blocks):
                c0 = q_col(l)
                dve.sem_inc(down_out[l], 1)
                with dve.Fori(0, blocks) as i:
                    for r in range(BLOCK):
                        if r < 2 * FJ and r % 2 == 1:
                            j = r // 2
                            dve.wait_ge(split_used, i * BLOCK + (v0 + r + 1))
                            dve.wait_ge(sg_ready[l], i * FJ + (j + 1))
                            if l == 0:
                                dve.wait_ge(flo_ready[l], i * FJ + (j - 1)) if j >= 2 else None
                                V.tensor_tensor(hf[:, j % 2, c0:T], ps[:, 2 + j % 2, c0:T], sg[:, j % 2, c0:T],
                                                ALU.mult).then_inc(fh_ready[l], 1)
                            else:
                                V.tensor_tensor(sg[:, j % 2, c0:T], ps[:, 2 + j % 2, c0:T], sg[:, j % 2, c0:T],
                                                ALU.mult).then_inc(swiglu_ready, 1)
                                dve.wait_ge(swiglu_ready, i * FJ + (j + 1))
                                dve.wait_ge(flo_ready[l], i * FJ + (j - 1)) if j >= 2 else None
                                V.tensor_tensor(hf[:, j % 2, c0:T], sg[:, j % 2, c0:T],
                                                cb[:, bass.ds(i, 1), :].rearrange("p a n -> p (a n)"),
                                                ALU.mult).then_inc(fh_ready[l], 1)
                        if r >= 2 * FJ:
                            m = r - 2 * FJ
                            dve.wait_ge(split_used, i * BLOCK + (v0 + r + 1))
                            if l == 0:
                                for kind, a, b in kinds_of(c0):
                                    g = 2 * (5 * KT + m) + kind
                                    ins = V.scalar_tensor_tensor(xT[:, m, a:b], ps[:, 4 + m % 2, a:b],
                                                                 mod[:, l, g:g + 1], xT[:, m, a:b],
                                                                 ALU.mult, ALU.add)
                            else:
                                ins = V.tensor_tensor(yacc[:, m, :], yacc[:, m, :], ps[:, 4 + m % 2, c0:T], ALU.add)
                            ins.then_inc(down_out[l], 1)
                        b = v0 + r + H
                        cols = DUNIT if 2 * FJ <= r + H < BLOCK else UNIT
                        split_lo(dve, b, BLOCK, i, cols)

            then(V.memset(ones[:, :], 1.0))
            V.memset(epsc[:, :], EPS).then_inc(init_done, 1)
            dve.wait_ge(const_in, 16 * N_CONST)
            then(V.tensor_scalar(negsink[:, :, :], sink[:, :, :], -1.0, None, ALU.mult))
            take_mods(0, 0, M0, 1)
            make_gain(0, 0)
            for v in range(H):
                lo(v)
            dve.wait_ge(x_in, 16)
            norm_apply(0)
            projection(0)
            take_mods(0, M0, MODT, 2)
            make_gain(0, 1)
            conv(0)
            gla(0)
            attention(0)
            out_projection(0)
            ffn(0, V_FFN0, 2)
            dve.wait_ge(down_out[0], 1 + 2 * KT)
            norm_apply(2)
            projection(1)
            conv(1)
            gla(1)
            attention(1)
            out_projection(1)
            then(V.memset(yacc[:, :, :], 0.0))
            dve.wait_ge(lg_done, 1)
            then(V.tensor_copy(logits[:, :, :], ps[:, 7, 0:2 * NE].rearrange("p (t e) -> p t e", t=2)))
            for t in range(2):
                then(V.max(top[:, t, :], logits[:, t, :]))
                then(V.max_index(topi[:, t, :], top[:, t, :], logits[:, t, :]))
            then(V.tensor_copy(topf[:, :, :], topi[:, :, :]))
            V.tensor_tensor(gate2[:, :, 0:1], top[:, :, 1:2], top[:, :, 0:1], ALU.subtract).then_inc(topd_ready, 1)
            dve.wait_ge(tope_ready, 1)
            then(V.tensor_scalar(gate2[:, :, 2:3], gate2[:, :, 1:2], 1.0, None, ALU.add))
            then(V.reciprocal(gate2[:, :, 2:3], gate2[:, :, 2:3]))
            then(V.tensor_tensor(gate2[:, :, 3:4], gate2[:, :, 1:2], gate2[:, :, 2:3], ALU.mult))
            for t in range(2):
                for w in range(2):
                    then(V.tensor_scalar(pick[:, t, w, :], iota[:, :], topf[:, t, w:w + 1],
                                         gate2[:, t, 2 + w:3 + w], ALU.is_equal, ALU.mult))
                then(V.tensor_tensor(pick[:, t, 0, :], pick[:, t, 0, :], pick[:, t, 1, :], ALU.add))
            for e in range(NE):
                if e >= 2:
                    dve.wait_ge(cb_done, e - 1)
                for t in range(2):
                    V.tensor_scalar(diag[:, e % 2, t, :], ident[:, :], pick[:, t, 0, e:e + 1], None,
                                    ALU.mult).then_inc(diag_ready, 1)
            dve.wait_ge(cb_out, NE)
            ffn(1, V_MOE, NE)
            for m in range(KT):
                if m == 0:
                    dve.wait_ge(down_out[1], 1 + NE * KT)
                g = 2 * (5 * KT + m) + 1
                V.scalar_tensor_tensor(xT[:, m, CTX:T], yacc[:, m, :], mod[:, 1, g:g + 1], xT[:, m, CTX:T],
                                       ALU.mult, ALU.add).then_inc(x_last, 1)
            dve.wait_ge(rs_ready, 4 + 1)
            for k in range(KT):
                then(V.tensor_tensor(xn[:, k % 2, CTX:T], xT[:, k, CTX:T], rs[:, CTX:T], ALU.mult))
                V.tensor_scalar(outT[:, k, :], xn[:, k % 2, CTX:T], final_g[:, k:k + 1], None,
                                ALU.mult).then_inc(out_ready, 1)



CONST_NAMES = ["ident", "rot", "cos", "sin", "amask", "gmask", "reset", "iota", "b_mod", "norm_g", "final_g",
               "sink", "w2", "gla_b", "gla_g", "conv_w", "router"]
N_CONST = len(CONST_NAMES)


def CONSTS(locals_):
    return [(n, locals_[n]) for n in CONST_NAMES]


def _constants():
    p = np.arange(P)
    f32 = np.float32
    rot = np.zeros((P, P), f32)
    for m in range(P):
        if m % HD < HD // 2:
            rot[m + HD // 2, m] = -1.0
        else:
            rot[m - HD // 2, m] = 1.0
    nf = HD // 4
    inv = (f32(10000.0) ** (-np.arange(nf, dtype=f32) / f32(nf))).astype(f32)
    tok = np.arange(LAT)
    ang = np.concatenate([(tok // 64).astype(f32)[:, None] * inv, (tok % 64).astype(f32)[:, None] * inv], 1)
    ang = ang[:, p % (HD // 2)].T
    q, k = p[:, None], p[None, :]
    amask = np.stack([np.where(k <= q, 0.0, -1e30), np.where(q <= k, 0.0, -1e30)], 1).astype(f32)
    s, t = p[:, None], p[None, :]
    same = s // CH == t // CH
    gmask = np.stack([np.tile(same & (s <= t), (1, 4)), np.tile(same & (s >= t), (1, 4))], 1).astype(np.int32)
    reset = np.broadcast_to((np.arange(T) % CH != 0).astype(f32), (P, T))
    return dict(ident=np.eye(P, dtype=f32), rot=rot, cos=np.cos(ang), sin=np.sin(ang), amask=amask, gmask=gmask,
                reset=reset, iota=np.broadcast_to(np.arange(NE, dtype=f32), (P, NE)))


def _units(w, n):
    k, cols = w.shape
    return w.reshape(k // P, P, cols // n, n).transpose(2, 1, 0, 3).reshape(cols // n, P, k // P * n)


def _layout(a):
    f = {n: np.asarray(v) for n, v in a.items()}
    o = _constants()
    o["x"] = np.concatenate([f["ctx"][0], f["x"][0]], 0).T.reshape(KT, P, T).transpose(1, 0, 2)
    o["c"] = np.stack([f["c_ctx"], f["c"][0]], 1).reshape(KT, P, 2).transpose(1, 0, 2).reshape(P, 2 * KT)
    o["w_mod"] = np.stack([_units(f["w_mod"][l], P) for l in range(LAYERS)])

    def cols(v, tiles):
        return np.repeat(v.reshape(tiles, P).T[:, :, None], 2, 2).reshape(P, 2 * tiles)

    o["b_mod"] = np.stack([cols(f["b_mod"][l], MODT) for l in range(LAYERS)], 1)
    o["norm_g"] = np.stack([np.stack([cols(f[n][l], KT) for n in ("norm1_g", "norm2_g")], 1)
                            for l in range(LAYERS)], 1)
    o["final_g"] = f["final_norm_g"].reshape(KT, P).T
    pair = [h for j in range(AT) for h in (j, AT + j)]
    o["sink"] = np.broadcast_to(f["attn_sink"][:, pair], (P, LAYERS, HEADS))
    fm, tv, tg, wo, w2 = [], [], [], [], []
    for l in range(LAYERS):
        w = f["w_in"][l]
        z = np.zeros((D, 16), w.dtype)
        la = np.concatenate([w[:, 2048:2064], z, w[:, 2064:2080], z, np.zeros((D, 64), w.dtype)], 1)
        aq = w[:, 0:512].reshape(D, HEADS, HD)[:, pair].reshape(D, 512)
        fm.append(_units(np.concatenate([la, w[:, 1024:1280], w[:, 768:1024], w[:, 512:640], aq,
                                         w[:, 2080:2848]], 1), P))
        for dst, c in ((tv, np.r_[640:768, 1280:1536]), (tg, np.r_[1536:2048])):
            n = len(c)
            dst.append(w[:, c].reshape(KT // 2, 2, P, n).transpose(0, 2, 1, 3).reshape(KT // 2, P, 2 * n))
        wout = f["w_out"][l]
        wo.append(_units(np.concatenate([wout[0:512].reshape(HEADS, HD, D)[pair].reshape(512, D), wout[512:]], 0),
                         P))
        z = np.zeros((16, GT * P), w.dtype)
        w2.append(np.concatenate([f["gla_w2_f"][l], z, f["gla_w2_b"][l], z], 0))
    o["w_fm"], o["w_tv"], o["w_tg"], o["w_out"] = map(np.stack, (fm, tv, tg, wo))
    o["w2"] = np.stack(w2, 1)
    o["gla_b"] = np.stack([np.stack([f[n][l].reshape(GT, P).T for n in ("gla_b_f", "gla_b_b")], 1)
                           for l in range(LAYERS)], 1)
    o["gla_g"] = np.stack([np.tile(f["gla_norm_g"][l], 2) for l in range(LAYERS)], 1)
    o["conv_w"] = np.stack([f["conv_w"][l].reshape(3, 2, P).transpose(2, 0, 1) for l in range(LAYERS)], 1)
    o["router"] = f["router_w"][0].reshape(KT, P, NE).transpose(1, 0, 2)

    def gate_up(w):
        k, n = w.shape
        return _units(w, P).reshape(2, n // 2 // P, P, UNIT).transpose(1, 0, 2, 3).reshape(n // P, P, UNIT)

    o["w_gu0"] = gate_up(f["ffn_w_gu"][0])
    o["w_dn0"] = np.concatenate([_units(f["ffn_w_down"][0][b * DUNIT:(b + 1) * DUNIT], P) for b in range(2)], 0)
    gu = [gate_up(f["expert_w_gu"][0, e]) for e in range(NE)]
    o["w_gu1"] = np.concatenate(gu + [np.zeros((H, P, UNIT), gu[0].dtype)], 0)
    o["w_dn1"] = np.concatenate([_units(f["expert_w_down"][0, e], P) for e in range(NE)], 0)
    return o


def kernel(**inputs):
    import concourse.bacc as _bacc
    from concourse.bass_utils import run_bass_kernel_spmd as _run

    nc = _bacc.Bacc("TRN2", target_bir_lowering=False, num_devices=1)
    arrays, aps = {}, {}
    for name, a in _layout(inputs).items():
        a = np.ascontiguousarray(a)
        arrays[f"in_{name}"] = a
        aps[name] = nc.dram_tensor(f"in_{name}", a.shape, mybir.dt.from_np(a.dtype), kind="ExternalInput").ap()
    aps["w_gu"] = [aps["w_gu0"], aps["w_gu1"]]
    aps["w_dn"] = [aps["w_dn0"], aps["w_dn1"]]
    out = nc.dram_tensor("out", (P, KT, LAT), F32, kind="ExternalOutput").ap()
    build(nc, aps, out)
    r = _run(nc, [arrays], core_ids=[0])
    return r.results[0]["out"].transpose(1, 0, 2).reshape(D, LAT).T.reshape(1, LAT, D)
```

```python
from contextlib import ExitStack

import numpy as np

import concourse.bass as bass
from concourse import mybir

F32 = mybir.dt.float32
F32R = mybir.dt.float32r
I32 = mybir.dt.int32
U32 = mybir.dt.uint32
ALU = mybir.AluOpType
ACT = mybir.ActivationFunctionType
AX = mybir.AxisListType

P = 128
D = 1024
KT = D // P
CTX, LAT = 256, 256
T = CTX + LAT
NTT = T // P
EPS = 1e-6
LAYERS = 2
HEADS, HD = 8, 64
AT = HEADS * HD // P
CH = 64
NCH = T // CH
GT = 2
TAU = 16.0
FM = 16
FJ = 11
NE = 8
MODT = 6 * D // P
UNIT = KT * P
DUNIT = FJ * P
R = 5
H = 3
PROJ, OUT, BLOCK = FM + 8, KT, 2 * FJ + KT
M0 = 16

LA, LK, LQ, AK, AQ, SB, SC, SX = 0, 1, 3, 5, 6, 10, 12, 14


def build(nc, d, out):
    ctx = ExitStack()
    with ctx:
        def sb(name, shape, dt=F32, stack=ctx):
            return stack.enter_context(nc.sbuf_tensor(name, shape, dt))

        raw = sb("raw", [P, R, DUNIT])
        whi = sb("whi", [P, H, DUNIT], F32R)
        wlo = sb("wlo", [P, H, DUNIT], F32R)
        xT = sb("xT", [P, KT, T])
        ident = sb("ident", [P, P])
        rot = sb("rot", [P, P])
        ones = sb("ones", [P, P])
        cos = sb("cos", [P, LAT])
        sin = sb("sin", [P, LAT])
        amask = sb("amask", [P, 2, P])
        gmask = sb("gmask", [P, 2, P], I32)
        reset = sb("reset", [P, T])
        iota = sb("iota", [P, NE])
        c_raw = sb("c_raw", [P, 2 * KT])
        c_act = sb("c_act", [P, KT, 2])
        c_split = sb("c_split", [P, KT, 4], F32R)
        modrow = sb("modrow", [4, 2, 512])
        modsum = sb("modsum", [P, 2, 8])
        b_mod = sb("b_mod", [P, LAYERS, 2 * MODT])
        norm_g = sb("norm_g", [P, LAYERS, 2, 2 * KT])
        final_g = sb("final_g", [P, KT])
        sink = sb("sink", [P, LAYERS, HEADS])
        w2 = sb("w2", [CH, LAYERS, GT * P])
        gla_b = sb("gla_b", [P, LAYERS, 2, GT])
        gla_g = sb("gla_g", [P, LAYERS])
        conv_w = sb("conv_w", [P, LAYERS, 3, 2])
        router = sb("router", [P, KT, NE])
        mod = sb("mod", [P, LAYERS, 2 * MODT])
        gain = sb("gain", [P, LAYERS, 2, 2 * KT])
        epsc = sb("epsc", [P, 1])
        rs = sb("rs", [P, T])
        sq = sb("sq", [P, 2, T])
        xn = sb("xn", [P, 2, T])
        hf = sb("hf", [P, 2, T])
        negsink = sb("negsink", [P, LAYERS, HEADS])
        mx = sb("mx", [P, NTT * HEADS])
        negm = sb("negm", [P, NTT * HEADS])
        psumrow = sb("psumrow", [P, NTT * HEADS])
        esink = sb("esink", [P, NTT * HEADS])
        rden = sb("rden", [P, NTT * HEADS])
        decay = sb("decay", [P, 2, GT * NCH])
        gss = sb("gss", [P, NTT * 8])
        logits = sb("logits", [P, 2, NE])
        top = sb("top", [P, 2, 8])
        topi = sb("topi", [P, 2, 8], U32)
        topf = sb("topf", [P, 2, 8])
        gate2 = sb("gate2", [P, 2, 4])
        pick = sb("pick", [P, 2, 2, NE])

        region = ExitStack()
        hhi = sb("hhi", [P, KT, T], F32R, region)
        hlo = sb("hlo", [P, KT, T], F32R, region)
        region.close()
        gtt = sb("gtt", [P, 2, GT, T])
        gt1, gt2 = gtt[:, 0, :, :], gtt[:, 1, :, :]
        gqp = sb("gqp", [P, 2, GT, T])
        gqb = sb("gqb", [P, 2, GT, T])
        gkt = sb("gkt", [P, NTT, 2, GT * P])
        gb, gkp, gk = sq, xn, hf

        region = ExitStack()
        fhi = sb("fhi", [P, FJ, T], F32R, region)
        flo = sb("flo", [P, FJ, T], F32R, region)
        sg = sb("sg", [P, 2, T], F32, region)
        yacc = sb("yacc", [P, KT, LAT], F32, region)
        cb = sb("cb", [P, NE, LAT], F32, region)
        diag = sb("diag", [P, 2, 2, P], F32, region)
        region.close()
        region = ExitStack()
        la = sb("la", [CH, T], F32, region)
        lk = sb("lk", [P, GT, T], F32, region)
        lq = sb("lq", [P, GT, T], F32, region)
        ak = sb("ak", [P, T], F32, region)
        aq = sb("aq", [P, AT, T], F32, region)
        s_b = sb("s_b", [P, 2, T], F32, region)
        s_c = sb("s_c", [P, 2, T], F32, region)
        cx = sb("cx", [P, 2, 2, LAT + 2], F32, region)
        vt = sb("vt", [P, NTT, 384], F32, region)
        gate = sb("gate", [P, NTT, 512], F32, region)
        part = ExitStack()
        state = sb("state", [P, 2, NCH + 1, GT * CH], F32, part)
        am = sb("am", [P, 2, 4 * P], F32, part)
        go = sb("go", [P, NTT, 512], F32, part)
        part.close()
        asc = sb("asc", [P, 3072], F32, region)
        akz = sb("akz", [P, 2, T], F32, region)
        region.close()
        region = ExitStack()
        outT = sb("outT", [P, KT, LAT], F32, region)
        region.close()

        prob = asc[:, 0:1536].rearrange("p (s n) -> p s n", s=3)
        probT = asc[:, 1536:2560].rearrange("p (s n) -> p s n", s=2)
        rt1 = asc[:, 0:1024]
        rt2 = asc[:, 1024:2048]

        ps = ctx.enter_context(nc.psum_tensor("ps", [P, 8, 512], F32))

        def sem(name):
            return ctx.enter_context(nc.semaphore(name))

        def sems(name, n):
            return [sem(f"{name}{i}") for i in range(n)]

        landed = sems("landed", R)
        hi_ready = sem("hi_ready")
        lo_ready = sem("lo_ready")
        split_used = sem("split_used")
        mod_done = sem("mod_done")
        modrow_out = sem("modrow_out")
        modT_done = sem("modT_done")
        mod_out = sem("mod_out")
        c_done = sem("c_done")
        c_hi = sem("c_hi")
        const_in = sem("const_in")
        x_in = sem("x_in")
        c_in = sem("c_in")
        init_done = sem("init_done")
        gain_ready = sem("gain_ready")
        sq_ready = sem("sq_ready")
        sumsq_done = sem("sumsq_done")
        rs_ready = sem("rs_ready")
        hf_ready = sem("hf_ready")
        hhi_done = sem("hhi_done")
        hlo_done = sem("hlo_done")
        fm_done = sems("fm_done", LAYERS)
        fm_out = sems("fm_out", LAYERS)
        cx_out = sems("cx_out", LAYERS)
        v_done = sems("v_done", LAYERS)
        v_out = sems("v_out", LAYERS)
        g_done = sems("g_done", LAYERS)
        g_out = sems("g_out", LAYERS)
        conv_out = sems("conv_out", LAYERS)
        z_done = sems("z_done", LAYERS)
        abs_done = sems("abs_done", LAYERS)
        sp_ready = sems("sp_ready", LAYERS)
        d_ready = sems("d_ready", LAYERS)
        e_ready = sems("e_ready", LAYERS)
        e_used = sems("e_used", LAYERS)
        kt_done = sems("kt_done", LAYERS)
        kt_out = sems("kt_out", LAYERS)
        dec_ready = sems("dec_ready", LAYERS)
        u_done = sems("u_done", LAYERS)
        st_ready = sems("st_ready", LAYERS)
        at_done = sems("at_done", LAYERS)
        am_ready = sems("am_ready", LAYERS)
        o_done = sems("o_done", LAYERS)
        o_out = sems("o_out", LAYERS)
        ss_ready = sems("ss_ready", LAYERS)
        grs_ready = sems("grs_ready", LAYERS)
        y_ready = sems("y_ready", LAYERS)
        yT_done = sems("yT_done", LAYERS)
        mixhi = sems("mixhi", LAYERS)
        mixlo = sems("mixlo", LAYERS)
        rot_done = sems("rot_done", LAYERS)
        s_done = sems("s_done", LAYERS)
        negm_ready = sems("negm_ready", LAYERS)
        p_ready = sems("p_ready", LAYERS)
        pT_done = sems("pT_done", LAYERS)
        pT_out = sems("pT_out", LAYERS)
        pv_done = sems("pv_done", LAYERS)
        esk_ready = sems("esk_ready", LAYERS)
        pn_ready = sems("pn_ready", LAYERS)
        akz_ready = sems("akz_ready", LAYERS)
        zeroed = sems("zeroed", LAYERS)
        ahi_ready = sems("ahi_ready", LAYERS)
        alo_ready = sems("alo_ready", LAYERS)
        proj_done = sems("proj_done", LAYERS)
        x_mixed = sems("x_mixed", LAYERS)
        gate_done = sems("gate_done", LAYERS)
        up_done = sems("up_done", LAYERS)
        sg_ready = sems("sg_ready", LAYERS)
        fh_ready = sems("fh_ready", LAYERS)
        fhi_ready = sems("fhi_ready", LAYERS)
        flo_ready = sems("flo_ready", LAYERS)
        down_done = sems("down_done", LAYERS)
        down_out = sems("down_out", LAYERS)
        swiglu_ready = sem("swiglu_ready")
        lg_done = sem("lg_done")
        topd_ready = sem("topd_ready")
        tope_ready = sem("tope_ready")
        diag_ready = sem("diag_ready")
        cb_done = sem("cb_done")
        cb_out = sem("cb_out")
        x_last = sem("x_last")
        out_ready = sem("out_ready")
        stored = sem("stored")
        act_order = sem("act_order")
        dve_order = sem("dve_order")

        def mods(l, q0, q1):
            return [("mod", l, q) for q in range(q0, q1)]

        def proj_units(l):
            fm = [("fm", l, m) for m in range(FM)]
            return (fm[:5] + [("tv", l, i) for i in range(4)] + fm[5:10] + [("tg", l, i) for i in range(4)]
                    + fm[10:])

        START = mods(0, 0, M0)
        proj0 = []
        q = M0
        for n, unit in enumerate(proj_units(0)):
            proj0.append(unit)
            more = min(MODT - q, 1 if n < 16 else 2)
            proj0 += mods(0, q, q + more)
            q += more
        assert q == MODT
        GLA_MODS, ATT_MODS = 16, 32
        PROJ_STAGE = [proj0, proj_units(1)]
        OUT_STAGE = [[("out", l, m) for m in range(OUT)] for l in range(LAYERS)]
        stream0 = START + proj0 + mods(1, 0, MODT) + OUT_STAGE[0]
        stream1 = PROJ_STAGE[1] + OUT_STAGE[1]
        V_PROJ = [len(START), len(stream0) + 2 * BLOCK]
        V_GLA0 = V_PROJ[0] + len(proj0)
        V_ATT0 = V_GLA0 + GLA_MODS
        V_OUT = [V_ATT0 + ATT_MODS, V_PROJ[1] + PROJ]
        V_FFN = [len(stream0), V_OUT[1] + OUT]
        V_END = V_FFN[1] + NE * BLOCK
        assert V_OUT[0] + OUT == V_FFN[0]

        def source(unit):
            kind, l, n = unit
            if kind == "mod":
                return d["w_mod"][l, n], UNIT
            if kind == "fm":
                return d["w_fm"][l, n], UNIT
            if kind == "tv":
                return d["w_tv"][l, n], 768
            if kind == "tg":
                return d["w_tg"][l, n], UNIT
            return d["w_out"][l, n], UNIT

        def unit_of(v):
            if v < len(stream0):
                return stream0[v]
            if V_PROJ[1] <= v < V_FFN[1]:
                return stream1[v - V_PROJ[1]]
            return None

        def cols_of(v):
            unit = unit_of(v)
            return source(unit)[1] if unit else UNIT

        def block_unit(l, i, r):
            if r < 2 * FJ:
                src = d["w_gu"][l][bass.ds(i * 2 * FJ + r, 1)]
                n = UNIT
            else:
                src = d["w_dn"][l][bass.ds(i * KT + r - 2 * FJ, 1)]
                n = DUNIT
            return src.rearrange("a p n -> (a p) n"), n

        block = ctx.enter_context(nc.Block())

        @block.sync
        def _(sp):
            def load(v, src, n):
                if v >= R:
                    sp.wait_ge(lo_ready, v - R + 1)
                sp.dma_start(raw[:, v % R, 0:n], src).then_inc(landed[v % R], 16)

            def ffn(l, v0, blocks):
                with sp.Fori(0, blocks) as i:
                    for r in range(BLOCK):
                        src, n = block_unit(l, i, r)
                        sp.wait_ge(lo_ready, i * BLOCK + (v0 + r - R + 1))
                        slot = (v0 + r) % R
                        sp.dma_start(raw[:, slot, 0:n], src).then_inc(landed[slot], 16)

            for v, unit in enumerate(stream0):
                load(v, *source(unit))
            ffn(0, V_FFN[0], 2)
            for n, unit in enumerate(stream1):
                load(V_PROJ[1] + n, *source(unit))
            ffn(1, V_FFN[1], NE)
            for n in range(H):
                load(V_END + n, d["w_gu"][1][NE * 2 * FJ + n], UNIT)

            for k in range(KT):
                sp.wait_ge(out_ready, k + 1)
                sp.dma_start(out[:, k, :], outT[:, k, :]).then_inc(stored, 16)
            sp.wait_ge(stored, 16 * KT)

        def split_hi(act, v, cols, i=None):
            slot = v % R
            if i is None:
                act.wait_ge(landed[slot], 16 * (v // R + 1))
                if v >= H:
                    act.wait_ge(split_used, v - H + 1)
            else:
                act.wait_ge(landed[slot], i * (16 * BLOCK // R) + 16 * (v // R + 1))
                act.wait_ge(split_used, i * BLOCK + (v - H + 1))
            nc.scalar.activation(whi[:, v % H, 0:cols], raw[:, slot, 0:cols], ACT.Copy).then_inc(hi_ready, 1)

        def split_lo(dve, v, cols, i=None):
            dve.wait_ge(hi_ready, v + 1 if i is None else i * BLOCK + (v + 1))
            nc.vector.tensor_tensor(wlo[:, v % H, 0:cols], raw[:, v % R, 0:cols],
                                    whi[:, v % H, 0:cols].bitcast(F32), ALU.subtract).then_inc(lo_ready, 1)

        def x_ready(eng, n, k):
            if n == 0:
                if k == 0:
                    eng.wait_ge(x_in, 16)
            elif n in (1, 3):
                eng.wait_ge(x_mixed[n // 2], k + 1)
            elif n == 2:
                eng.wait_ge(down_out[0], 1 + KT + k + 1)
            else:
                eng.wait_ge(x_last, k + 1)

        def MOD_BANK(g):
            g_gla = MODT // 4 - 1
            return 6 if g < g_gla else 5 if g < g_gla + GLA_MODS // 4 else 2

        def first_col(n):
            return CTX if n >= 3 else 0

        def q_col(l):
            return CTX if l else 0

        def att_tiles(l):
            return [2, 3] if l else [2, 3, 0, 1]

        def gla_tiles(dr):
            return [0, 1, 2, 3] if dr == 0 else [1, 0, 3, 2]

        def gla_chunks(dr):
            return [0, 1] if dr == 0 else [1, 0]

        def gla_reads(l):
            return range(2 if l else 0, NTT)

        @block.tensor
        def _(pe):
            def mod_unit(v):
                _kind, l, q = unit_of(v)
                g = l * MODT // 4 + q // 4
                if q % 4 == 0:
                    if g:
                        pe.wait_ge(modrow_out, g)
                    else:
                        pe.wait_ge(c_done, 1)
                if q % 4 == 1:
                    mod_turns(g)
                pe.wait_ge(lo_ready, v + 1)
                for kk in range(2):
                    k = 2 * (q % 4) + kk
                    for w in (whi, wlo):
                        mm = nc.tensor.matmul(ps[0:4, 7, :], c_split[:, k, :], w[:, v % H, kk * 512:(kk + 1) * 512],
                                              start=(k == 0 and w is whi), stop=(k == KT - 1 and w is wlo))
                mm.then_inc(split_used, 1)

            turned = [0]

            def mod_turns(n):
                for g in range(turned[0], n):
                    pe.wait_ge(modrow_out, g + 1)
                    if g:
                        pe.wait_ge(mod_out, g)
                    else:
                        pe.wait_ge(rs_ready, 1)
                    for m in range(4):
                        mm = nc.tensor.transpose(ps[:, MOD_BANK(g), 4 * m:4 * m + 4],
                                                 modrow[0:4, g % 2, m * P:(m + 1) * P], ident[0:4, 0:4])
                    mm.then_inc(modT_done, 1)
                turned[0] = n

            def three(outp, whs, wls, xh, xl, first, last):
                nc.tensor.matmul(outp, whs, xh, start=first, stop=False)
                nc.tensor.matmul(outp, whs, xl, start=False, stop=False)
                return nc.tensor.matmul(outp, wls, xh, start=False, stop=last)

            def fm_tile(v, outp, xh, xl, nk, norm=None):
                s = v % H
                for k in range(nk):
                    if norm is not None:
                        pe.wait_ge(hlo_done, KT * norm + k + 1)
                    mm = three(outp, whi[:, s, k * P:(k + 1) * P], wlo[:, s, k * P:(k + 1) * P],
                               xh(k), xl(k), k == 0, k == nk - 1)
                return mm

            def norm_sum(n, k):
                pe.wait_ge(sq_ready, KT * n + k + 1)
                nc.tensor.matmul(ps[:, 6, first_col(n):T], ones[:, :], sq[:, k % 2, first_col(n):T],
                                 start=(k == 0), stop=(k == KT - 1)).then_inc(sumsq_done, 1)

            def projection(l):
                def fm(v, f):
                    c0 = q_col(l) if f not in (LA, LK, LK + 1, AK) else 0
                    pe.wait_ge(lo_ready, v + 1)
                    if f >= 2:
                        pe.wait_ge(fm_out[l], f - 1)
                    fm_tile(v, ps[:, f % 2, c0:T], lambda k: hhi[:, k, c0:T], lambda k: hlo[:, k, c0:T],
                            KT, norm=2 * l if f == LA else None).then_inc(split_used, 1)

                def tm(v, i, n, t0):
                    pe.wait_ge(lo_ready, v + 1)
                    s = v % H
                    for kk in range(2):
                        k = 2 * i + kk
                        for t in range(t0, NTT):
                            o = ps[:, 2 + t, 0:n]
                            wh, wl = whi[:, s, kk * n:(kk + 1) * n], wlo[:, s, kk * n:(kk + 1) * n]
                            hh, hl = hhi[:, k, t * P:(t + 1) * P], hlo[:, k, t * P:(t + 1) * P]
                            nc.tensor.matmul(o, hh, wh, start=(k == 0), stop=False)
                            nc.tensor.matmul(o, hh, wl, start=False, stop=False)
                            mm = nc.tensor.matmul(o, hl, wh, start=False, stop=(k == KT - 1))
                    mm.then_inc(split_used, 1)

                for n, (kind, _l, m) in enumerate(PROJ_STAGE[l]):
                    v = V_PROJ[l] + n
                    if kind == "fm":
                        fm(v, m)
                    elif kind == "tv":
                        tm(v, m, 384, 0)
                    elif kind == "tg":
                        if m == 0:
                            pe.wait_ge(v_out[l], NTT)
                        tm(v, m, 512, 2 if l else 0)
                    else:
                        mod_unit(v)

            def gla(l):
                reads = list(gla_reads(l))
                n_u = n_at = n_o = 0
                for dr in range(2):
                    if dr == 0:
                        pe.wait_ge(fm_out[l], 14)
                        pe.wait_ge(cx_out[l], 2)
                        pe.wait_ge(v_out[l], NTT)
                        pe.wait_ge(g_out[l], len(reads))
                    else:
                        pe.wait_ge(o_out[l], len(reads))
                    for p in range(GT):
                        nc.tensor.matmul(ps[:, 2 * dr + p, :], w2[32 * dr:32 * dr + 32, l, p * P:(p + 1) * P],
                                         la[32 * dr:32 * dr + 32, :], start=True, stop=True
                                         ).then_inc(z_done[l], 1)
                    if dr and l == 0:
                        pe.wait_ge(mod_out, MODT // 4 + GLA_MODS // 8 - 1)
                    pe.wait_ge(e_used[l], 4 * dr + 4)
                    if dr:
                        pe.wait_ge(st_ready[l], 2 * NTT)
                    for p in range(GT):
                        for t in range(NTT):
                            mm = nc.tensor.transpose(ps[:, 4 + p, t * P:(t + 1) * P], gk[:, p, t * P:(t + 1) * P],
                                                     ident[:, :])
                        mm.then_inc(kt_done[l], 1)
                    pe.wait_ge(kt_out[l], GT * (dr + 1))
                    if dr == 0:
                        pe.wait_ge(zeroed[l], 1)
                        if l == 0:
                            pe.wait_ge(mod_out, MODT // 4 - 1)
                    for step, t in enumerate(gla_tiles(dr)):
                        if n_u >= 2:
                            pe.wait_ge(st_ready[l], 2 * (n_u - 1))
                        for c in range(2):
                            for h in range(4):
                                p, hh = h // 2, h % 2
                                mm = nc.tensor.matmul(
                                    ps[CH * hh:CH * hh + CH, (6, 4)[n_u % 2], (2 * c + p) * CH:(2 * c + p + 1) * CH],
                                    gkt[:, t, c, h * CH:(h + 1) * CH], vt[:, t, P + h * CH:P + (h + 1) * CH],
                                    start=True, stop=True)
                        mm.then_inc(u_done[l], 1)
                        n_u += 1
                        if t not in reads:
                            continue
                        if n_at >= 2:
                            pe.wait_ge(am_ready[l], n_at - 1)
                        for p in range(GT):
                            mm = nc.tensor.matmul(ps[:, n_at % 2, 2 * p * P:2 * (p + 1) * P],
                                                  gkp[:, p, t * P:(t + 1) * P], gqp[:, :, p, t * P:(t + 1) * P],
                                                  start=True, stop=True)
                        mm.then_inc(at_done[l], 1)
                        n_at += 1
                        if l == 0:
                            for n in range(2):
                                mod_unit(V_GLA0 + 2 * (n_u - 1) + n)
                        pe.wait_ge(am_ready[l], n_at)
                        pe.wait_ge(st_ready[l], 8 * dr + 2 * step + 1)
                        if n_o >= 2:
                            pe.wait_ge(o_out[l], n_o - 1)
                        bank = 2 + n_o % 2
                        for h in range(4):
                            pv0 = P + h // 2 * P
                            nc.tensor.matmul(ps[:, bank, h * P:(h + 1) * P], am[:, dr, h * P:(h + 1) * P],
                                             vt[:, t, pv0:pv0 + P], start=(h == 0), stop=False,
                                             skip_group_check=True)
                        for ci, c in enumerate(gla_chunks(dr)):
                            for h in range(4):
                                p, hh = h // 2, h % 2
                                o0 = h * P + hh * CH
                                mm = nc.tensor.matmul(
                                    ps[CH * c:CH * c + CH, bank, o0:o0 + CH],
                                    gqb[:, hh, p, t * P + CH * c:t * P + CH * c + CH],
                                    state[:, dr, 2 * step + ci, p * CH:(p + 1) * CH],
                                    start=False, stop=(ci == 1), skip_group_check=True)
                        mm.then_inc(o_done[l], 1)
                        n_o += 1
                pe.wait_ge(y_ready[l], 1)
                if l == 0:
                    pe.wait_ge(mod_out, MODT // 4 + GLA_MODS // 4 - 1)
                pe.wait_ge(st_ready[l], 4 * NTT)
                for f in range(GT):
                    for n, t in enumerate(reads):
                        mm = nc.tensor.transpose(ps[:, 4 + f, t * P:(t + 1) * P],
                                                 gb[:, n // 2, (n % 2) * 256 + f * P:(n % 2) * 256 + (f + 1) * P],
                                                 ident[:, :])
                    mm.then_inc(yT_done[l], 1)

            def attention(l):
                tiles = att_tiles(l)
                for j in range(AT + 1):
                    src = aq[:, j, CTX:T] if j < AT else ak[:, CTX:T]
                    mm = nc.tensor.matmul(ps[:, j // 2, (j % 2) * LAT:(j % 2) * LAT + LAT], rot[:, :], src,
                                          start=True, stop=True)
                mm.then_inc(rot_done[l], 1)
                n_items = len(tiles) * HEADS
                pe.wait_ge(akz_ready[l], 1)
                pe.wait_ge(zeroed[l], 2)
                pe.wait_ge(mixlo[l], GT)

                def keys(i):
                    return 4 if tiles[i // HEADS] >= 2 else 2

                def scores(i):
                    t, h = tiles[i // HEADS], i % HEADS
                    if i >= 2:
                        pe.wait_ge(p_ready[l], i - 1)
                    nc.tensor.matmul(ps[:, i % 2, 0:keys(i) * P], aq[:, h // 2, t * P:(t + 1) * P],
                                     akz[:, h % 2, 0:keys(i) * P], start=True, stop=True).then_inc(s_done[l], 1)

                def turn(i):
                    pe.wait_ge(pn_ready[l], i + 1)
                    if i >= 2:
                        pe.wait_ge(pT_out[l], i - 1)
                    for k in range(keys(i)):
                        mm = nc.tensor.transpose(ps[:, 3 + i % 2, k * P:(k + 1) * P],
                                                 prob[:, i % 3, k * P:(k + 1) * P], ident[:, :])
                    mm.then_inc(pT_done[l], 1)

                def pv(i):
                    n, h = i // HEADS, i % HEADS
                    pe.wait_ge(pT_out[l], i + 1)
                    if h == 0 and n >= 2:
                        pe.wait_ge(alo_ready[l], n - 1)
                    kv = CH * (h % 2)
                    for k in range(keys(i)):
                        mm = nc.tensor.matmul(ps[kv:kv + HD, 5 + n % 2, h // 2 * P:(h // 2 + 1) * P],
                                              vt[:, k, kv:kv + HD], probT[:, i % 2, k * P:(k + 1) * P],
                                              start=(k == 0), stop=(k == keys(i) - 1))
                    mm.then_inc(pv_done[l], 1)

                for i in range(n_items + 3):
                    if i < n_items:
                        scores(i)
                        if l == 0:
                            mod_unit(V_ATT0 + i)
                    if 2 <= i < n_items + 2:
                        turn(i - 2)
                    if i >= 3:
                        pv(i - 3)
                if l == 0:
                    mod_turns(2 * MODT // 4)

            def out_projection(l):
                v0 = V_OUT[l]
                c0 = q_col(l)
                n_att = len(att_tiles(l))
                pe.wait_ge(mixlo[l], 4)
                pe.wait_ge(alo_ready[l], n_att)
                for m in range(KT):
                    v = v0 + m
                    pe.wait_ge(lo_ready, v + 1)
                    if m >= 2:
                        pe.wait_ge(x_mixed[l], m - 1)
                    fm_tile(v, ps[:, m % 2, c0:T], lambda k: hhi[:, k, c0:T], lambda k: hlo[:, k, c0:T],
                            KT).then_inc(split_used, 1)
                    if m:
                        norm_sum(2 * l + 1, m - 1)
                norm_sum(2 * l + 1, KT - 1)

            def ffn(l, v0, blocks):
                c0 = q_col(l)
                pe.wait_ge(hlo_done, KT * (2 * l + 1) + KT)
                with pe.Fori(0, blocks) as i:
                    for j in range(FJ):
                        for part in range(2):
                            r = 2 * j + part
                            v = v0 + r
                            pe.wait_ge(lo_ready, i * BLOCK + (v + 1))
                            if part == 0 and j >= 2:
                                pe.wait_ge(fh_ready[l], i * FJ + (j - 1))
                            fm_tile(v, ps[:, 2 * part + j % 2, c0:T], lambda k: hhi[:, k, c0:T],
                                    lambda k: hlo[:, k, c0:T], KT).then_inc(split_used, 1)
                    pe.wait_ge(flo_ready[l], i * FJ + FJ)
                    for m in range(KT):
                        v = v0 + 2 * FJ + m
                        pe.wait_ge(lo_ready, i * BLOCK + (v + 1))
                        if m == 0:
                            pe.wait_ge(down_out[l], i * KT + 1)
                        if m >= 2:
                            pe.wait_ge(down_out[l], i * KT + m)
                        fm_tile(v, ps[:, 4 + m % 2, c0:T], lambda k: fhi[:, k, c0:T], lambda k: flo[:, k, c0:T],
                                FJ).then_inc(split_used, 1)

            pe.wait_ge(init_done, 1)
            pe.wait_ge(const_in, 16 * N_CONST)
            for k in range(KT):
                norm_sum(0, k)
            for v in range(len(START)):
                mod_unit(v)
            mod_turns(M0 // 4)
            projection(0)
            gla(0)
            attention(0)
            out_projection(0)
            ffn(0, V_FFN[0], 2)
            for k in range(KT):
                norm_sum(2, k)
            projection(1)
            gla(1)
            attention(1)
            out_projection(1)
            pe.wait_ge(hlo_done, KT * 3 + KT)
            for t in range(2):
                for k in range(KT):
                    for part in (hhi, hlo):
                        mm = nc.tensor.matmul(ps[:, 7, t * NE:(t + 1) * NE],
                                              part[:, k, CTX + t * P:CTX + (t + 1) * P].bitcast(F32),
                                              router[:, k, :], start=(k == 0 and part is hhi),
                                              stop=(k == KT - 1 and part is hlo))
            mm.then_inc(lg_done, 1)
            for e in range(NE):
                pe.wait_ge(diag_ready, 2 * e + 2)
                if e >= 2:
                    pe.wait_ge(cb_out, e - 1)
                nc.tensor.matmul(ps[:, 4 + e % 2, 0:LAT], ones[:, :], diag[:, e % 2, :, :], start=True,
                                 stop=True).then_inc(cb_done, 1)
            ffn(1, V_FFN[1], NE)
            for k in range(KT):
                norm_sum(4, k)

        @block.scalar
        def _(act):
            done = [0]

            def then(ins):
                done[0] += 1
                ins.then_inc(act_order, 1)
                act.wait_ge(act_order, done[0])

            for name, dst in CONSTS(locals_=dict(
                    ident=ident, rot=rot, cos=cos, sin=sin, amask=amask, gmask=gmask, reset=reset, iota=iota,
                    b_mod=b_mod, norm_g=norm_g, final_g=final_g, sink=sink, w2=w2, gla_b=gla_b, gla_g=gla_g,
                    conv_w=conv_w, router=router)):
                act.dma_start(dst[:], d[name]).then_inc(const_in, 16)

            def hi(v):
                split_hi(act, v, cols_of(v))

            def mod_rows(v):
                _kind, l, q = unit_of(v)
                if q % 4 == 3:
                    g = l * MODT // 4 + q // 4
                    act.wait_ge(split_used, v + 1)
                    if g >= 2:
                        act.wait_ge(modT_done, g - 1)
                    nc.scalar.activation(modrow[:, g % 2, :], ps[0:4, 7, :], ACT.Copy).then_inc(modrow_out, 1)

            def norm_squares(n, k):
                x_ready(act, n, k)
                if k >= 2:
                    act.wait_ge(sumsq_done, KT * n + k - 1)
                c0 = first_col(n)
                nc.scalar.activation(sq[:, k % 2, c0:T], xT[:, k, c0:T], ACT.Square).then_inc(sq_ready, 1)

            def norm_scale(n):
                act.wait_ge(sumsq_done, KT * n + KT)
                c0 = first_col(n)
                then(nc.scalar.activation(rs[:, c0:T], ps[:, 6, c0:T], ACT.Ln, bias=epsc[:, 0:1], scale=1.0 / D))
                nc.scalar.activation(rs[:, c0:T], rs[:, c0:T], ACT.Exp, scale=-0.5).then_inc(rs_ready, 1)

            def norm_hi(n):
                c0 = first_col(n)
                for k in range(KT):
                    act.wait_ge(hf_ready, KT * n + k + 1)
                    nc.scalar.activation(hhi[:, k, c0:T], hf[:, k % 2, c0:T], ACT.Copy).then_inc(hhi_done, 1)

            def projection(l):
                c0 = q_col(l)
                for n, (kind, _l, f) in enumerate(PROJ_STAGE[l]):
                    v = V_PROJ[l] + n
                    if kind == "fm" and f < SX:
                        act.wait_ge(split_used, v + 1)
                        src = ps[:, f % 2, :]
                        if f == LA:
                            dst, src = la[:, :], src[0:CH, :]
                        elif f < LQ:
                            dst = lk[:, f - LK, :]
                        elif f < AK:
                            dst, src = lq[:, f - LQ, c0:T], src[:, c0:T]
                        elif f == AK:
                            dst = ak[:, :]
                        elif f < SB:
                            dst, src = aq[:, f - AQ, c0:T], src[:, c0:T]
                        elif f < SC:
                            dst, src = s_b[:, f - SB, c0:T], src[:, c0:T]
                        else:
                            dst, src = s_c[:, f - SC, c0:T], src[:, c0:T]
                        nc.scalar.activation(dst, src, ACT.Copy).then_inc(fm_out[l], 1)
                    if kind == "tg" and f == 3:
                        act.wait_ge(split_used, v + 1)
                        for t in gla_reads(l):
                            nc.scalar.activation(gate[:, t, :], ps[:, 2 + t, :], ACT.Silu).then_inc(g_out[l], 1)
                    if kind == "mod":
                        mod_rows(v)
                    hi(v + H)

            def gla(l):
                reads = list(gla_reads(l))
                n_o = 0
                for dr in range(2):
                    if dr:
                        act.wait_ge(e_used[l], 4)
                        act.wait_ge(kt_done[l], GT)
                    for p in range(GT):
                        act.wait_ge(z_done[l], 2 * dr + p + 1)
                        nc.scalar.activation(gt1[:, p, :], ps[:, 2 * dr + p, :], ACT.Abs,
                                             bias=gla_b[:, l, dr, p:p + 1]).then_inc(abs_done[l], 1)
                    act.wait_ge(abs_done[l], GT * (dr + 1))
                    then(nc.scalar.activation(gt1[:, :, :], gt1[:, :, :], ACT.Exp, scale=-1.0))
                    nc.scalar.activation(gt1[:, :, :], gt1[:, :, :], ACT.Ln, bias=1.0).then_inc(sp_ready[l], 1)
                    act.wait_ge(d_ready[l], 2 * dr + 1)
                    nc.scalar.activation(gt1[:, :, :], gt2[:, :, :], ACT.Exp, scale=1.0 / TAU
                                         ).then_inc(e_ready[l], 1)
                    nc.scalar.activation(gk[:, :, :], gt2[:, :, :], ACT.Exp, scale=-1.0 / TAU
                                         ).then_inc(e_ready[l], 1)
                    act.wait_ge(e_used[l], 4 * dr + 1)
                    nc.scalar.activation(gt1[:, :, :], gb[:, :, :], ACT.Exp, scale=1.0 / TAU
                                         ).then_inc(e_ready[l], 1)
                    last = 0 if dr else CH - 1
                    nc.scalar.activation(decay[:, dr, :],
                                         gb[:, :, :].rearrange("p g (c n) -> p (g c) n", n=CH)[:, :, last],
                                         ACT.Exp, scale=1.0 / TAU).then_inc(dec_ready[l], 1)
                    act.wait_ge(d_ready[l], 2 * dr + 2)
                    act.wait_ge(e_used[l], 4 * dr + 2)
                    nc.scalar.activation(gk[:, :, :], gt2[:, :, :], ACT.Exp, scale=1.0 / TAU
                                         ).then_inc(e_ready[l], 1)
                    for p in range(GT):
                        act.wait_ge(kt_done[l], 2 * dr + p + 1)
                        if dr and p == 0:
                            act.wait_ge(u_done[l], NTT)
                        for c in range(2):
                            rows = slice(c * CH, (c + 1) * CH)
                            ins = nc.scalar.activation(gkt[rows, :, c, p * P:(p + 1) * P],
                                                       ps[rows, 4 + p, :].rearrange("p (t n) -> p t n", t=NTT),
                                                       ACT.Copy)
                        ins.then_inc(kt_out[l], 1)
                    for step, t in enumerate(gla_tiles(dr)):
                        if l == 0:
                            for n in range(2):
                                v = V_GLA0 + 2 * (NTT * dr + step) + n
                                mod_rows(v)
                                hi(v + H)
                        if t in reads:
                            act.wait_ge(o_done[l], n_o + 1)
                            nc.scalar.activation(
                                go[:, t, 256 * dr:256 * dr + 256].rearrange("p (g b n) -> p g b n", b=2, n=CH),
                                ps[:, 2 + n_o % 2, :].rearrange("p (g b n) -> p g b n", g=2, n=CH)[:, :, ::3, :],
                                ACT.Copy).then_inc(o_out[l], 1)
                            n_o += 1
                act.wait_ge(ss_ready[l], 1)
                n8 = 8 * len(reads)
                then(nc.scalar.activation(gss[:, 0:n8], gss[:, 0:n8], ACT.Ln, bias=epsc[:, 0:1], scale=1.0 / CH))
                nc.scalar.activation(gss[:, 0:n8], gss[:, 0:n8], ACT.Exp, scale=-0.5).then_inc(grs_ready[l], 1)
                c0 = q_col(l)
                act.wait_ge(yT_done[l], GT)
                for f in range(GT):
                    nc.scalar.activation(hhi[:, AT + f, c0:T], ps[:, 4 + f, c0:T], ACT.Copy,
                                         scale=gla_g[:, l:l + 1]).then_inc(mixhi[l], 1)
                act.wait_ge(conv_out[l], 1)
                for f in range(2):
                    nc.scalar.activation(hhi[:, AT + GT + f, c0:T], s_b[:, f, c0:T], ACT.Copy
                                         ).then_inc(mixhi[l], 1)

            def attention(l):
                tiles = att_tiles(l)
                n_items = len(tiles) * HEADS

                def keys(i):
                    return 4 if tiles[i // HEADS] >= 2 else 2

                def tail(n):
                    act.wait_ge(pv_done[l], HEADS * (n + 1))
                    t = tiles[n]
                    nc.scalar.activation(hhi[:, 0:AT, t * P:(t + 1) * P],
                                         ps[:, 5 + n % 2, :].rearrange("p (j n) -> p j n", j=AT), ACT.Copy
                                         ).then_inc(ahi_ready[l], 1)

                for i in range(n_items + 4):
                    if i >= 11 and i % 8 == 3:
                        tail((i - 11) // 8)
                    if i < n_items:
                        act.wait_ge(negm_ready[l], i + 1)
                        if i >= 3:
                            act.wait_ge(pT_done[l], i - 2)
                        nc.scalar.activation(prob[:, i % 3, 0:keys(i) * P], ps[:, i % 2, 0:keys(i) * P], ACT.Exp,
                                             bias=negm[:, i:i + 1], scale=HD ** -0.5,
                                             accum_out=psumrow[:, i:i + 1]).then_inc(p_ready[l], 1)
                        h = i % HEADS
                        nc.scalar.activation(esink[:, i:i + 1], sink[:, l, h:h + 1], ACT.Exp,
                                             bias=negm[:, i:i + 1]).then_inc(esk_ready[l], 1)
                    if 2 <= i < n_items + 2:
                        j = i - 2
                        act.wait_ge(pT_done[l], j + 1)
                        if j >= 2:
                            act.wait_ge(pv_done[l], j - 1)
                        nc.scalar.activation(probT[:, j % 2, 0:keys(j) * P], ps[:, 3 + j % 2, 0:keys(j) * P],
                                             ACT.Copy).then_inc(pT_out[l], 1)
                    if l == 0 and i < n_items:
                        mod_rows(V_ATT0 + i)
                        hi(V_ATT0 + i + H)

            def out_projection(l):
                v0 = V_OUT[l]
                for m in range(KT):
                    if m:
                        norm_squares(2 * l + 1, m - 1)
                    hi(v0 + m + H)
                norm_squares(2 * l + 1, KT - 1)
                norm_scale(2 * l + 1)
                norm_hi(2 * l + 1)

            def ffn(l, v0, blocks):
                c0 = q_col(l)
                with act.Fori(0, blocks) as i:
                    for r in range(BLOCK):
                        j = r // 2
                        if r < 2 * FJ and r % 2 == 0:
                            act.wait_ge(split_used, i * BLOCK + (v0 + r + 1))
                            if j >= 2:
                                act.wait_ge(fh_ready[l], i * FJ + (j - 1))
                            nc.scalar.activation(sg[:, j % 2, c0:T], ps[:, j % 2, c0:T], ACT.Silu
                                                 ).then_inc(sg_ready[l], 1)
                        if r < 2 * FJ and r % 2 == 1:
                            act.wait_ge(fh_ready[l], i * FJ + (j + 1))
                            nc.scalar.activation(fhi[:, j, c0:T], hf[:, j % 2, c0:T], ACT.Copy
                                                 ).then_inc(fhi_ready[l], 1)
                        b = v0 + r + H
                        cols = DUNIT if 2 * FJ <= r + H < BLOCK else UNIT
                        split_hi(act, b, cols, i)

            act.dma_start(c_raw[:, :], d["c"]).then_inc(c_in, 16)
            act.dma_start(xT[:, :, :], d["x"]).then_inc(x_in, 16)
            act.wait_ge(c_in, 16)
            then(nc.scalar.activation(c_act[:, :, :], c_raw[:, :].rearrange("p (k j) -> p k j", j=2), ACT.Silu))
            nc.scalar.activation(c_split[:, :, 0:2], c_act[:, :, :], ACT.Copy).then_inc(c_hi, 1)
            for v in range(H):
                hi(v)
            act.wait_ge(init_done, 1)
            for k in range(KT):
                norm_squares(0, k)
            norm_scale(0)
            for v in range(len(START)):
                mod_rows(v)
                hi(v + H)
            norm_hi(0)
            projection(0)
            gla(0)
            attention(0)
            out_projection(0)
            ffn(0, V_FFN[0], 2)
            for k in range(KT):
                norm_squares(2, k)
            norm_scale(2)
            norm_hi(2)
            projection(1)
            gla(1)
            attention(1)
            out_projection(1)
            act.wait_ge(topd_ready, 1)
            nc.scalar.activation(gate2[:, :, 1:2], gate2[:, :, 0:1], ACT.Exp).then_inc(tope_ready, 1)
            for e in range(NE):
                act.wait_ge(cb_done, e + 1)
                nc.scalar.activation(cb[:, e, :], ps[:, 4 + e % 2, 0:LAT], ACT.Copy).then_inc(cb_out, 1)
            ffn(1, V_FFN[1], NE)
            for k in range(KT):
                norm_squares(4, k)
            norm_scale(4)

        @block.gpsimd
        def _(pool):
            def norm_lo(n):
                c0 = first_col(n)
                for k in range(KT):
                    pool.wait_ge(hhi_done, KT * n + k + 1)
                    nc.gpsimd.tensor_tensor(hlo[:, k, c0:T], hf[:, k % 2, c0:T], hhi[:, k, c0:T].bitcast(F32),
                                            ALU.subtract).then_inc(hlo_done, 1)

            def ffn(l, blocks):
                c0 = q_col(l)
                with pool.Fori(0, blocks) as i:
                    for j in range(FJ):
                        pool.wait_ge(fhi_ready[l], i * FJ + (j + 1))
                        nc.gpsimd.tensor_tensor(flo[:, j, c0:T], hf[:, j % 2, c0:T], fhi[:, j, c0:T].bitcast(F32),
                                                ALU.subtract).then_inc(flo_ready[l], 1)

            def zeros(l):
                pool.wait_ge(z_done[l], 1)
                for n in range(2):
                    rows = slice(CH * (1 - n), CH * (2 - n))
                    for buf in (gqp[rows, n, :, :], gqb[rows, n, :, :], gkt[rows, :, n, :]):
                        ins = nc.gpsimd.memset(buf, 0.0)
                ins.then_inc(zeroed[l], 1)
                pool.wait_ge(y_ready[l], 1)
                for n in range(2):
                    ins = nc.gpsimd.memset(akz[CH * (1 - n):CH * (2 - n), n, :], 0.0)
                ins.then_inc(zeroed[l], 1)

            norm_lo(0)
            zeros(0)
            norm_lo(1)
            ffn(0, 2)
            norm_lo(2)
            zeros(1)
            norm_lo(3)
            ffn(1, NE)

        @block.vector
        def _(dve):
            V = nc.vector
            done = [0]

            def then(ins):
                done[0] += 1
                ins.then_inc(dve_order, 1)
                dve.wait_ge(dve_order, done[0])

            def lo(v):
                split_lo(dve, v, cols_of(v))

            taken = [0]

            def mods_in(n):
                for g in range(taken[0], n):
                    l, m = g // (MODT // 4), g % (MODT // 4)
                    dve.wait_ge(modT_done, g + 1)
                    then(V.tensor_reduce(modsum[:, g % 2, :].rearrange("p (m j) -> p m j", j=2),
                                         ps[:, MOD_BANK(g), 0:16].rearrange("p (m s j) -> p m j s", s=2, j=2),
                                         AX.X, ALU.add))
                    V.tensor_tensor(mod[:, l, 8 * m:8 * m + 8], modsum[:, g % 2, :], b_mod[:, l, 8 * m:8 * m + 8],
                                    ALU.add).then_inc(mod_out, 1)
                taken[0] = max(taken[0], n)

            def mod_step(v):
                _kind, l, q = unit_of(v)
                if q % 4 == 1:
                    mods_in(l * MODT // 4 + q // 4)

            def make_gain(l, which):
                m0 = 2 * (KT + 3 * KT * which)
                then(V.scalar_tensor_tensor(gain[:, l, which, :], mod[:, l, m0:m0 + 2 * KT], 1.0,
                                            norm_g[:, l, which, :], ALU.add, ALU.mult))

            def kinds_of(c0):
                return [(0, 0, CTX), (1, CTX, T)] if c0 == 0 else [(1, CTX, T)]

            def norm_apply(n):
                c0 = first_col(n)
                l, which = n // 2, n % 2
                dve.wait_ge(rs_ready, n + 1)
                for k in range(KT):
                    then(V.tensor_tensor(xn[:, k % 2, c0:T], xT[:, k, c0:T], rs[:, c0:T], ALU.mult))
                    if k >= 2:
                        dve.wait_ge(hlo_done, KT * n + k - 1)
                    for kind, a, b in kinds_of(c0):
                        sh = 2 * (3 * KT * which + k) + kind
                        ins = V.tensor_scalar(hf[:, k % 2, a:b], xn[:, k % 2, a:b],
                                              gain[:, l, which, 2 * k + kind:2 * k + kind + 1],
                                              mod[:, l, sh:sh + 1], ALU.mult, ALU.add)
                        if kind == 1:
                            ins.then_inc(hf_ready, 1)

            def projection(l):
                c0 = q_col(l)
                for n, (kind, _l, f) in enumerate(PROJ_STAGE[l]):
                    v = V_PROJ[l] + n
                    if kind == "tv" and f == 3:
                        dve.wait_ge(split_used, v + 1)
                        for t in range(NTT):
                            V.tensor_copy(vt[:, t, :], ps[:, 2 + t, 0:384]).then_inc(v_out[l], 1)
                    if kind == "fm" and f >= SX:
                        g = f - SX
                        dve.wait_ge(split_used, v + 1)
                        dve.wait_ge(fm_out[l], SC + g + 1)
                        if g == 0:
                            then(V.memset(cx[:, :, :, :], 0.0))
                        s0 = c0 // CTX
                        V.tensor_tensor(cx[:, g, s0:2, 1:LAT + 1],
                                        ps[:, f % 2, c0:T].rearrange("p (s n) -> p s n", n=LAT),
                                        s_c[:, g, c0:T].rearrange("p (s n) -> p s n", n=LAT),
                                        ALU.mult).then_inc(cx_out[l], 1)
                    lo(v + H)
                    if kind == "mod":
                        mod_step(v)

            def conv(l):
                c0 = q_col(l)
                s0 = c0 // CTX
                dve.wait_ge(cx_out[l], 2)
                for g in range(2):
                    y = s_c[:, g, c0:T].rearrange("p (s n) -> p s n", n=LAT)
                    then(V.tensor_scalar(y, cx[:, g, s0:2, 1:LAT + 1], conv_w[:, l, 1, g:g + 1], None, ALU.mult))
                    then(V.scalar_tensor_tensor(y, cx[:, g, s0:2, 0:LAT], conv_w[:, l, 0, g:g + 1], y,
                                                ALU.mult, ALU.add))
                    then(V.scalar_tensor_tensor(y, cx[:, g, s0:2, 2:LAT + 2], conv_w[:, l, 2, g:g + 1], y,
                                                ALU.mult, ALU.add))
                    ins = V.tensor_tensor(s_b[:, g, c0:T], s_c[:, g, c0:T], s_b[:, g, c0:T], ALU.mult)
                    if g == 0:
                        then(ins)
                ins.then_inc(conv_out[l], 1)

            def gla(l):
                reads = list(gla_reads(l))
                c0 = q_col(l)
                n_at = 0

                def chunks(x):
                    return x[:, :, :].rearrange("p g (c n) -> p (g c) n", n=CH)

                then(V.memset(am[:, :, :], 0.0))
                then(V.memset(state[:, :, 0, :], 0.0))
                for dr in range(2):
                    for p in range(GT):
                        dve.wait_ge(abs_done[l], 2 * dr + p + 1)
                        if dr and p == 0:
                            dve.wait_ge(e_ready[l], 4)
                        then(V.tensor_scalar(gt2[:, p, :], ps[:, 2 * dr + p, :], gla_b[:, l, dr, p:p + 1], 0.0,
                                             ALU.add, ALU.min))
                    dve.wait_ge(sp_ready[l], dr + 1)
                    then(V.tensor_tensor(gt2[:, :, :], gt2[:, :, :], gt1[:, :, :], ALU.subtract))
                    if dr:
                        dve.wait_ge(dec_ready[l], 1)
                    for p in range(GT):
                        if dr == 0:
                            o, m, x = gb[:, p, :], reset[:, :], gt2[:, p, :]
                        else:
                            o, m, x = gb[:, p, ::-1], reset[:, :], gt2[:, p, ::-1]
                        then(V.tensor_tensor_scan(o, m, x, 0.0, ALU.mult, ALU.add))
                    ref = CH // 2 if dr == 0 else CH - 1 - CH // 2
                    last = 0 if dr else CH - 1
                    V.tensor_tensor(chunks(gt2), chunks(gb),
                                    chunks(gb)[:, :, ref:ref + 1].broadcast_to([P, GT * NCH, CH]), ALU.subtract
                                    ).then_inc(d_ready[l], 1)
                    dve.wait_ge(e_ready[l], 4 * dr + 1)
                    if dr:
                        dve.wait_ge(o_done[l], len(reads))
                    for n in range(2):
                        rows = slice(CH * n, CH * (n + 1))
                        ins = V.scalar_tensor_tensor(gqp[rows, n, :, c0:T], gt1[rows, :, c0:T], HD ** -0.5,
                                                     lq[rows, :, c0:T], ALU.mult, ALU.mult)
                    ins.then_inc(e_used[l], 1)
                    dve.wait_ge(e_ready[l], 4 * dr + 2)
                    V.tensor_tensor(gkp[:, :, :], gk[:, :, :], lk[:, :, :], ALU.mult).then_inc(e_used[l], 1)
                    V.tensor_tensor(chunks(gt2), chunks(gb)[:, :, last:last + 1].broadcast_to([P, GT * NCH, CH]),
                                    chunks(gb), ALU.subtract).then_inc(d_ready[l], 1)
                    dve.wait_ge(e_ready[l], 4 * dr + 3)
                    for n in range(2):
                        rows = slice(CH * n, CH * (n + 1))
                        ins = V.scalar_tensor_tensor(gqb[rows, n, :, c0:T], gt1[rows, :, c0:T], HD ** -0.5,
                                                     lq[rows, :, c0:T], ALU.mult, ALU.mult)
                    ins.then_inc(e_used[l], 1)
                    dve.wait_ge(e_ready[l], 4 * dr + 4)
                    V.tensor_tensor(gk[:, :, :], gk[:, :, :], lk[:, :, :], ALU.mult).then_inc(e_used[l], 1)
                    dve.wait_ge(dec_ready[l], dr + 1)
                    for step, t in enumerate(gla_tiles(dr)):
                        n_u = NTT * dr + step
                        if t in reads:
                            dve.wait_ge(at_done[l], n_at + 1)
                            if n_at:
                                dve.wait_ge(o_done[l], n_at)
                            V.copy_predicated(am[:, dr, :].rearrange("p (h n) -> p h n", n=P),
                                              gmask[:, dr:dr + 1, :].broadcast_to([P, 4, P]),
                                              ps[:, n_at % 2, :].rearrange("p (h n) -> p h n", n=P)
                                              ).then_inc(am_ready[l], 1)
                            n_at += 1
                        dve.wait_ge(u_done[l], n_u + 1)
                        for ci, c in enumerate(gla_chunks(dr)):
                            for p in range(GT):
                                col = p * NCH + 2 * t + c
                                ins = V.scalar_tensor_tensor(
                                    state[:, dr, 2 * step + ci + 1, p * CH:(p + 1) * CH],
                                    state[:, dr, 2 * step + ci, p * CH:(p + 1) * CH],
                                    decay[:, dr, col:col + 1],
                                    ps[:, (6, 4)[n_u % 2], (2 * c + p) * CH:(2 * c + p + 1) * CH],
                                    ALU.mult, ALU.add)
                            ins.then_inc(st_ready[l], 1)
                            dve.wait_ge(st_ready[l], 2 * n_u + ci + 1)
                        if l == 0:
                            for n in range(2):
                                v = V_GLA0 + 2 * n_u + n
                                lo(v + H)
                                mod_step(v)
                n = len(reads)
                t0 = reads[0]
                o4 = go[:, t0:NTT, :]
                sqv = gtt[:, :, :, :].rearrange("p a g t -> p (a g t)")[:, 0:512 * n]
                dve.wait_ge(o_out[l], 2 * n)
                then(V.tensor_tensor(sqv.rearrange("p (t n) -> p t n", t=n), o4, o4, ALU.mult))
                V.tensor_reduce(gss[:, 0:8 * n], sqv.rearrange("p (h n) -> p h n", n=CH), AX.X, ALU.add
                                ).then_inc(ss_ready[l], 1)
                then(V.tensor_tensor(o4, o4, gate[:, t0:NTT, :], ALU.mult))
                dve.wait_ge(grs_ready[l], 1)
                oh = o4.rearrange("p t (h n) -> p (t h) n", n=CH)
                then(V.tensor_tensor(oh, oh, gss[:, 0:8 * n].rearrange("p (h o) -> p h o", o=1
                                                                       ).broadcast_to([P, 8 * n, CH]), ALU.mult))
                yv = gb[:, 0:n // 2, :].rearrange("p g (t n) -> p (g t) n", n=256)
                V.tensor_tensor(yv, o4[:, :, 0:256], o4[:, :, 256:512], ALU.add).then_inc(y_ready[l], 1)
                for f in range(GT):
                    dve.wait_ge(mixhi[l], f + 1)
                    V.scalar_tensor_tensor(hlo[:, AT + f, c0:T], ps[:, 4 + f, c0:T], gla_g[:, l:l + 1],
                                           hhi[:, AT + f, c0:T].bitcast(F32), ALU.mult, ALU.subtract
                                           ).then_inc(mixlo[l], 1)
                for f in range(2):
                    dve.wait_ge(mixhi[l], GT + f + 1)
                    V.tensor_tensor(hlo[:, AT + GT + f, c0:T], s_b[:, f, c0:T],
                                    hhi[:, AT + GT + f, c0:T].bitcast(F32), ALU.subtract).then_inc(mixlo[l], 1)

            def attention(l):
                tiles = att_tiles(l)
                n_items = len(tiles) * HEADS
                dve.wait_ge(y_ready[l], 1)
                dve.wait_ge(yT_done[l], GT)
                dve.wait_ge(rot_done[l], 1)
                r1 = rt1.rearrange("p (j n) -> p j n", j=AT)
                r2 = rt2.rearrange("p (j n) -> p j n", j=AT)
                V.tensor_tensor(r1, aq[:, :, CTX:T], cos[:, :].rearrange("p (o n) -> p o n", o=1
                                                                        ).broadcast_to([P, AT, LAT]), ALU.mult)
                then(V.tensor_tensor(r2, ps[:, 0:2, :].rearrange("p b (j n) -> p (b j) n", j=2),
                                     sin[:, :].rearrange("p (o n) -> p o n", o=1).broadcast_to([P, AT, LAT]),
                                     ALU.mult))
                then(V.tensor_tensor(aq[:, :, CTX:T], r1, r2, ALU.add))
                then(V.tensor_tensor(rt1[:, 0:LAT], ak[:, CTX:T], cos[:, :], ALU.mult))
                then(V.tensor_tensor(rt2[:, 0:LAT], ps[:, 2, 0:LAT], sin[:, :], ALU.mult))
                for kv in range(2):
                    rows = slice(kv * HD, (kv + 1) * HD)
                    V.tensor_tensor(akz[rows, kv, CTX:T], rt1[rows, 0:LAT], rt2[rows, 0:LAT], ALU.add)
                    ins = V.tensor_copy(akz[rows, kv, 0:CTX], ak[rows, 0:CTX])
                ins.then_inc(akz_ready[l], 1)

                def keys(i):
                    return 4 if tiles[i // HEADS] >= 2 else 2

                def tail(n):
                    dve.wait_ge(ahi_ready[l], n + 1)
                    t = tiles[n]
                    V.tensor_tensor(hlo[:, 0:AT, t * P:(t + 1) * P],
                                    ps[:, 5 + n % 2, :].rearrange("p (j n) -> p j n", j=AT),
                                    hhi[:, 0:AT, t * P:(t + 1) * P].bitcast(F32), ALU.subtract
                                    ).then_inc(alo_ready[l], 1)

                for i in range(n_items + 4):
                    if i >= 11 and i % 8 == 3:
                        tail((i - 11) // 8)
                    if i < n_items:
                        t, h = tiles[i // HEADS], i % HEADS
                        dve.wait_ge(s_done[l], i + 1)
                        if t >= 2:
                            blk = slice(3 * P, 4 * P) if t == 2 else slice(2 * P, 3 * P)
                            then(V.tensor_tensor(ps[:, i % 2, blk], ps[:, i % 2, blk], amask[:, t - 2, :], ALU.add))
                        then(V.tensor_reduce(mx[:, i:i + 1], ps[:, i % 2, 0:keys(i) * P], AX.X, ALU.max))
                        V.tensor_scalar(negm[:, i:i + 1], mx[:, i:i + 1], -(HD ** -0.5), negsink[:, l, h:h + 1],
                                        ALU.mult, ALU.min).then_inc(negm_ready[l], 1)
                    if 1 <= i <= n_items:
                        j = i - 1
                        dve.wait_ge(esk_ready[l], j + 1)
                        then(V.tensor_tensor(rden[:, j:j + 1], psumrow[:, j:j + 1], esink[:, j:j + 1], ALU.add))
                        then(V.reciprocal(rden[:, j:j + 1], rden[:, j:j + 1]))
                        V.tensor_scalar(prob[:, j % 3, 0:keys(j) * P], prob[:, j % 3, 0:keys(j) * P],
                                        rden[:, j:j + 1], None, ALU.mult).then_inc(pn_ready[l], 1)
                    if l == 0 and i < n_items:
                        lo(V_ATT0 + i + H)
                        mod_step(V_ATT0 + i)

            def out_projection(l):
                v0 = V_OUT[l]
                c0 = q_col(l)
                if l == 0:
                    mods_in(2 * MODT // 4)
                    dve.wait_ge(mod_out, 2 * MODT // 4)
                    make_gain(0, 1)
                    make_gain(1, 0)
                    make_gain(1, 1)
                for m in range(KT):
                    dve.wait_ge(split_used, v0 + m + 1)
                    for kind, a, b in kinds_of(c0):
                        g = 2 * (2 * KT + m) + kind
                        ins = V.scalar_tensor_tensor(xT[:, m, a:b], ps[:, m % 2, a:b], mod[:, l, g:g + 1],
                                                     xT[:, m, a:b], ALU.mult, ALU.add)
                        if kind == 1:
                            ins.then_inc(x_mixed[l], 1)
                    lo(v0 + m + H)
                norm_apply(2 * l + 1)

            def ffn(l, v0, blocks):
                c0 = q_col(l)
                dve.sem_inc(down_out[l], 1)
                with dve.Fori(0, blocks) as i:
                    for r in range(BLOCK):
                        if r < 2 * FJ and r % 2 == 1:
                            j = r // 2
                            dve.wait_ge(split_used, i * BLOCK + (v0 + r + 1))
                            dve.wait_ge(sg_ready[l], i * FJ + (j + 1))
                            if l == 0:
                                dve.wait_ge(flo_ready[l], i * FJ + (j - 1)) if j >= 2 else None
                                V.tensor_tensor(hf[:, j % 2, c0:T], ps[:, 2 + j % 2, c0:T], sg[:, j % 2, c0:T],
                                                ALU.mult).then_inc(fh_ready[l], 1)
                            else:
                                V.tensor_tensor(sg[:, j % 2, c0:T], ps[:, 2 + j % 2, c0:T], sg[:, j % 2, c0:T],
                                                ALU.mult).then_inc(swiglu_ready, 1)
                                dve.wait_ge(swiglu_ready, i * FJ + (j + 1))
                                dve.wait_ge(flo_ready[l], i * FJ + (j - 1)) if j >= 2 else None
                                V.tensor_tensor(hf[:, j % 2, c0:T], sg[:, j % 2, c0:T],
                                                cb[:, bass.ds(i, 1), :].rearrange("p a n -> p (a n)"),
                                                ALU.mult).then_inc(fh_ready[l], 1)
                        if r >= 2 * FJ:
                            m = r - 2 * FJ
                            dve.wait_ge(split_used, i * BLOCK + (v0 + r + 1))
                            if l == 0:
                                for kind, a, b in kinds_of(c0):
                                    g = 2 * (5 * KT + m) + kind
                                    ins = V.scalar_tensor_tensor(xT[:, m, a:b], ps[:, 4 + m % 2, a:b],
                                                                 mod[:, l, g:g + 1], xT[:, m, a:b],
                                                                 ALU.mult, ALU.add)
                            else:
                                ins = V.tensor_tensor(yacc[:, m, :], yacc[:, m, :], ps[:, 4 + m % 2, c0:T], ALU.add)
                            ins.then_inc(down_out[l], 1)
                        b = v0 + r + H
                        cols = DUNIT if 2 * FJ <= r + H < BLOCK else UNIT
                        split_lo(dve, b, cols, i)

            then(V.memset(ones[:, :], 1.0))
            V.memset(epsc[:, :], EPS).then_inc(init_done, 1)
            dve.wait_ge(const_in, 16 * N_CONST)
            then(V.tensor_scalar(negsink[:, :, :], sink[:, :, :], -1.0, None, ALU.mult))
            dve.wait_ge(c_hi, 1)
            V.tensor_tensor(c_split[:, :, 2:4], c_act[:, :, :], c_split[:, :, 0:2].bitcast(F32), ALU.subtract
                            ).then_inc(c_done, 1)
            for v in range(H):
                lo(v)
            for v in range(len(START)):
                lo(v + H)
                mod_step(v)
            mods_in(M0 // 4)
            dve.wait_ge(mod_out, M0 // 4)
            make_gain(0, 0)
            dve.wait_ge(x_in, 16)
            norm_apply(0)
            projection(0)
            conv(0)
            gla(0)
            attention(0)
            out_projection(0)
            ffn(0, V_FFN[0], 2)
            dve.wait_ge(down_out[0], 1 + 2 * KT)
            norm_apply(2)
            projection(1)
            conv(1)
            gla(1)
            attention(1)
            out_projection(1)
            then(V.memset(yacc[:, :, :], 0.0))
            dve.wait_ge(lg_done, 1)
            then(V.tensor_copy(logits[:, :, :], ps[:, 7, 0:2 * NE].rearrange("p (t e) -> p t e", t=2)))
            for t in range(2):
                then(V.max(top[:, t, :], logits[:, t, :]))
                then(V.max_index(topi[:, t, :], top[:, t, :], logits[:, t, :]))
            then(V.tensor_copy(topf[:, :, :], topi[:, :, :]))
            V.tensor_tensor(gate2[:, :, 0:1], top[:, :, 1:2], top[:, :, 0:1], ALU.subtract).then_inc(topd_ready, 1)
            dve.wait_ge(tope_ready, 1)
            then(V.tensor_scalar(gate2[:, :, 2:3], gate2[:, :, 1:2], 1.0, None, ALU.add))
            then(V.reciprocal(gate2[:, :, 2:3], gate2[:, :, 2:3]))
            then(V.tensor_tensor(gate2[:, :, 3:4], gate2[:, :, 1:2], gate2[:, :, 2:3], ALU.mult))
            for t in range(2):
                for w in range(2):
                    then(V.tensor_scalar(pick[:, t, w, :], iota[:, :], topf[:, t, w:w + 1],
                                         gate2[:, t, 2 + w:3 + w], ALU.is_equal, ALU.mult))
                then(V.tensor_tensor(pick[:, t, 0, :], pick[:, t, 0, :], pick[:, t, 1, :], ALU.add))
            for e in range(NE):
                if e >= 2:
                    dve.wait_ge(cb_done, e - 1)
                for t in range(2):
                    V.tensor_scalar(diag[:, e % 2, t, :], ident[:, :], pick[:, t, 0, e:e + 1], None,
                                    ALU.mult).then_inc(diag_ready, 1)
            dve.wait_ge(cb_out, NE)
            ffn(1, V_FFN[1], NE)
            for m in range(KT):
                if m == 0:
                    dve.wait_ge(down_out[1], 1 + NE * KT)
                g = 2 * (5 * KT + m) + 1
                V.scalar_tensor_tensor(xT[:, m, CTX:T], yacc[:, m, :], mod[:, 1, g:g + 1], xT[:, m, CTX:T],
                                       ALU.mult, ALU.add).then_inc(x_last, 1)
            dve.wait_ge(rs_ready, 4 + 1)
            for k in range(KT):
                then(V.tensor_tensor(xn[:, k % 2, CTX:T], xT[:, k, CTX:T], rs[:, CTX:T], ALU.mult))
                V.tensor_scalar(outT[:, k, :], xn[:, k % 2, CTX:T], final_g[:, k:k + 1], None,
                                ALU.mult).then_inc(out_ready, 1)



CONST_NAMES = ["ident", "rot", "cos", "sin", "amask", "gmask", "reset", "iota", "b_mod", "norm_g", "final_g",
               "sink", "w2", "gla_b", "gla_g", "conv_w", "router"]
N_CONST = len(CONST_NAMES)


def CONSTS(locals_):
    return [(n, locals_[n]) for n in CONST_NAMES]


def _constants():
    p = np.arange(P)
    f32 = np.float32
    rot = np.zeros((P, P), f32)
    for m in range(P):
        if m % HD < HD // 2:
            rot[m + HD // 2, m] = -1.0
        else:
            rot[m - HD // 2, m] = 1.0
    nf = HD // 4
    inv = (f32(10000.0) ** (-np.arange(nf, dtype=f32) / f32(nf))).astype(f32)
    tok = np.arange(LAT)
    ang = np.concatenate([(tok // 64).astype(f32)[:, None] * inv, (tok % 64).astype(f32)[:, None] * inv], 1)
    ang = ang[:, p % (HD // 2)].T
    q, k = p[:, None], p[None, :]
    amask = np.stack([np.where(k <= q, 0.0, -1e30), np.where(q <= k, 0.0, -1e30)], 1).astype(f32)
    s, t = p[:, None], p[None, :]
    same = s // CH == t // CH
    gmask = np.stack([same & (s <= t), same & (s >= t)], 1).astype(np.int32)
    reset = np.broadcast_to((np.arange(T) % CH != 0).astype(f32), (P, T))
    return dict(ident=np.eye(P, dtype=f32), rot=rot, cos=np.cos(ang), sin=np.sin(ang), amask=amask, gmask=gmask,
                reset=reset, iota=np.broadcast_to(np.arange(NE, dtype=f32), (P, NE)))


def _units(w, n):
    k, cols = w.shape
    return w.reshape(k // P, P, cols // n, n).transpose(2, 1, 0, 3).reshape(cols // n, P, k // P * n)


def _layout(a):
    f = {n: np.asarray(v) for n, v in a.items()}
    o = _constants()
    o["x"] = np.concatenate([f["ctx"][0], f["x"][0]], 0).T.reshape(KT, P, T).transpose(1, 0, 2)
    o["c"] = np.stack([f["c_ctx"], f["c"][0]], 1).reshape(KT, P, 2).transpose(1, 0, 2).reshape(P, 2 * KT)
    o["w_mod"] = (f["w_mod"].reshape(LAYERS, KT // 2, 2, P, MODT // 4, 512).transpose(0, 4, 1, 3, 2, 5)
                  .reshape(LAYERS, MODT, P, UNIT))

    def cols(v, tiles):
        return np.repeat(v.reshape(tiles, P).T[:, :, None], 2, 2).reshape(P, 2 * tiles)

    o["b_mod"] = np.stack([cols(f["b_mod"][l], MODT) for l in range(LAYERS)], 1)
    o["norm_g"] = np.stack([np.stack([cols(f[n][l], KT) for n in ("norm1_g", "norm2_g")], 1)
                            for l in range(LAYERS)], 1)
    o["final_g"] = f["final_norm_g"].reshape(KT, P).T
    pair = [h for j in range(AT) for h in (j, AT + j)]
    o["sink"] = np.broadcast_to(f["attn_sink"][:, pair], (P, LAYERS, HEADS))
    fm, tv, tg, wo, w2 = [], [], [], [], []
    for l in range(LAYERS):
        w = f["w_in"][l]
        z = np.zeros((D, 16), w.dtype)
        la = np.concatenate([w[:, 2048:2064], z, w[:, 2064:2080], z, np.zeros((D, 64), w.dtype)], 1)
        aq = w[:, 0:512].reshape(D, HEADS, HD)[:, pair].reshape(D, 512)
        fm.append(_units(np.concatenate([la, w[:, 1024:1280], w[:, 768:1024], w[:, 512:640], aq,
                                         w[:, 2080:2848]], 1), P))
        for dst, c in ((tv, np.r_[640:768, 1280:1536]), (tg, np.r_[1536:2048])):
            n = len(c)
            dst.append(w[:, c].reshape(KT // 2, 2, P, n).transpose(0, 2, 1, 3).reshape(KT // 2, P, 2 * n))
        wout = f["w_out"][l]
        wo.append(_units(np.concatenate([wout[0:512].reshape(HEADS, HD, D)[pair].reshape(512, D), wout[512:]], 0),
                         P))
        z = np.zeros((16, GT * P), w.dtype)
        w2.append(np.concatenate([f["gla_w2_f"][l], z, f["gla_w2_b"][l], z], 0))
    o["w_fm"], o["w_tv"], o["w_tg"], o["w_out"] = map(np.stack, (fm, tv, tg, wo))
    o["w2"] = np.stack(w2, 1)
    o["gla_b"] = np.stack([np.stack([f[n][l].reshape(GT, P).T for n in ("gla_b_f", "gla_b_b")], 1)
                           for l in range(LAYERS)], 1)
    o["gla_g"] = np.stack([np.tile(f["gla_norm_g"][l], 2) for l in range(LAYERS)], 1)
    o["conv_w"] = np.stack([f["conv_w"][l].reshape(3, 2, P).transpose(2, 0, 1) for l in range(LAYERS)], 1)
    o["router"] = f["router_w"][0].reshape(KT, P, NE).transpose(1, 0, 2)

    def gate_up(w):
        k, n = w.shape
        return _units(w, P).reshape(2, n // 2 // P, P, UNIT).transpose(1, 0, 2, 3).reshape(n // P, P, UNIT)

    o["w_gu0"] = gate_up(f["ffn_w_gu"][0])
    o["w_dn0"] = np.concatenate([_units(f["ffn_w_down"][0][b * DUNIT:(b + 1) * DUNIT], P) for b in range(2)], 0)
    gu = [gate_up(f["expert_w_gu"][0, e]) for e in range(NE)]
    o["w_gu1"] = np.concatenate(gu + [np.zeros((H, P, UNIT), gu[0].dtype)], 0)
    o["w_dn1"] = np.concatenate([_units(f["expert_w_down"][0, e], P) for e in range(NE)], 0)
    return o


def kernel(**inputs):
    import concourse.bacc as _bacc
    from concourse.bass_utils import run_bass_kernel_spmd as _run

    nc = _bacc.Bacc("TRN2", target_bir_lowering=False, num_devices=1)
    arrays, aps = {}, {}
    for name, a in _layout(inputs).items():
        a = np.ascontiguousarray(a)
        arrays[f"in_{name}"] = a
        aps[name] = nc.dram_tensor(f"in_{name}", a.shape, mybir.dt.from_np(a.dtype), kind="ExternalInput").ap()
    aps["w_gu"] = [aps["w_gu0"], aps["w_gu1"]]
    aps["w_dn"] = [aps["w_dn0"], aps["w_dn1"]]
    out = nc.dram_tensor("out", (P, KT, LAT), F32, kind="ExternalOutput").ap()
    build(nc, aps, out)
    r = _run(nc, [arrays], core_ids=[0])
    return r.results[0]["out"].transpose(1, 0, 2).reshape(D, LAT).T.reshape(1, LAT, D)
```

```python
from contextlib import ExitStack

import numpy as np

import concourse.bass as bass
from concourse import mybir

F32 = mybir.dt.float32
F32R = mybir.dt.float32r
I32 = mybir.dt.int32
U32 = mybir.dt.uint32
ALU = mybir.AluOpType
ACT = mybir.ActivationFunctionType
AX = mybir.AxisListType

P = 128
D = 1024
KT = D // P
CTX, LAT = 256, 256
T = CTX + LAT
NTT = T // P
EPS = 1e-6
LAYERS = 2
HEADS, HD = 8, 64
AT = HEADS * HD // P
CH = 64
NCH = T // CH
GT = 2
TAU = 16.0
FM = 16
FJ = 11
NE = 8
MODT = 6 * D // P
UNIT = KT * P
DUNIT = FJ * P
R = 5
H = 3
PROJ, OUT, BLOCK = FM + 8, KT, 2 * FJ + KT
M0 = 16
SQ0 = 4

LA, LK, LQ, AK, SB, SC, SX, AQ = 0, 1, 3, 5, 6, 8, 10, 12


def build(nc, d, out):
    ctx = ExitStack()
    with ctx:
        def sb(name, shape, dt=F32, stack=ctx):
            return stack.enter_context(nc.sbuf_tensor(name, shape, dt))

        raw = sb("raw", [P, R, DUNIT])
        whi = sb("whi", [P, H, DUNIT], F32R)
        wlo = sb("wlo", [P, H, DUNIT], F32R)
        xT = sb("xT", [P, KT, T])
        ident = sb("ident", [P, P])
        rot = sb("rot", [P, P])
        ones = sb("ones", [P, P])
        cos = sb("cos", [P, LAT])
        sin = sb("sin", [P, LAT])
        amask = sb("amask", [P, 2, P])
        gmask = sb("gmask", [P, 2, P], I32)
        reset = sb("reset", [P, T])
        iota = sb("iota", [P, NE])
        c_raw = sb("c_raw", [P, 2 * KT])
        c_act = sb("c_act", [P, KT, 2])
        c_split = sb("c_split", [P, KT, 4], F32R)
        modrow = sb("modrow", [4, 2, 512])
        modsum = sb("modsum", [P, 2, 8])
        b_mod = sb("b_mod", [P, LAYERS, 2 * MODT])
        norm_g = sb("norm_g", [P, LAYERS, 2, 2 * KT])
        final_g = sb("final_g", [P, KT])
        sink = sb("sink", [P, LAYERS, HEADS])
        w2 = sb("w2", [CH, LAYERS, GT * P])
        gla_b = sb("gla_b", [P, LAYERS, 2, GT])
        gla_g = sb("gla_g", [P, LAYERS])
        conv_w = sb("conv_w", [P, LAYERS, 3, 2])
        router = sb("router", [P, KT, NE])
        mod = sb("mod", [P, LAYERS, 2 * MODT])
        gain = sb("gain", [P, LAYERS, 2, 2 * KT])
        epsc = sb("epsc", [P, 1])
        rs = sb("rs", [P, T])
        sq = sb("sq", [P, 2, T])
        xn = sb("xn", [P, 2, T])
        hf = sb("hf", [P, 2, T])
        negsink = sb("negsink", [P, LAYERS, HEADS])
        mx = sb("mx", [P, NTT * HEADS])
        negm = sb("negm", [P, NTT * HEADS])
        psumrow = sb("psumrow", [P, NTT * HEADS])
        esink = sb("esink", [P, NTT * HEADS])
        rden = sb("rden", [P, NTT * HEADS])
        decay = sb("decay", [P, 2, GT * NCH])
        gss = sb("gss", [P, NTT * 8])
        logits = sb("logits", [P, 2, NE])
        top = sb("top", [P, 2, 8])
        topi = sb("topi", [P, 2, 8], U32)
        topf = sb("topf", [P, 2, 8])
        gate2 = sb("gate2", [P, 2, 4])
        pick = sb("pick", [P, 2, 2, NE])

        region = ExitStack()
        hhi = sb("hhi", [P, KT, T], F32R, region)
        hlo = sb("hlo", [P, KT, T], F32R, region)
        region.close()
        gtt = sb("gtt", [P, 2, GT, T])
        gqp = sb("gqp", [P, 2, GT, T])
        gqb = sb("gqb", [P, 2, GT, T])
        gkt = sb("gkt", [P, NTT, 2, GT * P])
        gb, gkp, gk = sq, xn, hf

        region = ExitStack()
        fhi = sb("fhi", [P, FJ, T], F32R, region)
        flo = sb("flo", [P, FJ, T], F32R, region)
        sg = sb("sg", [P, 2, T], F32, region)
        region.close()
        region = ExitStack()
        htm = sb("htm", [P, 2, D], F32, region)
        hs_hi = sb("hs_hi", [P, KT, P], F32R, region)
        hs_lo = sb("hs_lo", [P, KT, P], F32R, region)
        pair_in = sb("pair_in", [P, 2, P], F32, region)
        pair_w = sb("pair_w", [P, 2, P], F32, region)
        scat = sb("scat", [P, LAT], F32, region)
        esg = sb("esg", [P, 2, P], F32, region)
        eact = sb("eact", [P, 2, P], F32, region)
        ehi = sb("ehi", [P, FJ, P], F32R, region)
        elo = sb("elo", [P, FJ, P], F32R, region)
        ys = sb("ys", [P, D], F32, region)
        yacc = sb("yacc", [P, KT, LAT], F32, region)
        slots = sb("slots", [P, P], F32, region)
        before = sb("before", [P, P], F32, region)
        lgT = sb("lgT", [NE, LAT], F32, region)
        sel = sb("sel", [P, 2, NE], F32, region)
        sel0 = sb("sel0", [P, 2, NE], F32, region)
        posx = sb("posx", [P, 2, 2 * NE + 1], F32, region)
        pickx = sb("pickx", [P, 2, 2 * NE], F32, region)
        count = sb("count", [P, 4], F32, region)
        passes = sb("passes", [P, 2], I32, region)
        region.close()
        region = ExitStack()
        la = sb("la", [CH, T], F32, region)
        lk = sb("lk", [P, GT, T], F32, region)
        lq = sb("lq", [P, GT, T], F32, region)
        ak = sb("ak", [P, T], F32, region)
        aq = sb("aq", [P, AT, T], F32, region)
        s_b = sb("s_b", [P, 2, T], F32, region)
        s_c = sb("s_c", [P, 2, T], F32, region)
        cx = sb("cx", [P, 2, 2, LAT + 2], F32, region)
        vt = sb("vt", [P, NTT, 384], F32, region)
        gate = sb("gate", [P, NTT, 512], F32, region)
        part = ExitStack()
        state = sb("state", [P, 2, NCH + 1, GT * CH], F32, part)
        am = sb("am", [P, 2, 4 * P], F32, part)
        go = sb("go", [P, NTT, 512], F32, part)
        part.close()
        asc = sb("asc", [P, 3072], F32, region)
        akz = sb("akz", [P, 2, T], F32, region)
        region.close()
        region = ExitStack()
        outT = sb("outT", [P, KT, LAT], F32, region)
        region.close()

        gtf = go[:, :, :].rearrange("p (a g) t -> p a g t", a=2)
        gt1 = [gtf[:, 0, :, :], gtt[:, 0, :, :]]
        gt2 = [gtf[:, 1, :, :], gtt[:, 1, :, :]]

        prob = asc[:, 0:1536].rearrange("p (s n) -> p s n", s=3)
        probT = asc[:, 1536:2560].rearrange("p (s n) -> p s n", s=2)
        rt1 = asc[:, 0:1024]
        rt2 = asc[:, 1024:2048]

        ps = ctx.enter_context(nc.psum_tensor("ps", [P, 8, 512], F32))

        def sem(name):
            return ctx.enter_context(nc.semaphore(name))

        def sems(name, n):
            return [sem(f"{name}{i}") for i in range(n)]

        landed = sems("landed", R)
        hi_ready = sem("hi_ready")
        lo_ready = sem("lo_ready")
        split_used = sem("split_used")
        modrow_out = sem("modrow_out")
        modT_done = sem("modT_done")
        mod_out = sem("mod_out")
        c_done = sem("c_done")
        c_hi = sem("c_hi")
        const_in = sem("const_in")
        x_in = sem("x_in")
        c_in = sem("c_in")
        init_done = sem("init_done")
        sq_ready = sem("sq_ready")
        sumsq_done = sem("sumsq_done")
        rs_ready = sem("rs_ready")
        hf_ready = sem("hf_ready")
        hhi_done = sem("hhi_done")
        hlo_done = sem("hlo_done")
        fm_out = sems("fm_out", LAYERS)
        cx_out = sems("cx_out", LAYERS)
        v_out = sems("v_out", LAYERS)
        g_out = sems("g_out", LAYERS)
        conv_out = sems("conv_out", LAYERS)
        z_done = sems("z_done", LAYERS)
        abs_done = sems("abs_done", LAYERS)
        sp_ready = sems("sp_ready", LAYERS)
        d_ready = sems("d_ready", LAYERS)
        e_ready = sems("e_ready", LAYERS)
        e_used = sems("e_used", LAYERS)
        kt_done = sems("kt_done", LAYERS)
        kt_out = sems("kt_out", LAYERS)
        dec_ready = sems("dec_ready", LAYERS)
        u_done = sems("u_done", LAYERS)
        st_ready = sems("st_ready", LAYERS)
        at_done = sems("at_done", LAYERS)
        am_ready = sems("am_ready", LAYERS)
        o_done = sems("o_done", LAYERS)
        o_out = sems("o_out", LAYERS)
        ss_ready = sems("ss_ready", LAYERS)
        grs_ready = sems("grs_ready", LAYERS)
        y_ready = sems("y_ready", LAYERS)
        yT_done = sems("yT_done", LAYERS)
        mixhi = sems("mixhi", LAYERS)
        mixlo = sems("mixlo", LAYERS)
        rot_done = sems("rot_done", LAYERS)
        s_done = sems("s_done", LAYERS)
        negm_ready = sems("negm_ready", LAYERS)
        p_ready = sems("p_ready", LAYERS)
        pT_done = sems("pT_done", LAYERS)
        pT_out = sems("pT_out", LAYERS)
        pv_done = sems("pv_done", LAYERS)
        esk_ready = sems("esk_ready", LAYERS)
        pn_ready = sems("pn_ready", LAYERS)
        akz_ready = sems("akz_ready", LAYERS)
        zeroed = sems("zeroed", LAYERS)
        z_out = sems("z_out", LAYERS)
        ahi_ready = sems("ahi_ready", LAYERS)
        alo_ready = sems("alo_ready", LAYERS)
        x_mixed = sems("x_mixed", LAYERS)
        sg_ready = sems("sg_ready", LAYERS)
        fh_ready = sems("fh_ready", LAYERS)
        fhi_ready = sems("fhi_ready", LAYERS)
        flo_ready = sems("flo_ready", LAYERS)
        down_out = sems("down_out", LAYERS)
        lg_done = sem("lg_done")
        topd_ready = sem("topd_ready")
        tope_ready = sem("tope_ready")
        lgT_done = sem("lgT_done")
        lgT_out = sem("lgT_out")
        moe_const = sem("moe_const")
        sel_ready = sem("sel_ready")
        pos_done = sem("pos_done")
        passes_ready = sem("passes_ready")
        htm_done = sem("htm_done")
        htm_out = sem("htm_out")
        pair_ready = sem("pair_ready")
        gather_done = sem("gather_done")
        hs_half = sem("hs_half")
        hs_ready = sem("hs_ready")
        pairw_ready = sem("pairw_ready")
        scat_done = sem("scat_done")
        scat_out = sem("scat_out")
        aT_done = sem("aT_done")
        ys_ready = sem("ys_ready")
        sc_done = sem("sc_done")
        y_added = sem("y_added")
        x_last = sem("x_last")
        out_ready = sem("out_ready")
        stored = sem("stored")
        act_order = sem("act_order")
        dve_order = sem("dve_order")

        def mods(l, q0, q1):
            return [("mod", l, q) for q in range(q0, q1)]

        def proj_units(l):
            fm = [("fm", l, m) for m in range(FM)]
            return (fm[:5] + [("tv", l, i) for i in range(4)] + fm[5:10] + [("tg", l, i) for i in range(4)]
                    + fm[10:])

        START = mods(0, 0, M0)
        proj0 = []
        q = M0
        for n, unit in enumerate(proj_units(0)):
            proj0.append(unit)
            more = min(MODT - q, 1 if n < 16 else 2)
            proj0 += mods(0, q, q + more)
            q += more
        assert q == MODT
        GLA_MODS, ATT_MODS = 16, 32
        PROJ_STAGE = [proj0, proj_units(1)]
        OUT_STAGE = [[("out", l, m) for m in range(OUT)] for l in range(LAYERS)]
        stream0 = START + proj0 + mods(1, 0, MODT) + OUT_STAGE[0]
        stream1 = PROJ_STAGE[1] + OUT_STAGE[1]
        V_PROJ = [len(START), len(stream0) + 2 * BLOCK]
        V_GLA0 = V_PROJ[0] + len(proj0)
        V_ATT0 = V_GLA0 + GLA_MODS
        V_OUT = [V_ATT0 + ATT_MODS, V_PROJ[1] + PROJ]
        V_FFN = [len(stream0), V_OUT[1] + OUT]
        assert V_OUT[0] + OUT == V_FFN[0]

        def source(unit):
            kind, l, n = unit
            if kind == "mod":
                return d["w_mod"][l, n], UNIT
            if kind == "fm":
                return d["w_fm"][l, n], UNIT
            if kind == "tv":
                return d["w_tv"][l, n], 768
            if kind == "tg":
                return d["w_tg"][l, n], UNIT
            return d["w_out"][l, n], UNIT

        def unit_of(v):
            if v < len(stream0):
                return stream0[v]
            if V_PROJ[1] <= v < V_FFN[1]:
                return stream1[v - V_PROJ[1]]
            return None

        def cols_of(v):
            unit = unit_of(v)
            return source(unit)[1] if unit else UNIT

        pieces = [[] for _ in range(KT)]
        for u in range(KT):
            c = u * DUNIT
            while c < (u + 1) * DUNIT:
                n = min(512 - c % 512, (u + 1) * DUNIT - c)
                pieces[u].append((c // D, c % D, n, c - u * DUNIT))
                c += n

        def block_unit(l, i, r):
            if r < 2 * FJ:
                src = d["w_gu"][l][bass.ds(i * 2 * FJ + r, 1)]
                n = UNIT
            else:
                src = d["w_dn"][l][bass.ds(i * KT + r - 2 * FJ, 1)]
                n = DUNIT
            return src.rearrange("a p n -> (a p) n"), n

        block = ctx.enter_context(nc.Block())

        @block.sync
        def _(sp):
            def load(v, src, n):
                if v >= R:
                    sp.wait_ge(lo_ready, v - R + 1)
                sp.dma_start(raw[:, v % R, 0:n], src).then_inc(landed[v % R], 16)

            def ffn(l, v0, blocks):
                with sp.Fori(0, blocks) as i:
                    for r in range(BLOCK):
                        src, n = block_unit(l, i, r)
                        sp.wait_ge(lo_ready, i * BLOCK + (v0 + r - R + 1))
                        slot = (v0 + r) % R
                        sp.dma_start(raw[:, slot, 0:n], src).then_inc(landed[slot], 16)

            for v, unit in enumerate(stream0):
                load(v, *source(unit))
            ffn(0, V_FFN[0], 2)
            for n, unit in enumerate(stream1):
                load(V_PROJ[1] + n, *source(unit))
            v0 = V_FFN[1]
            for r in range(R):
                load(v0 + r, d["w_gu"][1][r], UNIT)
            sp.wait_ge(passes_ready, 1)
            rounds = sp.value_load(passes[0:1, 1:2], min_val=1, max_val=2)
            with sp.Fori(0, rounds) as b:
                with sp.Fori(0, NE) as e:
                    for r in range(BLOCK):
                        src, n = block_unit(1, e, r + R if r + R < BLOCK else r + R - BLOCK)
                        if r + R >= BLOCK:
                            src = d["w_gu"][1][bass.ds(e * 2 * FJ + (2 * FJ + r + R - BLOCK), 1)].rearrange(
                                "a p n -> (a p) n")
                        sp.wait_ge(lo_ready, b * (NE * BLOCK) + e * BLOCK + (v0 + r + 1))
                        slot = (v0 + r) % R
                        sp.dma_start(raw[:, slot, 0:n], src).then_inc(landed[slot], 16)
            for r in range(R):
                sp.wait_ge(landed[(v0 + r) % R], rounds * (16 * NE * BLOCK // R) + 16 * ((v0 + r) // R + 1))

            for k in range(KT):
                sp.wait_ge(out_ready, k + 1)
                sp.dma_start(out[:, k, :], outT[:, k, :]).then_inc(stored, 16)
            sp.wait_ge(stored, 16 * KT)

        def split_hi(act, v, cols, i=None):
            slot = v % R
            if i is None:
                act.wait_ge(landed[slot], 16 * (v // R + 1))
                if v >= H:
                    act.wait_ge(split_used, v - H + 1)
            else:
                act.wait_ge(landed[slot], i * (16 * BLOCK // R) + 16 * (v // R + 1))
                act.wait_ge(split_used, i * BLOCK + (v - H + 1))
            nc.scalar.activation(whi[:, v % H, 0:cols], raw[:, slot, 0:cols], ACT.Copy).then_inc(hi_ready, 1)

        def split_lo(dve, v, cols, i=None):
            dve.wait_ge(hi_ready, v + 1 if i is None else i * BLOCK + (v + 1))
            nc.vector.tensor_tensor(wlo[:, v % H, 0:cols], raw[:, v % R, 0:cols],
                                    whi[:, v % H, 0:cols].bitcast(F32), ALU.subtract).then_inc(lo_ready, 1)

        def x_ready(eng, n, k):
            if n == 0:
                if k == 0:
                    eng.wait_ge(x_in, 16)
            elif n in (1, 3):
                eng.wait_ge(x_mixed[n // 2], k + 1)
            elif n == 2:
                eng.wait_ge(down_out[0], 1 + KT + k + 1)
            else:
                eng.wait_ge(x_last, k + 1)

        def MOD_BANK(g):
            g_gla = MODT // 4 - 1
            return 5 if g < M0 // 4 else 6 if g < g_gla else 5 if g < g_gla + GLA_MODS // 4 else 2

        def projected(eng, l):
            eng.wait_ge(split_used, V_PROJ[l] + len(PROJ_STAGE[l]))

        def first_col(n):
            return CTX if n >= 3 else 0

        def q_col(l):
            return CTX if l else 0

        def att_tiles(l):
            return [2, 3] if l else [2, 3, 0, 1]

        def gla_tiles(dr):
            return [0, 1, 2, 3] if dr == 0 else [1, 0, 3, 2]

        def gla_chunks(dr):
            return [0, 1] if dr == 0 else [1, 0]

        def gla_reads(l):
            return range(2 if l else 0, NTT)

        @block.tensor
        def _(pe):
            def mod_unit(v):
                _kind, l, q = unit_of(v)
                g = l * MODT // 4 + q // 4
                if q % 4 == 0:
                    if g:
                        pe.wait_ge(modrow_out, g)
                    else:
                        pe.wait_ge(c_done, 1)
                if q % 4 == 1:
                    mod_turns(g)
                pe.wait_ge(lo_ready, v + 1)
                for kk in range(2):
                    k = 2 * (q % 4) + kk
                    for w in (whi, wlo):
                        mm = nc.tensor.matmul(ps[0:4, 7, :], c_split[:, k, :], w[:, v % H, kk * 512:(kk + 1) * 512],
                                              start=(k == 0 and w is whi), stop=(k == KT - 1 and w is wlo))
                mm.then_inc(split_used, 1)

            turned = [0]

            def mod_turns(n):
                for g in range(turned[0], n):
                    pe.wait_ge(modrow_out, g + 1)
                    if g:
                        pe.wait_ge(mod_out, g)
                    else:
                        pe.wait_ge(const_in, 16 * N_CONST)
                    for m in range(4):
                        mm = nc.tensor.transpose(ps[:, MOD_BANK(g), 4 * m:4 * m + 4],
                                                 modrow[0:4, g % 2, m * P:(m + 1) * P], ident[0:4, 0:4])
                    mm.then_inc(modT_done, 1)
                turned[0] = n

            def three(outp, whs, wls, xh, xl, first, last):
                nc.tensor.matmul(outp, whs, xh, start=first, stop=False)
                nc.tensor.matmul(outp, whs, xl, start=False, stop=False)
                return nc.tensor.matmul(outp, wls, xh, start=False, stop=last)

            def fm_tile(v, outp, xh, xl, nk, ready=None, order=None):
                s = v % H
                order = order or list(range(nk))
                for n, k in enumerate(order):
                    if ready:
                        ready(k)
                    mm = three(outp, whi[:, s, k * P:(k + 1) * P], wlo[:, s, k * P:(k + 1) * P],
                               xh(k), xl(k), n == 0, n == nk - 1)
                return mm

            def normed(n):
                return lambda k: pe.wait_ge(hlo_done, KT * n + k + 1)

            def norm_sum(n, k):
                pe.wait_ge(sq_ready, KT * n + k + 1)
                nc.tensor.matmul(ps[:, 6, first_col(n):T], ones[:, :], sq[:, k % 2, first_col(n):T],
                                 start=(k == 0), stop=(k == KT - 1)).then_inc(sumsq_done, 1)

            def projection(l):
                def fm(v, f):
                    c0 = q_col(l) if f not in (LA, LK, LK + 1, AK) else 0
                    pe.wait_ge(lo_ready, v + 1)
                    if SX <= f - 2 < AQ:
                        pe.wait_ge(cx_out[l], f - 2 - SX + 1)
                    elif f >= 2:
                        pe.wait_ge(fm_out[l], f - 1 - (AQ - SX if f - 2 >= AQ else 0))
                    fm_tile(v, ps[:, f % 2, c0:T], lambda k: hhi[:, k, c0:T], lambda k: hlo[:, k, c0:T],
                            KT, ready=normed(2 * l) if f == LA else None).then_inc(split_used, 1)

                def tm(v, i, n, t0):
                    pe.wait_ge(lo_ready, v + 1)
                    s = v % H
                    for kk in range(2):
                        k = 2 * i + kk
                        for t in range(t0, NTT):
                            o = ps[:, 2 + t, 0:n]
                            wh, wl = whi[:, s, kk * n:(kk + 1) * n], wlo[:, s, kk * n:(kk + 1) * n]
                            hh, hl = hhi[:, k, t * P:(t + 1) * P], hlo[:, k, t * P:(t + 1) * P]
                            nc.tensor.matmul(o, hh, wh, start=(k == 0), stop=False)
                            nc.tensor.matmul(o, hh, wl, start=False, stop=False)
                            mm = nc.tensor.matmul(o, hl, wh, start=False, stop=(k == KT - 1))
                    mm.then_inc(split_used, 1)

                for n, (kind, _l, m) in enumerate(PROJ_STAGE[l]):
                    v = V_PROJ[l] + n
                    if kind == "fm":
                        fm(v, m)
                        if m == AQ:
                            pe.wait_ge(g_out[l], len(list(gla_reads(l))))
                            for dr in range(2):
                                for p in range(GT):
                                    nc.tensor.matmul(ps[:, 2 + 2 * dr + p, :],
                                                     w2[32 * dr:32 * dr + 32, l, p * P:(p + 1) * P],
                                                     la[32 * dr:32 * dr + 32, :], start=True, stop=True
                                                     ).then_inc(z_done[l], 1)
                    elif kind == "tv":
                        tm(v, m, 384, 0)
                    elif kind == "tg":
                        if m == 0:
                            pe.wait_ge(v_out[l], NTT)
                        tm(v, m, 512, 2 if l else 0)
                    else:
                        mod_unit(v)

            def gla(l):
                reads = list(gla_reads(l))
                n_u = n_at = n_o = 0
                for dr in range(2):
                    if dr == 0:
                        pe.wait_ge(fm_out[l], 14)
                    if dr and l == 0:
                        pe.wait_ge(mod_out, MODT // 4 + GLA_MODS // 8 - 1)
                    pe.wait_ge(e_used[l], 4 * dr + 1)
                    if dr:
                        pe.wait_ge(st_ready[l], 2 * NTT)
                    for p in range(GT):
                        for t in range(NTT):
                            mm = nc.tensor.transpose(ps[:, 4 * dr + p, t * P:(t + 1) * P], gk[:, p, t * P:(t + 1) * P],
                                                     ident[:, :])
                        mm.then_inc(kt_done[l], 1)
                    pe.wait_ge(kt_out[l], GT * (dr + 1))
                    if dr == 0:
                        pe.wait_ge(zeroed[l], 1)
                        if l == 0:
                            pe.wait_ge(mod_out, MODT // 4 - 1)
                    for step, t in enumerate(gla_tiles(dr)):
                        if n_u == 1:
                            pe.wait_ge(z_out[l], 1)
                        if n_u >= 2:
                            pe.wait_ge(st_ready[l], 2 * (n_u - 1))
                        for c in range(2):
                            for h in range(4):
                                p, hh = h // 2, h % 2
                                mm = nc.tensor.matmul(
                                    ps[CH * hh:CH * hh + CH, (6, 4)[n_u % 2], (2 * c + p) * CH:(2 * c + p + 1) * CH],
                                    gkt[:, t, c, h * CH:(h + 1) * CH], vt[:, t, P + h * CH:P + (h + 1) * CH],
                                    start=True, stop=True)
                        mm.then_inc(u_done[l], 1)
                        n_u += 1
                        if t not in reads:
                            continue
                        pe.wait_ge(e_used[l], 4 * dr + 3)
                        if n_at >= 2:
                            pe.wait_ge(am_ready[l], n_at - 1)
                        for p in range(GT):
                            mm = nc.tensor.matmul(ps[:, n_at % 2, 2 * p * P:2 * (p + 1) * P],
                                                  gkp[:, p, t * P:(t + 1) * P], gqp[:, :, p, t * P:(t + 1) * P],
                                                  start=True, stop=True)
                        mm.then_inc(at_done[l], 1)
                        n_at += 1
                        if l == 0:
                            if n_at == 1:
                                pe.wait_ge(z_out[l], 1)
                            for n in range(2):
                                mod_unit(V_GLA0 + 2 * (n_u - 1) + n)
                        pe.wait_ge(am_ready[l], n_at)
                        pe.wait_ge(e_used[l], 4 * dr + 4)
                        pe.wait_ge(st_ready[l], 8 * dr + 2 * step + 1)
                        if n_o >= 2:
                            pe.wait_ge(o_out[l], n_o - 1)
                        bank = 2 + n_o % 2
                        for h in range(4):
                            pv0 = P + h // 2 * P
                            nc.tensor.matmul(ps[:, bank, h * P:(h + 1) * P], am[:, dr, h * P:(h + 1) * P],
                                             vt[:, t, pv0:pv0 + P], start=(h == 0), stop=False,
                                             skip_group_check=True)
                        for ci, c in enumerate(gla_chunks(dr)):
                            for h in range(4):
                                p, hh = h // 2, h % 2
                                o0 = h * P + hh * CH
                                mm = nc.tensor.matmul(
                                    ps[CH * c:CH * c + CH, bank, o0:o0 + CH],
                                    gqb[:, hh, p, t * P + CH * c:t * P + CH * c + CH],
                                    state[:, dr, 2 * step + ci, p * CH:(p + 1) * CH],
                                    start=False, stop=(ci == 1), skip_group_check=True)
                        mm.then_inc(o_done[l], 1)
                        n_o += 1
                pe.wait_ge(o_out[l], n_o)
                for j in range(AT + 1):
                    src = aq[:, j, CTX:T] if j < AT else ak[:, CTX:T]
                    mm = nc.tensor.matmul(ps[:, j // 2, (j % 2) * LAT:(j % 2) * LAT + LAT], rot[:, :], src,
                                          start=True, stop=True)
                mm.then_inc(rot_done[l], 1)
                pe.wait_ge(y_ready[l], 1)
                if l == 0:
                    pe.wait_ge(mod_out, MODT // 4 + GLA_MODS // 4 - 1)
                pe.wait_ge(st_ready[l], 4 * NTT)
                for f in range(GT):
                    for n, t in enumerate(reads):
                        mm = nc.tensor.transpose(ps[:, 4 + f, t * P:(t + 1) * P],
                                                 gb[:, n // 2, (n % 2) * 256 + f * P:(n % 2) * 256 + (f + 1) * P],
                                                 ident[:, :])
                    mm.then_inc(yT_done[l], 1)

            def attention(l):
                tiles = att_tiles(l)
                n_items = len(tiles) * HEADS
                pe.wait_ge(akz_ready[l], 1)
                pe.wait_ge(zeroed[l], 2)

                def keys(i):
                    return 4 if tiles[i // HEADS] >= 2 else 2

                def scores(i):
                    t, h = tiles[i // HEADS], i % HEADS
                    if i >= 2:
                        pe.wait_ge(p_ready[l], i - 1)
                    nc.tensor.matmul(ps[:, i % 2, 0:keys(i) * P], aq[:, h // 2, t * P:(t + 1) * P],
                                     akz[:, h % 2, 0:keys(i) * P], start=True, stop=True).then_inc(s_done[l], 1)

                def turn(i):
                    if i == 1:
                        pe.wait_ge(mixlo[l], GT)
                    pe.wait_ge(pn_ready[l], i + 1)
                    if i >= 2:
                        pe.wait_ge(pT_out[l], i - 1)
                    for k in range(keys(i)):
                        mm = nc.tensor.transpose(ps[:, 3 + i % 2, k * P:(k + 1) * P],
                                                 prob[:, i % 3, k * P:(k + 1) * P], ident[:, :])
                    mm.then_inc(pT_done[l], 1)

                def pv(i):
                    n, h = i // HEADS, i % HEADS
                    pe.wait_ge(pT_out[l], i + 1)
                    if h == 0 and n >= 2:
                        pe.wait_ge(alo_ready[l], n - 1)
                    kv = CH * (h % 2)
                    for k in range(keys(i)):
                        mm = nc.tensor.matmul(ps[kv:kv + HD, 5 + n % 2, h // 2 * P:(h // 2 + 1) * P],
                                              vt[:, k, kv:kv + HD], probT[:, i % 2, k * P:(k + 1) * P],
                                              start=(k == 0), stop=(k == keys(i) - 1))
                    mm.then_inc(pv_done[l], 1)

                for i in range(n_items + 3):
                    if i < n_items:
                        scores(i)
                    if 2 <= i < n_items + 2:
                        turn(i - 2)
                    if l == 0 and i < n_items:
                        mod_unit(V_ATT0 + i)
                    if i >= 3:
                        pv(i - 3)
                if l == 0:
                    mod_turns(2 * MODT // 4)

            def out_projection(l):
                v0 = V_OUT[l]
                c0 = q_col(l)
                n_att = len(att_tiles(l))
                pe.wait_ge(mixlo[l], 4)
                pe.wait_ge(p_ready[l], HEADS * n_att)

                def attended(k):
                    if k < AT:
                        pe.wait_ge(alo_ready[l], n_att)

                late = list(range(AT, KT)) + list(range(AT))
                for m in range(KT):
                    v = v0 + m
                    pe.wait_ge(lo_ready, v + 1)
                    if m >= 2:
                        pe.wait_ge(x_mixed[l], m - 1)
                    fm_tile(v, ps[:, m % 2, c0:T], lambda k: hhi[:, k, c0:T], lambda k: hlo[:, k, c0:T],
                            KT, ready=attended if m == 0 else None, order=late).then_inc(split_used, 1)
                    if m:
                        norm_sum(2 * l + 1, m - 1)
                norm_sum(2 * l + 1, KT - 1)

            def ffn(l, v0, blocks):
                c0 = q_col(l)
                with pe.Fori(0, blocks) as i:
                    for j in range(FJ):
                        for part in range(2):
                            r = 2 * j + part
                            v = v0 + r
                            pe.wait_ge(lo_ready, i * BLOCK + (v + 1))
                            if part == 0 and j >= 2:
                                pe.wait_ge(fh_ready[l], i * FJ + (j - 1))
                            fm_tile(v, ps[:, 2 * part + j % 2, c0:T], lambda k: hhi[:, k, c0:T],
                                    lambda k: hlo[:, k, c0:T], KT, ready=normed(2 * l + 1) if r == 0 else None
                                    ).then_inc(split_used, 1)
                    for m in range(KT):
                        v = v0 + 2 * FJ + m
                        pe.wait_ge(lo_ready, i * BLOCK + (v + 1))
                        if m == 0:
                            pe.wait_ge(down_out[l], i * KT + 1)
                        if m >= 2:
                            pe.wait_ge(down_out[l], i * KT + m)
                        fm_tile(v, ps[:, 4 + m % 2, c0:T], lambda k: fhi[:, k, c0:T], lambda k: flo[:, k, c0:T],
                                FJ, ready=(lambda k: pe.wait_ge(flo_ready[l], i * FJ + (k + 1))) if m == 0 else None
                                ).then_inc(split_used, 1)

            def gather(i):
                pe.wait_ge(pair_ready, i + 1)
                for k in range(KT):
                    for t in range(2):
                        mm = nc.tensor.matmul(ps[:, 6 + k // 4, (k % 4) * P:(k % 4 + 1) * P],
                                              htm[:, t, k * P:(k + 1) * P], pair_in[:, t, :],
                                              start=(t == 0), stop=(t == 1))
                mm.then_inc(gather_done, 1)

            def scatter(i, n):
                if n == 0:
                    pe.wait_ge(ys_ready, i + 1)
                    pe.wait_ge(scat_out, i + 1)
                if n >= 2:
                    pe.wait_ge(y_added, i * 4 + (n - 1))
                for f in range(2):
                    mm = nc.tensor.matmul(ps[:, 6 + n % 2, f * LAT:(f + 1) * LAT],
                                          ys[:, (2 * n + f) * P:(2 * n + f + 1) * P], scat[:, :],
                                          start=True, stop=True)
                mm.then_inc(sc_done, 1)

            def turn_act(i, j):
                pe.wait_ge(fh_ready[1], i * FJ + (j + 1))
                if j >= 2:
                    pe.wait_ge(flo_ready[1], i * FJ + (j - 1))
                nc.tensor.transpose(ps[:, 2 + j % 2, 0:P], eact[:, j % 2, :], ident[:, :]).then_inc(aT_done, 1)

            def experts():
                v0 = V_FFN[1]
                gather(0)
                pe.wait_ge(passes_ready, 1)
                n_pass = pe.value_load(passes[0:1, 0:1], min_val=NE, max_val=2 * NE)
                with pe.Fori(0, n_pass) as i:
                    pe.wait_ge(hs_ready, i + 1)
                    for j in range(FJ):
                        for half in range(2):
                            v = v0 + 2 * j + half
                            pe.wait_ge(lo_ready, i * BLOCK + (v + 1))
                            s = v % H
                            o = ps[:, j % 2, 0:2 * P]
                            for kk in range(4):
                                k = 4 * half + kk
                                wh, wl = whi[:, s, kk * 2 * P:(kk + 1) * 2 * P], wlo[:, s, kk * 2 * P:(kk + 1) * 2 * P]
                                nc.tensor.matmul(o, hs_hi[:, k, :], wh, start=(k == 0), stop=False)
                                nc.tensor.matmul(o, hs_hi[:, k, :], wl, start=False, stop=False)
                                mm = nc.tensor.matmul(o, hs_lo[:, k, :], wh, start=False, stop=(k == KT - 1))
                            mm.then_inc(split_used, 1)
                        if j:
                            turn_act(i, j - 1)
                        if 1 <= j <= 4:
                            scatter(i, j - 1)
                        if j == 6:
                            pe.wait_ge(pairw_ready, i + 1)
                            for t in range(2):
                                mm = nc.tensor.transpose(ps[:, 6, t * P:(t + 1) * P], pair_w[:, t, :], ident[:, :])
                            mm.then_inc(scat_done, 1)
                    for u in range(KT):
                        v = v0 + 2 * FJ + u
                        pe.wait_ge(lo_ready, i * BLOCK + (v + 1))
                        s = v % H
                        for j, c, n, w in pieces[u]:
                            pe.wait_ge(flo_ready[1], i * FJ + (j + 1))
                            o = ps[:, 4 + c // 512, c % 512:c % 512 + n]
                            nc.tensor.matmul(o, ehi[:, j, :], whi[:, s, w:w + n], start=(j == 0), stop=False,
                                             skip_group_check=True)
                            nc.tensor.matmul(o, ehi[:, j, :], wlo[:, s, w:w + n], start=False, stop=False,
                                             skip_group_check=True)
                            mm = nc.tensor.matmul(o, elo[:, j, :], whi[:, s, w:w + n], start=False,
                                                  stop=(j == FJ - 1), skip_group_check=True)
                        mm.then_inc(split_used, 1)
                        if u == 0:
                            turn_act(i, FJ - 1)
                        if u == 1:
                            pe.wait_ge(scat_out, i + 2)
                            gather(i + 1)
                for n in range(4):
                    scatter(n_pass, n)

            pe.wait_ge(init_done, 1)
            for v in range(len(START)):
                mod_unit(v)
                if SQ0 < v <= SQ0 + KT:
                    norm_sum(0, v - SQ0 - 1)
            mod_turns(M0 // 4)
            projection(0)
            gla(0)
            attention(0)
            out_projection(0)
            ffn(0, V_FFN[0], 2)
            for k in range(KT):
                norm_sum(2, k)
            projection(1)
            gla(1)
            attention(1)
            out_projection(1)
            for k in range(KT):
                pe.wait_ge(hlo_done, KT * 3 + k + 1)
                for part in (hhi, hlo):
                    mm = nc.tensor.matmul(ps[0:NE, 7, 0:LAT], router[:, k, :], part[:, k, CTX:T].bitcast(F32),
                                          start=(k == 0 and part is hhi), stop=(k == KT - 1 and part is hlo))
            mm.then_inc(lgT_done, 1)
            for t in range(2):
                for k in range(KT):
                    for part in (hhi, hlo):
                        mm = nc.tensor.matmul(ps[:, 2 * t + k // 4, (k % 4) * P:(k % 4 + 1) * P],
                                              part[:, k, CTX + t * P:CTX + (t + 1) * P].bitcast(F32), ident[:, :],
                                              start=(part is hhi), stop=(part is hlo))
                mm.then_inc(htm_done, 1)
                if t == 0:
                    pe.wait_ge(lgT_out, 1)
                    for n in range(2):
                        mm = nc.tensor.transpose(ps[:, 7, n * NE:(n + 1) * NE], lgT[:, n * P:(n + 1) * P],
                                                 ident[0:NE, 0:NE])
                    mm.then_inc(lg_done, 1)
            pe.wait_ge(sel_ready, 1)
            pe.wait_ge(moe_const, 32)
            nc.tensor.matmul(ps[:, 6, 0:NE], before[:, :], sel[:, 0, :], start=True, stop=True)
            nc.tensor.matmul(ps[:, 6, NE:2 * NE], ones[:, :], sel[:, 0, :], start=True, stop=False)
            nc.tensor.matmul(ps[:, 6, NE:2 * NE], before[:, :], sel[:, 1, :], start=False, stop=True)
            nc.tensor.matmul(ps[:, 6, 2 * NE:3 * NE], ones[:, :], sel[:, 0, :], start=True, stop=False)
            nc.tensor.matmul(ps[:, 6, 2 * NE:3 * NE], ones[:, :], sel[:, 1, :], start=False, stop=True
                             ).then_inc(pos_done, 1)
            pe.wait_ge(htm_out, 2)
            experts()
            for k in range(KT):
                norm_sum(4, k)

        @block.scalar
        def _(act):
            done = [0]

            def then(ins):
                done[0] += 1
                ins.then_inc(act_order, 1)
                act.wait_ge(act_order, done[0])

            act.dma_start(c_raw[:, :], d["c"]).then_inc(c_in, 16)
            act.dma_start(xT[:, :, :], d["x"]).then_inc(x_in, 16)
            for name, dst in CONSTS(locals_=dict(
                    ident=ident, rot=rot, cos=cos, sin=sin, amask=amask, gmask=gmask, reset=reset, iota=iota,
                    b_mod=b_mod, norm_g=norm_g, final_g=final_g, sink=sink, w2=w2, gla_b=gla_b, gla_g=gla_g,
                    conv_w=conv_w, router=router)):
                act.dma_start(dst[:], d[name]).then_inc(const_in, 16)

            def hi(v):
                split_hi(act, v, cols_of(v))

            def mod_rows(v):
                _kind, l, q = unit_of(v)
                if q % 4 == 3:
                    g = l * MODT // 4 + q // 4
                    act.wait_ge(split_used, v + 1)
                    if g >= 2:
                        act.wait_ge(modT_done, g - 1)
                    nc.scalar.activation(modrow[:, g % 2, :], ps[0:4, 7, :], ACT.Copy).then_inc(modrow_out, 1)

            def norm_squares(n, k):
                x_ready(act, n, k)
                if k >= 2:
                    act.wait_ge(sumsq_done, KT * n + k - 1)
                c0 = first_col(n)
                nc.scalar.activation(sq[:, k % 2, c0:T], xT[:, k, c0:T], ACT.Square).then_inc(sq_ready, 1)

            def norm_scale(n):
                act.wait_ge(sumsq_done, KT * n + KT)
                c0 = first_col(n)
                then(nc.scalar.activation(rs[:, c0:T], ps[:, 6, c0:T], ACT.Ln, bias=epsc[:, 0:1], scale=1.0 / D))
                nc.scalar.activation(rs[:, c0:T], rs[:, c0:T], ACT.Exp, scale=-0.5).then_inc(rs_ready, 1)

            def norm_hi(n):
                c0 = first_col(n)
                for k in range(KT):
                    act.wait_ge(hf_ready, KT * n + k + 1)
                    nc.scalar.activation(hhi[:, k, c0:T], hf[:, k % 2, c0:T], ACT.Copy).then_inc(hhi_done, 1)

            def projection(l):
                c0 = q_col(l)
                for n, (kind, _l, f) in enumerate(PROJ_STAGE[l]):
                    v = V_PROJ[l] + n
                    if kind == "fm" and not SX <= f < AQ:
                        act.wait_ge(split_used, v + 1)
                        src = ps[:, f % 2, :]
                        if f == LA:
                            dst, src = la[:, :], src[0:CH, :]
                        elif f < LQ:
                            dst = lk[:, f - LK, :]
                        elif f < AK:
                            dst, src = lq[:, f - LQ, c0:T], src[:, c0:T]
                        elif f == AK:
                            dst = ak[:, :]
                        elif f < SC:
                            dst, src = s_b[:, f - SB, c0:T], src[:, c0:T]
                        elif f < SX:
                            dst, src = s_c[:, f - SC, c0:T], src[:, c0:T]
                        else:
                            dst, src = aq[:, f - AQ, c0:T], src[:, c0:T]
                        nc.scalar.activation(dst, src, ACT.Copy).then_inc(fm_out[l], 1)
                    if kind == "tg" and f == 3:
                        act.wait_ge(split_used, v + 1)
                        for t in gla_reads(l):
                            nc.scalar.activation(gate[:, t, :], ps[:, 2 + t, :], ACT.Silu).then_inc(g_out[l], 1)
                    if kind == "mod":
                        mod_rows(v)
                    hi(v + H)
                    if kind == "fm" and f == AQ + 1:
                        logits_abs(l, 0)
                        softplus(l, 0)
                    if kind == "fm" and f == AQ + 2:
                        key_exp(l, 0)
                    if kind == "fm" and f == AQ + 3:
                        ref_exps(l, 0)

            def logits_abs(l, dr):
                for p in range(GT):
                    act.wait_ge(z_done[l], 2 * dr + p + 1)
                    nc.scalar.activation(gt1[dr][:, p, :], ps[:, 2 + 2 * dr + p, :], ACT.Abs,
                                         bias=gla_b[:, l, dr, p:p + 1]).then_inc(abs_done[l], 1)

            def softplus(l, dr):
                act.wait_ge(abs_done[l], GT * (dr + 1))
                then(nc.scalar.activation(gt1[dr], gt1[dr], ACT.Exp, scale=-1.0))
                nc.scalar.activation(gt1[dr], gt1[dr], ACT.Ln, bias=1.0).then_inc(sp_ready[l], 1)

            def key_exp(l, dr):
                act.wait_ge(d_ready[l], 2 * dr + 1)
                if dr:
                    act.wait_ge(kt_done[l], GT)
                nc.scalar.activation(gk[:, :, :], gt2[dr], ACT.Exp, scale=1.0 / TAU).then_inc(e_ready[l], 1)
                last = 0 if dr else CH - 1
                nc.scalar.activation(decay[:, dr, :],
                                     gb[:, :, :].rearrange("p g (c n) -> p (g c) n", n=CH)[:, :, last],
                                     ACT.Exp, scale=1.0 / TAU).then_inc(dec_ready[l], 1)

            def ref_exps(l, dr):
                act.wait_ge(d_ready[l], 2 * dr + 2)
                nc.scalar.activation(gt1[dr], gt2[dr], ACT.Exp, scale=1.0 / TAU).then_inc(e_ready[l], 1)
                act.wait_ge(e_ready[l], 4 * dr + 2)
                nc.scalar.activation(gt2[dr], gt2[dr], ACT.Exp, scale=-1.0 / TAU).then_inc(e_ready[l], 1)

            def query_exp(l, dr):
                act.wait_ge(e_used[l], 4 * dr + 3)
                nc.scalar.activation(gt1[dr], gb[:, :, :], ACT.Exp, scale=1.0 / TAU).then_inc(e_ready[l], 1)

            def gla(l):
                reads = list(gla_reads(l))
                n_o = 0
                for dr in range(2):
                    if dr == 0:
                        projected(act, l)
                        logits_abs(l, 1)
                    for p in range(GT):
                        act.wait_ge(kt_done[l], 2 * dr + p + 1)
                        if dr and p == 0:
                            act.wait_ge(u_done[l], NTT)
                        for c in range(2):
                            rows = slice(c * CH, (c + 1) * CH)
                            ins = nc.scalar.activation(gkt[rows, :, c, p * P:(p + 1) * P],
                                                       ps[rows, 4 * dr + p, :].rearrange("p (t n) -> p t n", t=NTT),
                                                       ACT.Copy)
                        ins.then_inc(kt_out[l], 1)
                    query_exp(l, dr)
                    if dr == 0:
                        softplus(l, 1)
                    for step, t in enumerate(gla_tiles(dr)):
                        if l == 0:
                            for n in range(2):
                                v = V_GLA0 + 2 * (NTT * dr + step) + n
                                mod_rows(v)
                                hi(v + H)
                        if t in reads:
                            act.wait_ge(o_done[l], n_o + 1)
                            nc.scalar.activation(
                                go[:, t, 256 * dr:256 * dr + 256].rearrange("p (g b n) -> p g b n", b=2, n=CH),
                                ps[:, 2 + n_o % 2, :].rearrange("p (g b n) -> p g b n", g=2, n=CH)[:, :, ::3, :],
                                ACT.Copy).then_inc(o_out[l], 1)
                            n_o += 1
                        if dr == 0 and step == 1:
                            key_exp(l, 1)
                        if dr == 0 and step == 2:
                            ref_exps(l, 1)
                act.wait_ge(ss_ready[l], 2)
                n8 = 8 * len(reads)
                then(nc.scalar.activation(gss[:, 0:n8], gss[:, 0:n8], ACT.Ln, bias=epsc[:, 0:1], scale=1.0 / CH))
                nc.scalar.activation(gss[:, 0:n8], gss[:, 0:n8], ACT.Exp, scale=-0.5).then_inc(grs_ready[l], 1)
                c0 = q_col(l)
                act.wait_ge(yT_done[l], GT)
                for f in range(GT):
                    nc.scalar.activation(hhi[:, AT + f, c0:T], ps[:, 4 + f, c0:T], ACT.Copy,
                                         scale=gla_g[:, l:l + 1]).then_inc(mixhi[l], 1)
                act.wait_ge(conv_out[l], 2)
                for f in range(2):
                    nc.scalar.activation(hhi[:, AT + GT + f, c0:T], s_b[:, f, c0:T], ACT.Copy
                                         ).then_inc(mixhi[l], 1)

            def attention(l):
                tiles = att_tiles(l)
                n_items = len(tiles) * HEADS

                def keys(i):
                    return 4 if tiles[i // HEADS] >= 2 else 2

                def tail(n):
                    act.wait_ge(pv_done[l], HEADS * (n + 1))
                    t = tiles[n]
                    nc.scalar.activation(hhi[:, 0:AT, t * P:(t + 1) * P],
                                         ps[:, 5 + n % 2, :].rearrange("p (j n) -> p j n", j=AT), ACT.Copy
                                         ).then_inc(ahi_ready[l], 1)

                for i in range(n_items + 4):
                    if i >= 11 and i % 8 == 3:
                        tail((i - 11) // 8)
                    if i < n_items:
                        act.wait_ge(negm_ready[l], i + 1)
                        if i >= 3:
                            act.wait_ge(pT_done[l], i - 2)
                        nc.scalar.activation(prob[:, i % 3, 0:keys(i) * P], ps[:, i % 2, 0:keys(i) * P], ACT.Exp,
                                             bias=negm[:, i:i + 1], scale=HD ** -0.5,
                                             accum_out=psumrow[:, i:i + 1]).then_inc(p_ready[l], 1)
                        h = i % HEADS
                        nc.scalar.activation(esink[:, i:i + 1], sink[:, l, h:h + 1], ACT.Exp,
                                             bias=negm[:, i:i + 1]).then_inc(esk_ready[l], 1)
                    if 2 <= i < n_items + 2:
                        j = i - 2
                        act.wait_ge(pT_done[l], j + 1)
                        if j >= 2:
                            act.wait_ge(pv_done[l], j - 1)
                        nc.scalar.activation(probT[:, j % 2, 0:keys(j) * P], ps[:, 3 + j % 2, 0:keys(j) * P],
                                             ACT.Copy).then_inc(pT_out[l], 1)
                    if l == 0 and i < n_items:
                        mod_rows(V_ATT0 + i)
                        hi(V_ATT0 + i + H)

            def out_projection(l):
                v0 = V_OUT[l]
                for m in range(KT):
                    if m:
                        norm_squares(2 * l + 1, m - 1)
                    hi(v0 + m + H)
                norm_squares(2 * l + 1, KT - 1)
                norm_scale(2 * l + 1)
                norm_hi(2 * l + 1)

            def ffn(l, v0, blocks):
                c0 = q_col(l)
                with act.Fori(0, blocks) as i:
                    for r in range(BLOCK):
                        j = r // 2
                        if r < 2 * FJ and r % 2 == 0:
                            act.wait_ge(split_used, i * BLOCK + (v0 + r + 1))
                            if j >= 2:
                                act.wait_ge(fh_ready[l], i * FJ + (j - 1))
                            nc.scalar.activation(sg[:, j % 2, c0:T], ps[:, j % 2, c0:T], ACT.Silu
                                                 ).then_inc(sg_ready[l], 1)
                        if r < 2 * FJ and r % 2 == 1:
                            act.wait_ge(fh_ready[l], i * FJ + (j + 1))
                            nc.scalar.activation(fhi[:, j, c0:T], hf[:, j % 2, c0:T], ACT.Copy
                                                 ).then_inc(fhi_ready[l], 1)
                        b = v0 + r + H
                        cols = DUNIT if 2 * FJ <= r + H < BLOCK else UNIT
                        split_hi(act, b, cols, i)

            def slots_hi(i):
                act.wait_ge(gather_done, i + 1)
                nc.scalar.activation(hs_hi[:, :, :].rearrange("p k n -> p (k n)"),
                                     ps[:, 6:8, :].rearrange("p b n -> p (b n)"), ACT.Copy).then_inc(hs_half, 1)

            def act_hi(i, j):
                act.wait_ge(aT_done, i * FJ + (j + 1))
                nc.scalar.activation(ehi[:, j, :], ps[:, 2 + j % 2, 0:P], ACT.Copy).then_inc(fhi_ready[1], 1)

            def experts():
                v0 = V_FFN[1]
                act.sem_inc(ys_ready, 1)
                act.sem_inc(scat_out, 1)
                slots_hi(0)
                act.wait_ge(passes_ready, 1)
                n_pass = act.value_load(passes[0:1, 0:1], min_val=NE, max_val=2 * NE)
                with act.Fori(0, n_pass) as i:
                    for r in range(BLOCK):
                        j = r // 2
                        if r < 2 * FJ and r % 2 == 1:
                            act.wait_ge(split_used, i * BLOCK + (v0 + r + 1))
                            if j >= 2:
                                act.wait_ge(fh_ready[1], i * FJ + (j - 1))
                            nc.scalar.activation(esg[:, j % 2, :], ps[:, j % 2, 0:P], ACT.Silu
                                                 ).then_inc(sg_ready[1], 1)
                            if j:
                                act_hi(i, j - 1)
                        split_hi(act, v0 + r + H, DUNIT if 2 * FJ <= r + H < BLOCK else UNIT, i)
                        if r == 13:
                            act.wait_ge(scat_done, i + 1)
                            nc.scalar.activation(scat[:, :], ps[:, 6, 0:LAT], ACT.Copy).then_inc(scat_out, 1)
                        if r == 2 * FJ:
                            act_hi(i, FJ - 1)
                        if r == 2 * FJ + 1:
                            slots_hi(i + 1)
                    act.wait_ge(split_used, i * BLOCK + (v0 + BLOCK))
                    nc.scalar.activation(ys[:, :], ps[:, 4:6, :].rearrange("p b n -> p (b n)"), ACT.Copy
                                         ).then_inc(ys_ready, 1)

            act.wait_ge(c_in, 16)
            then(nc.scalar.activation(c_act[:, :, :], c_raw[:, :].rearrange("p (k j) -> p k j", j=2), ACT.Silu))
            nc.scalar.activation(c_split[:, :, 0:2], c_act[:, :, :], ACT.Copy).then_inc(c_hi, 1)
            for v in range(H):
                hi(v)
            act.wait_ge(init_done, 1)
            for v in range(len(START)):
                mod_rows(v)
                hi(v + H)
                if SQ0 <= v < SQ0 + KT:
                    norm_squares(0, v - SQ0)
            norm_scale(0)
            norm_hi(0)
            projection(0)
            gla(0)
            attention(0)
            out_projection(0)
            ffn(0, V_FFN[0], 2)
            for k in range(KT):
                norm_squares(2, k)
            norm_scale(2)
            norm_hi(2)
            projection(1)
            gla(1)
            attention(1)
            act.wait_ge(mixlo[1], 4)
            act.wait_ge(alo_ready[1], len(att_tiles(1)))
            for dst, name in ((slots, "slots"), (before, "before")):
                act.dma_start(dst[:], d[name]).then_inc(moe_const, 16)
            out_projection(1)
            act.wait_ge(lgT_done, 1)
            nc.scalar.activation(lgT[:, :], ps[0:NE, 7, 0:LAT], ACT.Copy).then_inc(lgT_out, 1)
            for t in range(2):
                act.wait_ge(htm_done, t + 1)
                nc.scalar.activation(htm[:, t, :], ps[:, 2 * t:2 * t + 2, :].rearrange("p b n -> p (b n)"), ACT.Copy
                                     ).then_inc(htm_out, 1)
            act.wait_ge(topd_ready, 1)
            nc.scalar.activation(gate2[:, :, 1:2], gate2[:, :, 0:1], ACT.Exp).then_inc(tope_ready, 1)
            experts()
            for k in range(KT):
                norm_squares(4, k)
            norm_scale(4)

        @block.gpsimd
        def _(pool):
            def norm_lo(n):
                c0 = first_col(n)
                for k in range(KT):
                    pool.wait_ge(hhi_done, KT * n + k + 1)
                    nc.gpsimd.tensor_tensor(hlo[:, k, c0:T], hf[:, k % 2, c0:T], hhi[:, k, c0:T].bitcast(F32),
                                            ALU.subtract).then_inc(hlo_done, 1)

            def ffn(l, blocks):
                c0 = q_col(l)
                with pool.Fori(0, blocks) as i:
                    for j in range(FJ):
                        pool.wait_ge(fhi_ready[l], i * FJ + (j + 1))
                        nc.gpsimd.tensor_tensor(flo[:, j, c0:T], hf[:, j % 2, c0:T], fhi[:, j, c0:T].bitcast(F32),
                                                ALU.subtract).then_inc(flo_ready[l], 1)

            def zeros(l):
                projected(pool, l)
                for n in range(2):
                    rows = slice(CH * (1 - n), CH * (2 - n))
                    for buf in (gqp[rows, n, :, :], gqb[rows, n, :, :], gkt[rows, :, n, :]):
                        ins = nc.gpsimd.memset(buf, 0.0)
                ins.then_inc(zeroed[l], 1)
                pool.wait_ge(y_ready[l], 1)
                for n in range(2):
                    ins = nc.gpsimd.memset(akz[CH * (1 - n):CH * (2 - n), n, :], 0.0)
                ins.then_inc(zeroed[l], 1)

            norm_lo(0)
            zeros(0)
            norm_lo(1)
            ffn(0, 2)
            norm_lo(2)
            zeros(1)
            norm_lo(3)

        @block.vector
        def _(dve):
            V = nc.vector
            done = [0]

            def then(ins):
                done[0] += 1
                ins.then_inc(dve_order, 1)
                dve.wait_ge(dve_order, done[0])

            def lo(v):
                split_lo(dve, v, cols_of(v))

            taken = [0]

            def mods_in(n):
                for g in range(taken[0], n):
                    l, m = g // (MODT // 4), g % (MODT // 4)
                    dve.wait_ge(modT_done, g + 1)
                    then(V.tensor_reduce(modsum[:, g % 2, :].rearrange("p (m j) -> p m j", j=2),
                                         ps[:, MOD_BANK(g), 0:16].rearrange("p (m s j) -> p m j s", s=2, j=2),
                                         AX.X, ALU.add))
                    V.tensor_tensor(mod[:, l, 8 * m:8 * m + 8], modsum[:, g % 2, :], b_mod[:, l, 8 * m:8 * m + 8],
                                    ALU.add).then_inc(mod_out, 1)
                taken[0] = max(taken[0], n)

            def mod_step(v):
                _kind, l, q = unit_of(v)
                if q % 4 == 1:
                    mods_in(l * MODT // 4 + q // 4)

            def make_gain(l, which):
                m0 = 2 * (KT + 3 * KT * which)
                then(V.scalar_tensor_tensor(gain[:, l, which, :], mod[:, l, m0:m0 + 2 * KT], 1.0,
                                            norm_g[:, l, which, :], ALU.add, ALU.mult))

            def kinds_of(c0):
                return [(0, 0, CTX), (1, CTX, T)] if c0 == 0 else [(1, CTX, T)]

            def norm_apply(n):
                c0 = first_col(n)
                l, which = n // 2, n % 2
                dve.wait_ge(rs_ready, n + 1)
                for k in range(KT):
                    then(V.tensor_tensor(xn[:, k % 2, c0:T], xT[:, k, c0:T], rs[:, c0:T], ALU.mult))
                    if k >= 2:
                        dve.wait_ge(hlo_done, KT * n + k - 1)
                    for kind, a, b in kinds_of(c0):
                        sh = 2 * (3 * KT * which + k) + kind
                        ins = V.tensor_scalar(hf[:, k % 2, a:b], xn[:, k % 2, a:b],
                                              gain[:, l, which, 2 * k + kind:2 * k + kind + 1],
                                              mod[:, l, sh:sh + 1], ALU.mult, ALU.add)
                        if kind == 1:
                            ins.then_inc(hf_ready, 1)

            def projection(l):
                c0 = q_col(l)
                for n, (kind, _l, f) in enumerate(PROJ_STAGE[l]):
                    v = V_PROJ[l] + n
                    if kind == "tv" and f == 3:
                        dve.wait_ge(split_used, v + 1)
                        for t in range(NTT):
                            V.tensor_copy(vt[:, t, :], ps[:, 2 + t, 0:384]).then_inc(v_out[l], 1)
                    if kind == "fm" and SX <= f < AQ:
                        g = f - SX
                        dve.wait_ge(split_used, v + 1)
                        dve.wait_ge(fm_out[l], SC + g + 1)
                        if g == 0:
                            then(V.memset(cx[:, :, :, :], 0.0))
                        s0 = c0 // CTX
                        V.tensor_tensor(cx[:, g, s0:2, 1:LAT + 1],
                                        ps[:, f % 2, c0:T].rearrange("p (s n) -> p s n", n=LAT),
                                        s_c[:, g, c0:T].rearrange("p (s n) -> p s n", n=LAT),
                                        ALU.mult).then_inc(cx_out[l], 1)
                    lo(v + H)
                    if kind == "mod":
                        mod_step(v)
                    if kind == "fm" and AQ <= f < AQ + 2:
                        conv(l, f - AQ)
                    if kind == "fm" and f == AQ:
                        then(V.memset(am[:, :, :], 0.0))
                        then(V.memset(state[:, :, 0, :], 0.0))
                    if kind == "fm" and f == AQ + 1:
                        logits_min(l, 0)
                        log_decay(l, 0)
                    if kind == "fm" and f == AQ + 2:
                        decayed_keys(l, 0)
                    if kind == "fm" and f == AQ + 3:
                        ref_keys(l, 0)

            def chunks(x):
                return x.rearrange("p g (c n) -> p (g c) n", n=CH)

            def logits_min(l, dr):
                for p in range(GT):
                    dve.wait_ge(abs_done[l], 2 * dr + p + 1)
                    ins = V.tensor_scalar(gt2[dr][:, p, :], ps[:, 2 + 2 * dr + p, :], gla_b[:, l, dr, p:p + 1], 0.0,
                                          ALU.add, ALU.min)
                    if p == GT - 1 and dr:
                        ins.then_inc(z_out[l], 1)
                        dve.wait_ge(z_out[l], 1)
                    else:
                        then(ins)

            def log_decay(l, dr):
                dve.wait_ge(sp_ready[l], dr + 1)
                then(V.tensor_tensor(gt2[dr], gt2[dr], gt1[dr], ALU.subtract))
                if dr:
                    dve.wait_ge(dec_ready[l], 1)
                for p in range(GT):
                    if dr == 0:
                        o, m, x = gb[:, p, :], reset[:, :], gt2[dr][:, p, :]
                    else:
                        o, m, x = gb[:, p, ::-1], reset[:, :], gt2[dr][:, p, ::-1]
                    then(V.tensor_tensor_scan(o, m, x, 0.0, ALU.mult, ALU.add))
                last = 0 if dr else CH - 1
                gbc = chunks(gb[:, :, :])
                V.tensor_tensor(chunks(gt2[dr]), gbc[:, :, last:last + 1].broadcast_to([P, GT * NCH, CH]), gbc,
                                ALU.subtract).then_inc(d_ready[l], 1)

            def decayed_keys(l, dr):
                dve.wait_ge(e_ready[l], 4 * dr + 1)
                V.tensor_tensor(gk[:, :, :], gk[:, :, :], lk[:, :, :], ALU.mult).then_inc(e_used[l], 1)
                ref = CH // 2 if dr == 0 else CH - 1 - CH // 2
                gbc = chunks(gb[:, :, :])
                V.tensor_tensor(chunks(gt2[dr]), gbc, gbc[:, :, ref:ref + 1].broadcast_to([P, GT * NCH, CH]),
                                ALU.subtract).then_inc(d_ready[l], 1)

            def ref_keys(l, dr):
                dve.wait_ge(e_ready[l], 4 * dr + 3)
                V.tensor_tensor(gkp[:, :, :], gt2[dr], lk[:, :, :], ALU.mult).then_inc(e_used[l], 1)

            def queries(l, dr, dst):
                c0 = q_col(l)
                for n in range(2):
                    rows = slice(CH * n, CH * (n + 1))
                    ins = V.scalar_tensor_tensor(dst[rows, n, :, c0:T], gt1[dr][rows, :, c0:T], HD ** -0.5,
                                                 lq[rows, :, c0:T], ALU.mult, ALU.mult)
                ins.then_inc(e_used[l], 1)

            def conv(l, g):
                c0 = q_col(l)
                s0 = c0 // CTX
                dve.wait_ge(cx_out[l], g + 1)
                y = s_c[:, g, c0:T].rearrange("p (s n) -> p s n", n=LAT)
                then(V.tensor_scalar(y, cx[:, g, s0:2, 1:LAT + 1], conv_w[:, l, 1, g:g + 1], None, ALU.mult))
                then(V.scalar_tensor_tensor(y, cx[:, g, s0:2, 0:LAT], conv_w[:, l, 0, g:g + 1], y,
                                            ALU.mult, ALU.add))
                then(V.scalar_tensor_tensor(y, cx[:, g, s0:2, 2:LAT + 2], conv_w[:, l, 2, g:g + 1], y,
                                            ALU.mult, ALU.add))
                V.tensor_tensor(s_b[:, g, c0:T], s_c[:, g, c0:T], s_b[:, g, c0:T], ALU.mult
                                ).then_inc(conv_out[l], 1)

            def outputs_gated(l, dr):
                reads = list(gla_reads(l))
                n = len(reads)
                dve.wait_ge(o_out[l], n * (dr + 1))
                o = go[:, reads[0]:NTT, 256 * dr:256 * (dr + 1)]
                sqv = gtt[:, 0, :, :].rearrange("p g t -> p (g t)")[:, 0:256 * n].rearrange("p (t n) -> p t n", t=n)
                then(V.tensor_tensor(sqv, o, o, ALU.mult))
                V.tensor_reduce(gss[:, 0:8 * n].rearrange("p (t d h) -> p t d h", d=2, h=4)[:, :, dr, :],
                                sqv.rearrange("p t (h n) -> p t h n", n=CH), AX.X, ALU.add).then_inc(ss_ready[l], 1)
                then(V.tensor_tensor(o, o, gate[:, reads[0]:NTT, 256 * dr:256 * (dr + 1)], ALU.mult))

            def gla(l):
                reads = list(gla_reads(l))
                c0 = q_col(l)
                n_at = 0

                for dr in range(2):
                    if dr == 0:
                        projected(dve, l)
                    else:
                        ref_keys(l, dr)
                        dve.wait_ge(o_done[l], len(reads))
                    queries(l, dr, gqp)
                    if dr == 0:
                        logits_min(l, 1)
                    dve.wait_ge(e_ready[l], 4 * dr + 4)
                    queries(l, dr, gqb)
                    dve.wait_ge(dec_ready[l], dr + 1)
                    for step, t in enumerate(gla_tiles(dr)):
                        n_u = NTT * dr + step
                        if t in reads:
                            dve.wait_ge(at_done[l], n_at + 1)
                            if n_at:
                                dve.wait_ge(o_done[l], n_at)
                            V.copy_predicated(am[:, dr, :].rearrange("p (h n) -> p h n", n=P),
                                              gmask[:, dr:dr + 1, :].broadcast_to([P, 4, P]),
                                              ps[:, n_at % 2, :].rearrange("p (h n) -> p h n", n=P)
                                              ).then_inc(am_ready[l], 1)
                            n_at += 1
                        dve.wait_ge(u_done[l], n_u + 1)
                        for ci, c in enumerate(gla_chunks(dr)):
                            for p in range(GT):
                                col = p * NCH + 2 * t + c
                                ins = V.scalar_tensor_tensor(
                                    state[:, dr, 2 * step + ci + 1, p * CH:(p + 1) * CH],
                                    state[:, dr, 2 * step + ci, p * CH:(p + 1) * CH],
                                    decay[:, dr, col:col + 1],
                                    ps[:, (6, 4)[n_u % 2], (2 * c + p) * CH:(2 * c + p + 1) * CH],
                                    ALU.mult, ALU.add)
                            ins.then_inc(st_ready[l], 1)
                            dve.wait_ge(st_ready[l], 2 * n_u + ci + 1)
                        if l == 0:
                            for n in range(2):
                                v = V_GLA0 + 2 * n_u + n
                                lo(v + H)
                                mod_step(v)
                        if dr == 0 and step == 0:
                            log_decay(l, 1)
                        if dr == 0 and step == 2:
                            decayed_keys(l, 1)
                        if dr == 1 and step == 1:
                            outputs_gated(l, 0)
                outputs_gated(l, 1)
                n = len(reads)
                t0 = reads[0]
                o4 = go[:, t0:NTT, :]
                dve.wait_ge(grs_ready[l], 1)
                oh = o4.rearrange("p t (h n) -> p (t h) n", n=CH)
                then(V.tensor_tensor(oh, oh, gss[:, 0:8 * n].rearrange("p (h o) -> p h o", o=1
                                                                       ).broadcast_to([P, 8 * n, CH]), ALU.mult))
                yv = gb[:, 0:n // 2, :].rearrange("p g (t n) -> p (g t) n", n=256)
                V.tensor_tensor(yv, o4[:, :, 0:256], o4[:, :, 256:512], ALU.add).then_inc(y_ready[l], 1)

            def attention(l):
                tiles = att_tiles(l)
                n_items = len(tiles) * HEADS
                dve.wait_ge(y_ready[l], 1)
                dve.wait_ge(rot_done[l], 1)
                r1 = rt1.rearrange("p (j n) -> p j n", j=AT)
                r2 = rt2.rearrange("p (j n) -> p j n", j=AT)
                V.tensor_tensor(r1, aq[:, :, CTX:T], cos[:, :].rearrange("p (o n) -> p o n", o=1
                                                                        ).broadcast_to([P, AT, LAT]), ALU.mult)
                then(V.tensor_tensor(r2, ps[:, 0:2, :].rearrange("p b (j n) -> p (b j) n", j=2),
                                     sin[:, :].rearrange("p (o n) -> p o n", o=1).broadcast_to([P, AT, LAT]),
                                     ALU.mult))
                then(V.tensor_tensor(aq[:, :, CTX:T], r1, r2, ALU.add))
                then(V.tensor_tensor(rt1[:, 0:LAT], ak[:, CTX:T], cos[:, :], ALU.mult))
                then(V.tensor_tensor(rt2[:, 0:LAT], ps[:, 2, 0:LAT], sin[:, :], ALU.mult))
                for kv in range(2):
                    rows = slice(kv * HD, (kv + 1) * HD)
                    V.tensor_tensor(akz[rows, kv, CTX:T], rt1[rows, 0:LAT], rt2[rows, 0:LAT], ALU.add)
                    ins = V.tensor_copy(akz[rows, kv, 0:CTX], ak[rows, 0:CTX])
                ins.then_inc(akz_ready[l], 1)

                c0 = q_col(l)
                for f in range(GT):
                    dve.wait_ge(mixhi[l], f + 1)
                    V.scalar_tensor_tensor(hlo[:, AT + f, c0:T], ps[:, 4 + f, c0:T], gla_g[:, l:l + 1],
                                           hhi[:, AT + f, c0:T].bitcast(F32), ALU.mult, ALU.subtract
                                           ).then_inc(mixlo[l], 1)
                for f in range(2):
                    dve.wait_ge(mixhi[l], GT + f + 1)
                    V.tensor_tensor(hlo[:, AT + GT + f, c0:T], s_b[:, f, c0:T],
                                    hhi[:, AT + GT + f, c0:T].bitcast(F32), ALU.subtract).then_inc(mixlo[l], 1)

                def keys(i):
                    return 4 if tiles[i // HEADS] >= 2 else 2

                def tail(n):
                    dve.wait_ge(ahi_ready[l], n + 1)
                    t = tiles[n]
                    V.tensor_tensor(hlo[:, 0:AT, t * P:(t + 1) * P],
                                    ps[:, 5 + n % 2, :].rearrange("p (j n) -> p j n", j=AT),
                                    hhi[:, 0:AT, t * P:(t + 1) * P].bitcast(F32), ALU.subtract
                                    ).then_inc(alo_ready[l], 1)

                for i in range(n_items + 4):
                    if i >= 11 and i % 8 == 3:
                        tail((i - 11) // 8)
                    if i < n_items:
                        t, h = tiles[i // HEADS], i % HEADS
                        dve.wait_ge(s_done[l], i + 1)
                        if t >= 2:
                            blk = slice(3 * P, 4 * P) if t == 2 else slice(2 * P, 3 * P)
                            then(V.tensor_tensor(ps[:, i % 2, blk], ps[:, i % 2, blk], amask[:, t - 2, :], ALU.add))
                        then(V.tensor_reduce(mx[:, i:i + 1], ps[:, i % 2, 0:keys(i) * P], AX.X, ALU.max))
                        V.tensor_scalar(negm[:, i:i + 1], mx[:, i:i + 1], -(HD ** -0.5), negsink[:, l, h:h + 1],
                                        ALU.mult, ALU.min).then_inc(negm_ready[l], 1)
                    if 1 <= i <= n_items:
                        j = i - 1
                        dve.wait_ge(esk_ready[l], j + 1)
                        then(V.tensor_tensor(rden[:, j:j + 1], psumrow[:, j:j + 1], esink[:, j:j + 1], ALU.add))
                        then(V.reciprocal(rden[:, j:j + 1], rden[:, j:j + 1]))
                        V.tensor_scalar(prob[:, j % 3, 0:keys(j) * P], prob[:, j % 3, 0:keys(j) * P],
                                        rden[:, j:j + 1], None, ALU.mult).then_inc(pn_ready[l], 1)
                    if l == 0 and 1 <= i <= n_items:
                        lo(V_ATT0 + i - 1 + H)
                        mod_step(V_ATT0 + i - 1)

            def out_projection(l):
                v0 = V_OUT[l]
                c0 = q_col(l)
                if l == 0:
                    mods_in(2 * MODT // 4)
                    dve.wait_ge(mod_out, 2 * MODT // 4)
                    make_gain(0, 1)
                    make_gain(1, 0)
                    make_gain(1, 1)
                for m in range(KT):
                    dve.wait_ge(split_used, v0 + m + 1)
                    for kind, a, b in kinds_of(c0):
                        g = 2 * (2 * KT + m) + kind
                        ins = V.scalar_tensor_tensor(xT[:, m, a:b], ps[:, m % 2, a:b], mod[:, l, g:g + 1],
                                                     xT[:, m, a:b], ALU.mult, ALU.add)
                        if kind == 1:
                            ins.then_inc(x_mixed[l], 1)
                    lo(v0 + m + H)
                norm_apply(2 * l + 1)

            def ffn(l, v0, blocks):
                c0 = q_col(l)
                dve.sem_inc(down_out[l], 1)
                with dve.Fori(0, blocks) as i:
                    for r in range(BLOCK):
                        if r < 2 * FJ and r % 2 == 1:
                            j = r // 2
                            dve.wait_ge(split_used, i * BLOCK + (v0 + r + 1))
                            dve.wait_ge(sg_ready[l], i * FJ + (j + 1))
                            if j >= 2:
                                dve.wait_ge(flo_ready[l], i * FJ + (j - 1))
                            V.tensor_tensor(hf[:, j % 2, c0:T], ps[:, 2 + j % 2, c0:T], sg[:, j % 2, c0:T],
                                            ALU.mult).then_inc(fh_ready[l], 1)
                        if r >= 2 * FJ:
                            m = r - 2 * FJ
                            dve.wait_ge(split_used, i * BLOCK + (v0 + r + 1))
                            for kind, a, b in kinds_of(c0):
                                g = 2 * (5 * KT + m) + kind
                                ins = V.scalar_tensor_tensor(xT[:, m, a:b], ps[:, 4 + m % 2, a:b],
                                                             mod[:, l, g:g + 1], xT[:, m, a:b],
                                                             ALU.mult, ALU.add)
                            ins.then_inc(down_out[l], 1)
                        b = v0 + r + H
                        cols = DUNIT if 2 * FJ <= r + H < BLOCK else UNIT
                        split_lo(dve, b, cols, i)

            def pair(i):
                for t in range(2):
                    ins = V.tensor_scalar(pair_in[:, t, :], slots[:, :], posx[:, t, bass.ds(i, 1)], None,
                                          ALU.is_equal)
                ins.then_inc(pair_ready, 1)

            def slots_lo(i):
                dve.wait_ge(hs_half, i + 1)
                V.tensor_tensor(hs_lo[:, :, :].rearrange("p k n -> p (k n)"),
                                ps[:, 6:8, :].rearrange("p b n -> p (b n)"),
                                hs_hi[:, :, :].rearrange("p k n -> p (k n)").bitcast(F32), ALU.subtract
                                ).then_inc(hs_ready, 1)

            def act_lo(i, j):
                dve.wait_ge(fhi_ready[1], i * FJ + (j + 1))
                V.tensor_tensor(elo[:, j, :], ps[:, 2 + j % 2, 0:P], ehi[:, j, :].bitcast(F32), ALU.subtract
                                ).then_inc(flo_ready[1], 1)

            def add(i, n):
                dve.wait_ge(sc_done, i * 4 + (n + 1))
                y = yacc[:, 2 * n:2 * n + 2, :].rearrange("p f n -> p (f n)")
                V.tensor_tensor(y, y, ps[:, 6 + n % 2, :], ALU.add).then_inc(y_added, 1)

            def experts():
                v0 = V_FFN[1]
                dve.wait_ge(moe_const, 32)
                pair(0)
                slots_lo(0)
                n_pass = dve.value_load(passes[0:1, 0:1], min_val=NE, max_val=2 * NE)
                with dve.Fori(0, n_pass) as i:
                    for r in range(BLOCK):
                        j = r // 2
                        if r < 2 * FJ and r % 2 == 1:
                            dve.wait_ge(sg_ready[1], i * FJ + (j + 1))
                            if j >= 2:
                                dve.wait_ge(aT_done, i * FJ + (j - 1))
                            V.tensor_tensor(eact[:, j % 2, :], esg[:, j % 2, :], ps[:, j % 2, P:2 * P], ALU.mult
                                            ).then_inc(fh_ready[1], 1)
                            if j:
                                act_lo(i, j - 1)
                        split_lo(dve, v0 + r + H, DUNIT if 2 * FJ <= r + H < BLOCK else UNIT, i)
                        if r in (3, 5, 7, 9):
                            add(i, (r - 3) // 2)
                        if r == 9:
                            for t in range(2):
                                ins = V.tensor_scalar(pair_w[:, t, :], slots[:, :], posx[:, t, bass.ds(i, 1)],
                                                      pickx[:, t, bass.ds(i, 1)], ALU.is_equal, ALU.mult)
                            ins.then_inc(pairw_ready, 1)
                            pair(i + 1)
                        if r == 2 * FJ:
                            act_lo(i, FJ - 1)
                        if r == 2 * FJ + 1:
                            slots_lo(i + 1)
                for n in range(4):
                    add(n_pass, n)
                dve.wait_ge(y_added, n_pass * 4 + 4)

            then(V.memset(ones[:, :], 1.0))
            V.memset(epsc[:, :], EPS).then_inc(init_done, 1)
            dve.wait_ge(c_hi, 1)
            V.tensor_tensor(c_split[:, :, 2:4], c_act[:, :, :], c_split[:, :, 0:2].bitcast(F32), ALU.subtract
                            ).then_inc(c_done, 1)
            for v in range(H):
                lo(v)
            for v in range(len(START)):
                if v == 4:
                    dve.wait_ge(const_in, 16 * N_CONST)
                    then(V.tensor_scalar(negsink[:, :, :], sink[:, :, :], -1.0, None, ALU.mult))
                lo(v + H)
                mod_step(v)
            mods_in(M0 // 4)
            dve.wait_ge(mod_out, M0 // 4)
            make_gain(0, 0)
            dve.wait_ge(x_in, 16)
            norm_apply(0)
            projection(0)
            gla(0)
            attention(0)
            out_projection(0)
            ffn(0, V_FFN[0], 2)
            dve.wait_ge(down_out[0], 1 + 2 * KT)
            norm_apply(2)
            projection(1)
            gla(1)
            attention(1)
            out_projection(1)
            then(V.memset(yacc[:, :, :], 0.0))
            then(V.memset(ys[:, :], 0.0))
            then(V.memset(scat[:, :], 0.0))
            then(V.memset(posx[:, :, :], -1.0))
            dve.wait_ge(lg_done, 1)
            then(V.tensor_copy(logits[:, :, :], ps[:, 7, 0:2 * NE].rearrange("p (t e) -> p t e", t=2)))
            for t in range(2):
                then(V.max(top[:, t, :], logits[:, t, :]))
                then(V.max_index(topi[:, t, :], top[:, t, :], logits[:, t, :]))
            then(V.tensor_copy(topf[:, :, :], topi[:, :, :]))
            V.tensor_tensor(gate2[:, :, 0:1], top[:, :, 1:2], top[:, :, 0:1], ALU.subtract).then_inc(topd_ready, 1)
            for t in range(2):
                then(V.tensor_scalar(sel0[:, t, :], iota[:, :], topf[:, t, 0:1], None, ALU.is_equal))
                then(V.tensor_scalar(sel[:, t, :], iota[:, :], topf[:, t, 1:2], None, ALU.is_equal))
            V.tensor_tensor(sel[:, :, :], sel[:, :, :], sel0[:, :, :], ALU.add).then_inc(sel_ready, 1)
            dve.wait_ge(sel_ready, 1)
            dve.wait_ge(tope_ready, 1)
            then(V.tensor_scalar(gate2[:, :, 2:3], gate2[:, :, 1:2], 1.0, None, ALU.add))
            then(V.reciprocal(gate2[:, :, 2:3], gate2[:, :, 2:3]))
            then(V.tensor_tensor(gate2[:, :, 3:4], gate2[:, :, 1:2], gate2[:, :, 2:3], ALU.mult))
            for t in range(2):
                for w in range(2):
                    then(V.tensor_scalar(pick[:, t, w, :], iota[:, :], topf[:, t, w:w + 1],
                                         gate2[:, t, 2 + w:3 + w], ALU.is_equal, ALU.mult))
                for b in range(2):
                    then(V.tensor_tensor(pickx[:, t, b * NE:(b + 1) * NE], pick[:, t, 0, :], pick[:, t, 1, :],
                                         ALU.add))
            dve.wait_ge(pos_done, 1)
            then(V.tensor_reduce(count[:, 0:1], ps[:, 6, 2 * NE:3 * NE], AX.X, ALU.max))
            then(V.tensor_scalar(count[:, 1:2], count[:, 0:1], P + 0.5, 1.0, ALU.is_gt, ALU.add))
            then(V.tensor_scalar(count[:, 2:3], count[:, 1:2], float(NE), None, ALU.mult))
            then(V.tensor_copy(passes[:, 0:1], count[:, 2:3]))
            V.tensor_copy(passes[:, 1:2], count[:, 1:2]).then_inc(passes_ready, 1)
            then(V.scalar_tensor_tensor(sel0[:, :, :], ps[:, 6, 0:2 * NE].rearrange("p (t e) -> p t e", t=2), 1.0,
                                        sel[:, :, :], ALU.add, ALU.mult))
            for b in range(2):
                then(V.tensor_scalar(posx[:, :, b * NE:(b + 1) * NE], sel0[:, :, :], -1.0 - P * b, None, ALU.add))
            experts()
            for m in range(KT):
                g = 2 * (5 * KT + m) + 1
                V.scalar_tensor_tensor(xT[:, m, CTX:T], yacc[:, m, :], mod[:, 1, g:g + 1], xT[:, m, CTX:T],
                                       ALU.mult, ALU.add).then_inc(x_last, 1)
            dve.wait_ge(rs_ready, 4 + 1)
            for k in range(KT):
                then(V.tensor_tensor(xn[:, k % 2, CTX:T], xT[:, k, CTX:T], rs[:, CTX:T], ALU.mult))
                V.tensor_scalar(outT[:, k, :], xn[:, k % 2, CTX:T], final_g[:, k:k + 1], None,
                                ALU.mult).then_inc(out_ready, 1)



CONST_NAMES = ["ident", "rot", "cos", "sin", "amask", "gmask", "reset", "iota", "b_mod", "norm_g", "final_g",
               "sink", "w2", "gla_b", "gla_g", "conv_w", "router"]
N_CONST = len(CONST_NAMES)


def CONSTS(locals_):
    return [(n, locals_[n]) for n in CONST_NAMES]


def _constants():
    p = np.arange(P)
    f32 = np.float32
    rot = np.zeros((P, P), f32)
    for m in range(P):
        if m % HD < HD // 2:
            rot[m + HD // 2, m] = -1.0
        else:
            rot[m - HD // 2, m] = 1.0
    nf = HD // 4
    inv = (f32(10000.0) ** (-np.arange(nf, dtype=f32) / f32(nf))).astype(f32)
    tok = np.arange(LAT)
    ang = np.concatenate([(tok // 64).astype(f32)[:, None] * inv, (tok % 64).astype(f32)[:, None] * inv], 1)
    ang = ang[:, p % (HD // 2)].T
    q, k = p[:, None], p[None, :]
    amask = np.stack([np.where(k <= q, 0.0, -1e30), np.where(q <= k, 0.0, -1e30)], 1).astype(f32)
    s, t = p[:, None], p[None, :]
    same = s // CH == t // CH
    gmask = np.stack([same & (s <= t), same & (s >= t)], 1).astype(np.int32)
    reset = np.broadcast_to((np.arange(T) % CH != 0).astype(f32), (P, T))
    return dict(slots=np.broadcast_to(np.arange(P, dtype=f32), (P, P)), before=(s < t).astype(f32),
                ident=np.eye(P, dtype=f32), rot=rot, cos=np.cos(ang), sin=np.sin(ang), amask=amask, gmask=gmask,
                reset=reset, iota=np.broadcast_to(np.arange(NE, dtype=f32), (P, NE)))


def _units(w, n):
    k, cols = w.shape
    return w.reshape(k // P, P, cols // n, n).transpose(2, 1, 0, 3).reshape(cols // n, P, k // P * n)


def _layout(a):
    f = {n: np.asarray(v) for n, v in a.items()}
    o = _constants()
    o["x"] = np.concatenate([f["ctx"][0], f["x"][0]], 0).T.reshape(KT, P, T).transpose(1, 0, 2)
    o["c"] = np.stack([f["c_ctx"], f["c"][0]], 1).reshape(KT, P, 2).transpose(1, 0, 2).reshape(P, 2 * KT)
    o["w_mod"] = (f["w_mod"].reshape(LAYERS, KT // 2, 2, P, MODT // 4, 512).transpose(0, 4, 1, 3, 2, 5)
                  .reshape(LAYERS, MODT, P, UNIT))

    def cols(v, tiles):
        return np.repeat(v.reshape(tiles, P).T[:, :, None], 2, 2).reshape(P, 2 * tiles)

    o["b_mod"] = np.stack([cols(f["b_mod"][l], MODT) for l in range(LAYERS)], 1)
    o["norm_g"] = np.stack([np.stack([cols(f[n][l], KT) for n in ("norm1_g", "norm2_g")], 1)
                            for l in range(LAYERS)], 1)
    o["final_g"] = f["final_norm_g"].reshape(KT, P).T
    pair = [h for j in range(AT) for h in (j, AT + j)]
    o["sink"] = np.broadcast_to(f["attn_sink"][:, pair], (P, LAYERS, HEADS))
    fm, tv, tg, wo, w2 = [], [], [], [], []
    for l in range(LAYERS):
        w = f["w_in"][l]
        z = np.zeros((D, 16), w.dtype)
        la = np.concatenate([w[:, 2048:2064], z, w[:, 2064:2080], z, np.zeros((D, 64), w.dtype)], 1)
        aq = w[:, 0:512].reshape(D, HEADS, HD)[:, pair].reshape(D, 512)
        fm.append(_units(np.concatenate([la, w[:, 1024:1280], w[:, 768:1024], w[:, 512:640],
                                         w[:, 2080:2848], aq], 1), P))
        for dst, c in ((tv, np.r_[640:768, 1280:1536]), (tg, np.r_[1536:2048])):
            n = len(c)
            dst.append(w[:, c].reshape(KT // 2, 2, P, n).transpose(0, 2, 1, 3).reshape(KT // 2, P, 2 * n))
        wout = f["w_out"][l]
        wo.append(_units(np.concatenate([wout[0:512].reshape(HEADS, HD, D)[pair].reshape(512, D), wout[512:]], 0),
                         P))
        z = np.zeros((16, GT * P), w.dtype)
        w2.append(np.concatenate([f["gla_w2_f"][l], z, f["gla_w2_b"][l], z], 0))
    o["w_fm"], o["w_tv"], o["w_tg"], o["w_out"] = map(np.stack, (fm, tv, tg, wo))
    o["w2"] = np.stack(w2, 1)
    o["gla_b"] = np.stack([np.stack([f[n][l].reshape(GT, P).T for n in ("gla_b_f", "gla_b_b")], 1)
                           for l in range(LAYERS)], 1)
    o["gla_g"] = np.stack([np.tile(f["gla_norm_g"][l], 2) for l in range(LAYERS)], 1)
    o["conv_w"] = np.stack([f["conv_w"][l].reshape(3, 2, P).transpose(2, 0, 1) for l in range(LAYERS)], 1)
    o["router"] = f["router_w"][0].reshape(KT, P, NE).transpose(1, 0, 2)

    def gate_up(w):
        k, n = w.shape
        return _units(w, P).reshape(2, n // 2 // P, P, UNIT).transpose(1, 0, 2, 3).reshape(n // P, P, UNIT)

    o["w_gu0"] = gate_up(f["ffn_w_gu"][0])
    o["w_dn0"] = np.concatenate([_units(f["ffn_w_down"][0][b * DUNIT:(b + 1) * DUNIT], P) for b in range(2)], 0)
    gu = (f["expert_w_gu"][0].reshape(NE, 2, 4, P, 2, FJ, P).transpose(0, 5, 1, 3, 2, 4, 6)
          .reshape(NE * 2 * FJ, P, UNIT))
    o["w_gu1"] = np.concatenate([gu, gu[:R]], 0)
    o["w_dn1"] = (f["expert_w_down"][0].reshape(NE, FJ, P, KT // 4, 512).transpose(0, 2, 1, 3, 4)
                  .reshape(NE, P, KT, DUNIT).transpose(0, 2, 1, 3).reshape(NE * KT, P, DUNIT))
    return o


def kernel(**inputs):
    import concourse.bacc as _bacc
    from concourse.bass_utils import run_bass_kernel_spmd as _run

    nc = _bacc.Bacc("TRN2", target_bir_lowering=False, num_devices=1)
    arrays, aps = {}, {}
    for name, a in _layout(inputs).items():
        a = np.ascontiguousarray(a)
        arrays[f"in_{name}"] = a
        aps[name] = nc.dram_tensor(f"in_{name}", a.shape, mybir.dt.from_np(a.dtype), kind="ExternalInput").ap()
    aps["w_gu"] = [aps["w_gu0"], aps["w_gu1"]]
    aps["w_dn"] = [aps["w_dn0"], aps["w_dn1"]]
    out = nc.dram_tensor("out", (P, KT, LAT), F32, kind="ExternalOutput").ap()
    build(nc, aps, out)
    r = _run(nc, [arrays], core_ids=[0])
    return r.results[0]["out"].transpose(1, 0, 2).reshape(D, LAT).T.reshape(1, LAT, D)
```
